# Optimizing a Trainium2 kernel written in Bass

```python
import jax, jax.numpy as jnp
from jax import lax
import numpy as np

D_MODEL = 1024
BATCH = 1
SEQ = 256
DEPTH = 4

N_MIXERS = 3
EPS = 1e-6
D_FF = 2816
MLSTM_HEADS = 4
MLSTM_DH = D_MODEL // MLSTM_HEADS
MLSTM_CHUNK = 64
CONV_WIDTH = 4
MLSTM_F_BIAS = 3.0
FOX_HEADS = 8
FOX_DH = D_MODEL // FOX_HEADS
Q_BLOCK = 128
FOX_F_BIAS = 2.0
GLA_HEADS = 4
GLA_DK_TOTAL = D_MODEL // 2
GLA_DK = GLA_DK_TOTAL // GLA_HEADS
GLA_DV = D_MODEL // GLA_HEADS
GLA_RANK = 16
GLA_TAU = 16.0
GLA_CHUNK = 64
N_A = (DEPTH + 2) // 3
N_B = (DEPTH + 1) // 3
N_C = DEPTH // 3

kernel_name = "hybrid_mlstm_fox_gla_macaron"

def rmsnorm(x, w):
    xf = x.astype(jnp.float32)
    y = xf * lax.rsqrt(jnp.mean(xf * xf, axis=-1, keepdims=True) + EPS)
    return (y * w.astype(jnp.float32)).astype(x.dtype)

def swiglu(x, w_in, w_out):
    g, u = jnp.split(x @ w_in, 2, axis=-1)
    return (jax.nn.silu(g) * u) @ w_out

def split_heads(t, n_heads):
    b, s, w = t.shape
    return t.reshape(b, s, n_heads, w // n_heads).transpose(0, 2, 1, 3)

def to_chunks(t, size):
    b, h, s = t.shape[:3]
    t = t.reshape(b, h, s // size, size, *t.shape[3:])
    return jnp.moveaxis(t, 2, 0)

def from_chunks(t):
    nc, b, h, l, d = t.shape
    return jnp.moveaxis(t, 0, 2).reshape(b, h, nc * l, d)

def causal_conv(x, w):
    k, c = w.shape
    return lax.conv_general_dilated(x, w[:, None, :], window_strides=(1,), padding=[(k - 1, 0)],
                                    dimension_numbers=('NWC', 'WIO', 'NWC'), feature_group_count=c)

def mlstm_chunkwise(q, k, v, log_i, log_f):
    b, h, s, dh = q.shape
    L = MLSTM_CHUNK
    causal = jnp.tril(jnp.ones((L, L), dtype=bool))

    def step(carry, inp):
        C, n, m = carry
        qc, kc, vc, ic, fc = inp
        bcum = jnp.cumsum(fc, axis=-1)
        log_d = jnp.where(causal, bcum[..., :, None] - bcum[..., None, :] + ic[..., None, :], -jnp.inf)
        log_inter = bcum + m[..., None]
        m_t = jnp.maximum(log_inter, jnp.max(log_d, axis=-1))
        d = jnp.exp(log_d - m_t[..., None])
        inter = jnp.exp(log_inter - m_t)
        sc = jnp.einsum('bhtd,bhsd->bhts', qc, kc) * d
        num = jnp.einsum('bhts,bhse->bhte', sc, vc) + inter[..., None] * jnp.einsum('bhtd,bhde->bhte', qc, C)
        den = jnp.sum(sc, axis=-1) + inter * jnp.einsum('bhtd,bhd->bht', qc, n)
        h_out = num / jnp.maximum(jnp.abs(den), jnp.exp(-m_t))[..., None]
        b_last = bcum[..., -1]
        log_w = b_last[..., None] - bcum + ic
        m_new = jnp.maximum(b_last + m, jnp.max(log_w, axis=-1))
        w = jnp.exp(log_w - m_new[..., None])
        decay = jnp.exp(b_last + m - m_new)
        C = decay[..., None, None] * C + jnp.einsum('bhs,bhsd,bhse->bhde', w, kc, vc)
        n = decay[..., None] * n + jnp.einsum('bhs,bhsd->bhd', w, kc)
        return (C, n, m_new), h_out

    init = (jnp.zeros((b, h, dh, dh), jnp.float32), jnp.zeros((b, h, dh), jnp.float32),
            jnp.zeros((b, h), jnp.float32))
    xs = (to_chunks(q, L), to_chunks(k, L), to_chunks(v, L), to_chunks(log_i, L), to_chunks(log_f, L))
    _, hs = lax.scan(step, init, xs)
    return from_chunks(hs)

def mlstm_mixer(x, w_in, b_gate, conv_w, norm_w, w_out):
    b, s, _ = x.shape
    H, D = MLSTM_HEADS, D_MODEL
    proj = x @ w_in
    qk, v, o, gates = jnp.split(proj, [2 * D, 3 * D, 4 * D], axis=-1)
    qk = jax.nn.silu(causal_conv(qk, conv_w))
    q, k = jnp.split(qk, 2, axis=-1)
    gates = gates.astype(jnp.float32) + b_gate.astype(jnp.float32)
    log_i = gates[..., :H].transpose(0, 2, 1)
    log_f = jax.nn.log_sigmoid(gates[..., H:]).transpose(0, 2, 1)
    q = split_heads(q, H).astype(jnp.float32) * MLSTM_DH ** -0.5
    k = split_heads(k, H).astype(jnp.float32)
    v = split_heads(v, H).astype(jnp.float32)
    hs = mlstm_chunkwise(q, k, v, log_i, log_f).astype(x.dtype)
    hs = rmsnorm(hs.transpose(0, 2, 1, 3), norm_w.reshape(H, MLSTM_DH)).reshape(b, s, D)
    return (jax.nn.sigmoid(o) * hs) @ w_out

def fox_attention(q, k, v, F):
    b, h, s, dh = q.shape
    nb = s // Q_BLOCK
    qb = jnp.moveaxis(q.reshape(b, h, nb, Q_BLOCK, dh), 2, 0)
    Fb = jnp.moveaxis(F.reshape(b, h, nb, Q_BLOCK), 2, 0)
    kpos = jnp.arange(s)
    scale = dh ** -0.5

    def block(args):
        qi, Fi, i = args
        qpos = i * Q_BLOCK + jnp.arange(Q_BLOCK)
        logits = jnp.einsum('bhqd,bhkd->bhqk', qi, k, preferred_element_type=jnp.float32) * scale
        logits = logits + Fi[..., :, None] - F[..., None, :]
        logits = jnp.where(kpos[None, :] <= qpos[:, None], logits, -jnp.inf)
        p = jax.nn.softmax(logits, axis=-1)
        return jnp.einsum('bhqk,bhkd->bhqd', p.astype(v.dtype), v)

    out = lax.map(block, (qb, Fb, jnp.arange(nb)))
    return from_chunks(out)

def fox_mixer(x, w_in, b_f, qk_norm, w_out):
    b, s, _ = x.shape
    H, D = FOX_HEADS, D_MODEL
    proj = x @ w_in
    q, k, v, o, fg = jnp.split(proj, [D, 2 * D, 3 * D, 4 * D], axis=-1)
    log_f = jax.nn.log_sigmoid(fg.astype(jnp.float32) + b_f.astype(jnp.float32))
    F = jnp.cumsum(log_f, axis=1).transpose(0, 2, 1)
    q = rmsnorm(split_heads(q, H), qk_norm[0])
    k = rmsnorm(split_heads(k, H), qk_norm[1])
    v = split_heads(v, H)
    att = fox_attention(q, k, v, F).transpose(0, 2, 1, 3).reshape(b, s, D)
    return (att * jax.nn.sigmoid(o)) @ w_out

def gla_chunked(q, k, v, log_a):
    b, h, s, dk = q.shape
    dv = v.shape[-1]
    L = GLA_CHUNK
    causal = jnp.tril(jnp.ones((L, L), dtype=bool))

    def step(S_prev, inp):
        qc, kc, vc, gc = inp
        g = jnp.cumsum(gc, axis=2)
        rel = jnp.where(causal[:, :, None], g[:, :, :, None, :] - g[:, :, None, :, :], -jnp.inf)
        A = jnp.einsum('bhtd,bhsd,bhtsd->bhts', qc, kc, jnp.exp(rel))
        o = jnp.einsum('bhts,bhse->bhte', A, vc) + jnp.einsum('bhtd,bhde->bhte', qc * jnp.exp(g), S_prev)
        g_last = g[:, :, -1]
        S_new = jnp.exp(g_last)[..., None] * S_prev + jnp.einsum(
            'bhsd,bhse->bhde', kc * jnp.exp(g_last[:, :, None, :] - g), vc)
        return S_new, o

    init = jnp.zeros((b, h, dk, dv), jnp.float32)
    xs = (to_chunks(q, L), to_chunks(k, L), to_chunks(v, L), to_chunks(log_a, L))
    _, os_ = lax.scan(step, init, xs)
    return from_chunks(os_)

def gla_mixer(x, w_in, w_gate_up, b_gate, norm_w, w_out):
    b, s, _ = x.shape
    H, D, DKT = GLA_HEADS, D_MODEL, GLA_DK_TOTAL
    proj = x @ w_in
    q, k, v, r, glr = jnp.split(proj, [DKT, 2 * DKT, 2 * DKT + D, 2 * DKT + 2 * D], axis=-1)
    log_a = jax.nn.log_sigmoid((glr @ w_gate_up).astype(jnp.float32) + b_gate.astype(jnp.float32)) / GLA_TAU
    q = split_heads(q, H).astype(jnp.float32) * GLA_DK ** -0.5
    k = split_heads(k, H).astype(jnp.float32)
    v = split_heads(v, H).astype(jnp.float32)
    log_a = split_heads(log_a, H)
    o = gla_chunked(q, k, v, log_a).astype(x.dtype)
    o = rmsnorm(o.transpose(0, 2, 1, 3), norm_w.reshape(H, GLA_DV)).reshape(b, s, D)
    return (o * jax.nn.silu(r)) @ w_out

def setup_inputs(seed: int = 0) -> dict:
    key = jax.random.key(seed)
    ks = jax.random.split(key, 24)
    D, F = D_MODEL, D_FF
    nrm = lambda k, shape, fan_in: jax.random.normal(k, shape, jnp.float32) * fan_in ** -0.5
    gain = lambda k, shape: 1.0 + 0.02 * jax.random.normal(k, shape, jnp.float32)
    small = lambda k, shape: 0.01 * jax.random.normal(k, shape, jnp.float32)
    mlstm_b = jnp.concatenate([small(ks[6], (N_A, MLSTM_HEADS)),
                               MLSTM_F_BIAS + 0.1 * jax.random.normal(ks[7], (N_A, MLSTM_HEADS), jnp.float32)], axis=-1)
    return {
        "x": jax.random.normal(ks[0], (BATCH, SEQ, D), jnp.float32),
        "norm_w": gain(ks[1], (DEPTH, 3, D)),
        "ffn_w_in": nrm(ks[2], (DEPTH, 2, D, 2 * F), D),
        "ffn_w_out": nrm(ks[3], (DEPTH, 2, F, D), F),
        "mlstm_w_in": nrm(ks[4], (N_A, D, 4 * D + 2 * MLSTM_HEADS), D),
        "mlstm_b_gate": mlstm_b,
        "mlstm_conv_w": nrm(ks[8], (N_A, CONV_WIDTH, 2 * D), CONV_WIDTH),
        "mlstm_norm_w": gain(ks[9], (N_A, D)),
        "mlstm_w_out": nrm(ks[10], (N_A, D, D), D),
        "fox_w_in": nrm(ks[11], (N_B, D, 4 * D + FOX_HEADS), D),
        "fox_b_f": FOX_F_BIAS + 0.1 * jax.random.normal(ks[12], (N_B, FOX_HEADS), jnp.float32),
        "fox_qk_norm": gain(ks[13], (N_B, 2, FOX_DH)),
        "fox_w_out": nrm(ks[14], (N_B, D, D), D),
        "gla_w_in": nrm(ks[15], (N_C, D, 2 * GLA_DK_TOTAL + 2 * D + GLA_RANK), D),
        "gla_w_gate_up": nrm(ks[16], (N_C, GLA_RANK, GLA_DK_TOTAL), GLA_RANK),
        "gla_b_gate": small(ks[17], (N_C, GLA_DK_TOTAL)),
        "gla_norm_w": gain(ks[18], (N_C, D)),
        "gla_w_out": nrm(ks[19], (N_C, D, D), D),
        "final_norm_w": gain(ks[20], (D,)),
    }

def reference(x, norm_w, ffn_w_in, ffn_w_out, mlstm_w_in, mlstm_b_gate, mlstm_conv_w, mlstm_norm_w,
              mlstm_w_out, fox_w_in, fox_b_f, fox_qk_norm, fox_w_out, gla_w_in, gla_w_gate_up, gla_b_gate,
              gla_norm_w, gla_w_out, final_norm_w):
    for layer in range(DEPTH):
        kind, j = layer % N_MIXERS, layer // N_MIXERS
        x = x + 0.5 * swiglu(rmsnorm(x, norm_w[layer, 0]), ffn_w_in[layer, 0], ffn_w_out[layer, 0])
        xn = rmsnorm(x, norm_w[layer, 1])
        if kind == 0:
            mix = mlstm_mixer(xn, mlstm_w_in[j], mlstm_b_gate[j], mlstm_conv_w[j], mlstm_norm_w[j], mlstm_w_out[j])
        elif kind == 1:
            mix = fox_mixer(xn, fox_w_in[j], fox_b_f[j], fox_qk_norm[j], fox_w_out[j])
        else:
            mix = gla_mixer(xn, gla_w_in[j], gla_w_gate_up[j], gla_b_gate[j], gla_norm_w[j], gla_w_out[j])
        x = x + mix
        x = x + 0.5 * swiglu(rmsnorm(x, norm_w[layer, 2]), ffn_w_in[layer, 1], ffn_w_out[layer, 1])
    return rmsnorm(x, final_norm_w)


_drawn_inputs = setup_inputs


def setup_inputs(seed=0):
    import zlib

    import numpy as np

    out = dict(_drawn_inputs(seed))
    spreads = {}
    factors = {'mlstm_norm_w': 3.292,
     'fox_b_f': 43.216,
     'fox_qk_norm': 8.0,
     'gla_b_gate': 8.0,
     'gla_norm_w': 20.52,
     'final_norm_w': 8.782}
    for name, (base, spread) in spreads.items():
        noise = np.random.default_rng([zlib.crc32(name.encode()), seed]).standard_normal(out[name].shape)
        drawn = base * np.exp(spread * noise) if base else spread * noise
        out[name] = __import__('jax').numpy.asarray(drawn.astype(out[name].dtype))
    for name, factor in factors.items():
        out[name] = (out[name] * factor).astype(out[name].dtype)
    return out
```

```python
from contextlib import ExitStack

import concourse.bass as bass
from concourse import mybir

F32 = mybir.dt.float32
F32R = mybir.dt.float32r
U8 = mybir.dt.uint8
ALU = mybir.AluOpType
ACT = mybir.ActivationFunctionType
AX = mybir.AxisListType

P = 128
SEQ = 256
D = 1024
F = 2816
DEPTH = 4
EPS = 1e-6
NT = SEQ // P
KT = D // P
UNIT = 2048
BANK = 512
HC = 256
NCH = F // HC
FFN_UNITS = 3 * NCH
RAW = 6
SPL = 3
AHEAD = SPL
OUT_UNITS = 4

MH, MDH = 4, 256
FH, FDH = 8, 128
GH, GDK, GDV, GRANK, GTAU = 4, 128, 256, 16, 16.0
GCOLS = {"A": 2 * MH, "B": FH, "C": GRANK}
PROJ_UNITS = {"A": 16, "B": 16, "C": 12}
NEG = -1e30

KINDS = "ABC"
SUBS = []
for _layer in range(DEPTH):
    SUBS += [("F", 2 * _layer), (KINDS[_layer % 3], _layer // 3), ("F", 2 * _layer + 1)]

FIRST_UNIT, FIRST_CHUNK, STAGE, OUT_NO, VEC = [], [], [], [], []
_u = _c = _s = _o = _v = 0
for _kind, _ in SUBS:
    FIRST_UNIT.append(_u)
    FIRST_CHUNK.append(_c)
    STAGE.append(_s)
    OUT_NO.append(_o)
    VEC.append(_v)
    _u += FFN_UNITS if _kind == "F" else PROJ_UNITS[_kind] + OUT_UNITS
    _c += NCH if _kind == "F" else PROJ_UNITS[_kind] // 2
    _s += 1 if _kind == "F" else 2
    _o += 1
    _v += 2 if _kind in "AC" else 1
N_UNITS, N_OUT, N_STAGE, N_VEC = _u, _o, _s, _v + 1

NORM_GROUPS = [(0, 0, 6), (0, 1, 7), (1, 0, 0), (1, 1, 1)]
MIX_GROUPS = {"A": [(0, 0, 6), (1, 0, 7), (0, 1, 0), (1, 1, 1)],
              "B": [(0, 0, 0), (1, 0, 1), (0, 1, 2), (1, 1, 3)],
              "C": [(0, 0, 6), (1, 0, 7), (0, 1, 0), (1, 1, 1)]}
HEAD_BANK = [6, 0, 2, 4]

GLA_PE = {0: 6, 1: 6, 2: 7, 3: 7, 4: 8, 5: 9, 6: 10, 7: 10, 8: 11}
GLA_LEVELS = 9


def build(nc, stream, x, vecs, gate_w, mg_bias, conv_w, fox_b, fox_qk, gla_up, gla_b, masks, ident_in, out):
    with ExitStack() as ctx:
        def sb(name, shape, dt=F32):
            return ctx.enter_context(nc.sbuf_tensor(name, shape, dt))

        def sems(prefix, names):
            return {n: ctx.enter_context(nc.semaphore(prefix + n)) for n in names.split()}

        raw = sb("raw", [P, RAW, UNIT])
        w_hi = sb("w_hi", [P, SPL, UNIT], F32R)
        w_lo = sb("w_lo", [P, SPL, UNIT], F32R)
        xres = sb("xres", [P, NT, D])
        src = sb("src", [P, NT, D])
        xt_hi = sb("xt_hi", [P, NT, KT, P], F32R)
        xt_lo = sb("xt_lo", [P, NT, KT, P], F32R)
        vec = sb("vec", [P, 2, D])
        nat = sb("nat", [P, 2, NT, BANK])
        silu_g = nat[:, 0, :, 0:HC]
        hid = nat[:, 1, :, 0:HC]
        og = nat[:, :, :, :].rearrange("p a t n -> p (a t n)").rearrange("p (t n) -> p t n", t=NT)
        ht_hi = sb("ht_hi", [P, 2, NT, P], F32R)
        ht_lo = sb("ht_lo", [P, 2, NT, P], F32R)
        qkt = sb("qkt", [P, 16, SEQ])
        vaug = sb("vaug", [P, NT, MH, MDH + 1])
        scr = sb("scr", [P, 18, SEQ])
        ident = sb("ident", [P, P])
        ones = sb("ones", [P, SEQ])
        lvl_mask = sb("lvl_mask", [P, 8, P], U8)
        gw_hi = sb("gw_hi", [P, DEPTH, P], F32R)
        gw_lo = sb("gw_lo", [P, DEPTH, P], F32R)
        gw_raw = scr[:, 0:2, :].rearrange("p a n -> p (a n)").rearrange("p (l n) -> p l n", l=DEPTH)
        mask_raw = scr[:, 4:8, :].rearrange("p a n -> p (a n)").rearrange("p (l n) -> p l n", l=8)
        gbias = sb("gbias", [P, DEPTH, 8])
        convw = sb("convw", [P, 2, 16, 4])
        qkw = sb("qkw", [P, 2])
        glaup = sb("glaup", [GRANK, GH * GDK])
        glab = sb("glab", [P, GH])
        ssum = sb("ssum", [P, NT])
        msum = sb("msum", [P, NT])
        rms = sb("rms", [P, NT])
        nhalf = sb("nhalf", [P, 8])
        gates = sb("gates", [P, NT, 16])
        cols = sb("cols", [P, 2, 2 * 8])
        rden = sb("rden", [P, 2, 8])
        hss = sb("hss", [P, 32])
        hms = sb("hms", [P, 32])
        hrs = sb("hrs", [P, 32])
        hrr = sb("hrr", [P, 8])
        rowmax = sb("rowmax", [P, 2, FH])
        rowsum = sb("rowsum", [P, 2, FH])
        rrow = sb("rrow", [P, 2, FH])
        ps = ctx.enter_context(nc.psum_tensor("ps", [P, 8, BANK], F32))

        landed = [ctx.enter_context(nc.semaphore(f"landed{j}")) for j in range(RAW)]
        vec_landed = [ctx.enter_context(nc.semaphore(f"vec_landed{j}")) for j in range(2)]
        G = sems("", "const x_in out_sent w_hi_ready w_lo_ready unit_used tile0_done acc0_done src_ready turned "
                     "xt_hi_ready xt_lo_ready x_new sq_ready ms_ready rms_ready silu_ready hid_ready ht_turned "
                     "ht_hi_ready ht_lo_ready gw_hi_ready gw_lo_ready init y_final masks_ready pool_chain")
        MS = [sems(f"m{j}_", "nat_ready turned tap0 taps conv_ready gate_mm gates_ready gates_turned soft rows "
                             "en_ready cols_turned cols_ready mb_done dec_arg dec_exp dec_ready s_done pm_ready "
                             "v_ready pv_done rd_ready ss_ready rs_ready og_ready ogw_ready") for j in range(2)]
        FS = sems("f_", "nat_ready sq red ss_scaled rn_ready natn_ready turned qk_ready gate_mm gates_ready "
                        "gates_turned soft rows cols_turned cols_ready fb_done fb_copied fb_ready s_done z_ready "
                        "max_ready p_ready sum_inv p_turned pt_ready pv_done v_ready og_ready y_done")
        LS = sems("g_", "nat_ready turned qk_ready gate_mm glr_ready glr_turned glrt_ready z_done z_ready soft "
                        "rows diff_ready e_ready qs_ready ks_ready lvl_done a_ready ax_ready v_ready pv_done "
                        "ss_ready rs_ready og_ready ogw_ready")
        block = ctx.enter_context(nc.Block())

        flat = scr[:, :, :].rearrange("p a n -> p (a n)")
        decay = flat[:, 0:1536].rearrange("p (h n) -> p h n", h=MH)
        probs = flat[:, 1536:3072].rearrange("p (h n) -> p h n", h=MH)
        rowbuf = flat[:, 3072:4608].rearrange("p (r n) -> p r n", n=SEQ)
        fbias = flat[:, 0:3072].rearrange("p (h n) -> p h n", h=FH)
        zbuf = flat[:, 3072:3840].rearrange("p (b n) -> p b n", b=2)
        ptbuf = flat[:, 3840:4608].rearrange("p (b n) -> p b n", b=2)
        gcum = flat[:, 0:1024]
        ebuf = flat[:, 1024:3072].rearrange("p (b n) -> p b n", b=2)
        amat = flat[:, 3072:4096].rearrange("p (m n) -> p m n", m=8)
        across = flat[:, 4096:4608].rearrange("p (h n) -> p h n", h=GH)
        squares = flat[:, 0:1536].rearrange("p (k n) -> p k n", n=MDH)
        glrt = flat[0:GRANK, 4096:4352]
        qkflat = qkt[:, :, :].rearrange("p a n -> p (a n)")
        srcflat = src[:, :, :].rearrange("p t n -> p (t n)")
        qs = [qkflat[:, 2048:3072], srcflat[:, 0:1024]]
        ks = [qkflat[:, 3072:4096], srcflat[:, 1024:2048]]

        def landed_at(u):
            return 16 * (u // RAW + 1)

        def looped(n):
            return NCH // 2 - (1 if n == len(SUBS) - 1 else 0)

        def in_stream(i, v):
            return not isinstance(i, int) or 6 * i + v < N_UNITS

        def halves(ap, size):
            return ap.rearrange("p (b two s) -> p b two s", two=2, s=size)

        @block.sync
        def _(sp):
            for t in range(NT):
                sp.dma_start(xres[:, t, :], x[0, t * P:(t + 1) * P, :]).then_inc(G["x_in"], 16)
            for u in range(RAW):
                sp.dma_start(raw[:, u, :], stream[u]).then_inc(landed[u], 16)
            with sp.Fori(1, N_UNITS // RAW) as i:
                for j in range(RAW):
                    sp.wait_ge(G["w_lo_ready"], i * RAW + (j + 1 - RAW))
                    sp.dma_start(raw[:, j, :], stream[i * RAW + j]).then_inc(landed[j], 16)
            for u in range(N_UNITS // RAW * RAW, N_UNITS):
                sp.wait_ge(G["w_lo_ready"], u + 1 - RAW)
                sp.dma_start(raw[:, u % RAW, :], stream[u]).then_inc(landed[u % RAW], 16)
            for t in range(NT):
                sp.wait_ge(G["y_final"], t + 1)
                sp.dma_start(out[0, t * P:(t + 1) * P, :], src[:, t, :]).then_inc(G["out_sent"], 16)
            sp.wait_ge(G["out_sent"], 16 * NT)

        @block.gpsimd
        def _(pool):
            consts = [(ident[:], ident_in), (mask_raw, masks), (gbias[:], mg_bias), (convw[:], conv_w),
                      (qkw[:], fox_qk), (glaup[:], gla_up), (glab[:], gla_b)]

            def load_vec(v):
                pool.dma_start(vec[:, v % 2, :], vecs[v:v + 1, :].to_broadcast([P, D])).then_inc(
                    vec_landed[v % 2], 16)

            pool.dma_start(gw_raw, gate_w).then_inc(G["const"], 16)
            load_vec(0)
            load_vec(1)
            for dst, a in consts:
                pool.dma_start(dst, a).then_inc(G["const"], 16)
            nc.gpsimd.memset(nhalf[:], -0.5).then_inc(G["init"], 1)
            nc.gpsimd.memset(ones[:], 1.0).then_inc(G["init"], 1)
            nc.gpsimd.memset(vaug[:, :, :, MDH:MDH + 1], 1.0).then_inc(G["init"], 1)
            nc.gpsimd.memset(hss[:], 1.0).then_inc(G["init"], 1)
            pool.wait_ge(G["init"], 4)
            links = [0]

            def link(ins):
                links[0] += 1
                ins.then_inc(G["pool_chain"], 1)
                pool.wait_ge(G["pool_chain"], links[0])

            def input_rms(k):
                pool.wait_ge(G["sq_ready"], NT * (k + 1))
                nc.gpsimd.tensor_scalar(msum[:], ssum[:], 1.0 / D, EPS, ALU.mult, ALU.add).then_inc(G["ms_ready"], 1)
                pool.wait_ge(G["ms_ready"], k + 1)
                nc.gpsimd.tensor_tensor(rms[:], msum[:], nhalf[:, 0:NT], ALU.pow).then_inc(G["rms_ready"], 1)

            def weigh_gate(S, v, half):
                if half == 0:
                    pool.wait_ge(vec_landed[v % 2], 16 * (v // 2 + 1))
                for t in range(NT):
                    pool.wait_ge(S["og_ready"], NT * half + t + 1)
                    part = og[:, t, half * BANK:(half + 1) * BANK]
                    nc.gpsimd.tensor_tensor(part, part, vec[:, v % 2, half * BANK:(half + 1) * BANK],
                                            ALU.mult).then_inc(S["ogw_ready"], 1)

            def head_rms(S, h, den):
                pool.wait_ge(S["ss_ready"], 2 * (h + 1))
                c = slice(2 * h, 2 * h + 2)
                link(nc.gpsimd.tensor_scalar(hms[:, c], hss[:, c], 1.0 / MDH, EPS, ALU.mult, ALU.add))
                if not den:
                    nc.gpsimd.tensor_tensor(hrr[:, c], hms[:, c], nhalf[:, 0:2], ALU.pow).then_inc(S["rs_ready"], 1)
                    return
                link(nc.gpsimd.tensor_tensor(hrs[:, c], hms[:, c], nhalf[:, 0:2], ALU.pow))
                nc.gpsimd.tensor_tensor(hrr[:, c], hrs[:, c], rden[:, 1, c], ALU.mult).then_inc(S["rs_ready"], 1)

            norm_no = 0
            for n, (kind, j) in enumerate(SUBS):
                input_rms(norm_no)
                norm_no += 1
                if VEC[n] + 2 < N_VEC:
                    pool.wait_ge(G["src_ready"], 4 * STAGE[n] + 4)
                    load_vec(VEC[n] + 2)
                if kind == "A":
                    S = MS[j]
                    pool.wait_ge(S["dec_exp"], 1)
                    for part in (decay[:, :, 0:P], decay[:, :, 2 * P:3 * P]):
                        nc.gpsimd.affine_select(out=part, in_=part, compare_op=ALU.is_ge, fill=0.0, base=0,
                                                pattern=[[0, MH], [1, P]], channel_multiplier=-1).then_inc(
                            S["dec_ready"], 1)
                    weigh_gate(S, VEC[n] + 1, 0)
                    for h in range(3):
                        head_rms(S, h, True)
                    weigh_gate(S, VEC[n] + 1, 1)
                    pool.wait_ge(S["ogw_ready"], 4)
                    if VEC[n] + 3 < N_VEC:
                        load_vec(VEC[n] + 3)
                    head_rms(S, 3, True)
                if kind == "B":
                    for m in range(4):
                        pool.wait_ge(FS["red"], 2 * (m + 1))
                        c = slice(8 * m, 8 * m + 8)
                        nc.gpsimd.tensor_scalar(hms[:, c], hss[:, c], 1.0 / FDH, EPS, ALU.mult, ALU.add).then_inc(
                            FS["ss_scaled"], 1)
                        pool.wait_ge(FS["ss_scaled"], m + 1)
                        nc.gpsimd.tensor_tensor(hrs[:, c], hms[:, c], nhalf[:, 0:8], ALU.pow).then_inc(
                            FS["rn_ready"], 1)
                    pool.wait_ge(FS["fb_copied"], 2 * FH)
                    for part, base in ((fbias[:, :, 0:P], 0), (fbias[:, :, 2 * P:3 * P], 0)):
                        nc.gpsimd.affine_select(out=part, in_=part, compare_op=ALU.is_ge, fill=NEG, base=base,
                                                pattern=[[0, FH], [-1, P]], channel_multiplier=1).then_inc(
                            FS["fb_ready"], 1)
                if kind == "C":
                    S = LS
                    pool.wait_ge(G["turned"], 4 * STAGE[n] + 4)
                    link(nc.gpsimd.memset(qs[0], 0.0))
                    link(nc.gpsimd.memset(ks[0], 0.0))
                    link(nc.gpsimd.memset(srcflat[:, :], 0.0))
                    link(nc.gpsimd.memset(amat[:, :, :], 0.0))
                    for lv in range(1, GLA_LEVELS):
                        size = 1 << (lv - 1)
                        if lv == 1:
                            pool.wait_ge(S["qk_ready"], 4)
                        pool.wait_ge(S["e_ready"], lv)
                        if lv >= 3:
                            pool.wait_ge(S["lvl_done"], lv - 1)
                        nc.gpsimd.tensor_tensor(halves(ks[lv % 2], size)[:, :, 0, :],
                                                halves(qkflat[:, 1024:2048], size)[:, :, 0, :],
                                                halves(ebuf[:, lv % 2, :], size)[:, :, 0, :],
                                                ALU.mult).then_inc(S["ks_ready"], 1)
                    for half in range(2):
                        weigh_gate(S, VEC[n] + 1, half)
                    pool.wait_ge(S["ogw_ready"], 4)
                    if VEC[n] + 3 < N_VEC:
                        load_vec(VEC[n] + 3)
                    for h in range(GH):
                        head_rms(S, h, False)
            input_rms(norm_no)

        @block.scalar
        def _(act):
            def split_hi(u, at=None, used=None):
                if u >= N_UNITS:
                    return
                act.wait_ge(landed[u % RAW], landed_at(u) if at is None else at)
                if u >= SPL:
                    act.wait_ge(G["unit_used"], u - SPL + 1 if used is None else used)
                nc.scalar.activation(w_hi[:, u % SPL, :], raw[:, u % RAW, :], ACT.Copy).then_inc(G["w_hi_ready"], 1)

            def stage_hi(s, groups, some):
                for g in some:
                    t, half, bank = groups[g]
                    act.wait_ge(G["turned"], 4 * s + g + 1)
                    nc.scalar.activation(xt_hi[:, t, 4 * half:4 * half + 4, :],
                                         ps[:, bank, :].rearrange("p (k n) -> p k n", k=4),
                                         ACT.Copy).then_inc(G["xt_hi_ready"], 1)

            def square_rows(s):
                for t in range(NT):
                    act.wait_ge(G["src_ready"], 4 * s + 2 * t + 2)
                    nc.scalar.activation(nat[:, t, :, :].rearrange("p t n -> p (t n)"), xres[:, t, :], ACT.Square,
                                         accum_out=ssum[:, t:t + 1]).then_inc(G["sq_ready"], 1)

            def wait_tile(t, chunk, unit):
                if t == 0:
                    act.wait_ge(G["tile0_done"], chunk + 1)
                else:
                    act.wait_ge(G["unit_used"], unit + 1)

            def ffn_chunk(chunk, ua, first, split_at):
                for t in range(NT):
                    wait_tile(t, chunk, ua + 1)
                    if first:
                        act.wait_ge(G["rms_ready"], first)
                    nc.scalar.activation(silu_g[:, t, :], ps[:, 4 + t, 0:HC], ACT.Silu,
                                         scale=rms[:, t:t + 1]).then_inc(G["silu_ready"], 1)

            def hidden_hi(count):
                act.wait_ge(G["ht_turned"], count)
                nc.scalar.activation(ht_hi[:, :, :, :], ps[:, 6, :].rearrange("p (k t n) -> p k t n", k=2, t=NT),
                                     ACT.Copy).then_inc(G["ht_hi_ready"], 1)

            def ffn(n, j, norm_no):
                u0, c0, h0 = FIRST_UNIT[n], FIRST_CHUNK[n], NCH * j
                split_hi(u0 + 3)
                ffn_chunk(c0, u0, norm_no + 1, None)
                split_hi(u0 + 4)

                def body(i):
                    for b in range(2):
                        ua = u0 + 2 + 3 * b
                        hidden_hi(i * 2 + (h0 + b + 1))
                        for q in range(3):
                            if q == 1:
                                ffn_chunk(i * 2 + (c0 + 1 + b), i * 6 + ua, 0, None)
                            v = ua + AHEAD + q
                            if not in_stream(i, v):
                                continue
                            split_hi(v, at=i * 16 + landed_at(v), used=i * 6 + (v - SPL + 1))

                with act.Fori(0, looped(n)) as i:
                    body(i)
                for i in range(looped(n), NCH // 2):
                    body(i)
                hidden_hi(h0 + NCH)

            def head_square(S, h, den):
                act.wait_ge(S["pv_done"], h + 1)
                if den:
                    act.wait_ge(S["rd_ready"], 3 * (h + 1))
                for t in range(NT):
                    k = 2 * h + t
                    q = k % 6
                    if k >= 6:
                        act.wait_ge(S["ss_ready"], k - 5)
                    nc.scalar.activation(squares[:, q, :], ps[:, HEAD_BANK[h] + t, 0:MDH],
                                         ACT.Square, scale=rden[:, 1, k:k + 1] if den else 1.0,
                                         accum_out=hss[:, k:k + 1]).then_inc(S["ss_ready"], 1)

            def log_sigmoid_part(S, gate_ap, tmp, ready, value):
                act.wait_ge(ready, value)
                nc.scalar.activation(tmp, gate_ap, ACT.Abs).then_inc(S["soft"], 1)
                act.wait_ge(S["soft"], 1)
                nc.scalar.activation(tmp, tmp, ACT.Exp, scale=-1.0).then_inc(S["soft"], 1)
                act.wait_ge(S["soft"], 2)
                nc.scalar.activation(tmp, tmp, ACT.Ln, bias=1.0).then_inc(S["soft"], 1)

            def v_piece(t, m, kind):
                if kind == "B":
                    return vaug[:, t, :, :].rearrange("p h n -> p (h n)")[:, m * BANK:(m + 1) * BANK]
                return vaug[:, t, 2 * m:2 * m + 2, 0:MDH]

            def gate_half(t, m):
                return og[:, t, m * BANK:(m + 1) * BANK]

            def plan_a(n, j):
                S, c0, u0 = MS[j], FIRST_CHUNK[n], FIRST_UNIT[n]
                slots = {k: [] for k in range(16)}

                def evac(m):
                    for t in range(NT):
                        wait_tile(t, c0 + m, u0 + 2 * m + 1)
                        bank = ps[:, 4 + t, :]
                        r = rms[:, t:t + 1]
                        if m < 4:
                            nc.scalar.activation(nat[:, m % 2, t, :], bank, ACT.Copy, scale=r).then_inc(
                                S["nat_ready"], 1)
                        elif m < 6:
                            nc.scalar.activation(v_piece(t, m - 4, "A"), bank.rearrange("p (h n) -> p h n", h=2),
                                                 ACT.Copy, scale=r).then_inc(S["v_ready"], 1)
                        else:
                            if m == 6 and t == 0:
                                act.wait_ge(S["turned"], 4)
                            nc.scalar.activation(gate_half(t, m - 6), bank, ACT.Sigmoid, scale=r).then_inc(
                                S["og_ready"], 1)

                def first_tap(m):
                    act.wait_ge(S["turned"], m + 1)
                    for c in range(4):
                        ct = 4 * m + c
                        nc.scalar.activation(qkt[:, ct, :], ps[:, 2 * (m % 2) + c // 2, (c % 2) * SEQ:(c % 2 + 1) * SEQ],
                                             ACT.Copy, scale=convw[:, j, ct, 3:4]).then_inc(S["tap0"], 1)

                def conv_silu(m):
                    act.wait_ge(S["taps"], 12 * (m + 1))
                    part = qkt[:, 4 * m:4 * m + 4, :]
                    nc.scalar.activation(part, part, ACT.Silu).then_inc(S["conv_ready"], 1)

                def soft():
                    log_sigmoid_part(S, ps[0:MH, 7, SEQ:2 * SEQ], rowbuf[0:MH, 0, :], S["gates_turned"], 1)

                def en():
                    act.wait_ge(S["rows"], 5)
                    nc.scalar.activation(rowbuf[0:MH, 5, :], rowbuf[0:MH, 5, :], ACT.Exp, scale=-1.0).then_inc(
                        S["en_ready"], 1)

                def cols_copy():
                    act.wait_ge(S["cols_turned"], 1)
                    nc.scalar.activation(cols[:, :, 0:8], ps[:, 6, 0:16].rearrange("p (a n) -> p a n", a=2),
                                         ACT.Copy).then_inc(S["cols_ready"], 1)

                def dec_exp():
                    act.wait_ge(S["dec_arg"], 8)
                    nc.scalar.activation(decay[:, :, :], decay[:, :, :], ACT.Exp, scale=-1.0).then_inc(S["dec_exp"], 1)

                for m in range(8):
                    slots[2 * m + 1].append(lambda m=m: evac(m))
                for m in range(4):
                    slots[2 * m + 2].append(lambda m=m: first_tap(m))
                    slots[2 * m + 3].append(lambda m=m: conv_silu(m))
                slots[1].append(soft)
                slots[2].append(en)
                slots[3].append(cols_copy)
                slots[6].append(dec_exp)
                for h in range(3):
                    slots[13].append(lambda h=h: head_square(S, h, True))
                slots[15].append(lambda: head_square(S, 3, True))
                return slots

            def plan_b(n, j):
                S, c0, u0 = FS, FIRST_CHUNK[n], FIRST_UNIT[n]
                slots = {k: [] for k in range(16)}

                def evac(m):
                    for t in range(NT):
                        wait_tile(t, c0 + m, u0 + 2 * m + 1)
                        bank = ps[:, 4 + t, :]
                        r = rms[:, t:t + 1]
                        if m < 4:
                            nc.scalar.activation(nat[:, m % 2, t, :], bank, ACT.Copy, scale=r).then_inc(
                                S["nat_ready"], 1)
                        elif m < 6:
                            nc.scalar.activation(v_piece(t, m - 4, "B"), bank, ACT.Copy, scale=r).then_inc(
                                S["v_ready"], 1)
                        else:
                            if m == 6 and t == 0:
                                act.wait_ge(S["turned"], 4)
                            nc.scalar.activation(gate_half(t, m - 6), bank, ACT.Sigmoid, scale=r).then_inc(
                                S["og_ready"], 1)

                def qk_evac(m):
                    act.wait_ge(S["turned"], m + 1)
                    for b in range(2):
                        nc.scalar.activation(qkt[:, 4 * m + 2 * b:4 * m + 2 * b + 2, :],
                                             ps[:, 2 * (m % 2) + b, :].rearrange("p (h n) -> p h n", h=2),
                                             ACT.Copy, scale=qkw[:, m // 2:m // 2 + 1]).then_inc(S["qk_ready"], 1)

                def soft():
                    log_sigmoid_part(S, ps[0:FH, 7, 0:SEQ], zbuf[0:FH, 0, 0:SEQ], S["gates_turned"], 1)

                def cols_copy():
                    act.wait_ge(S["cols_turned"], 1)
                    nc.scalar.activation(cols[:, 0, :], ps[:, 7, 0:16], ACT.Copy).then_inc(S["cols_ready"], 1)

                def fb_copy(q):
                    act.wait_ge(S["fb_done"], q + 1)
                    if q == 0:
                        act.wait_ge(S["cols_ready"], 1)
                    for h in (2 * q, 2 * q + 1):
                        row = ps[:, 6 + q % 2, (h % 2) * SEQ:(h % 2 + 1) * SEQ]
                        nc.scalar.activation(fbias[:, h, 0:P], row[:, 0:P], ACT.Identity, scale=-1.0,
                                             bias=cols[:, 0, h:h + 1]).then_inc(S["fb_copied"], 1)
                        nc.scalar.activation(fbias[:, h, P:3 * P], row, ACT.Identity, scale=-1.0,
                                             bias=cols[:, 0, FH + h:FH + h + 1]).then_inc(S["fb_copied"], 1)

                def exps(h):
                    act.wait_ge(S["max_ready"], 2 * (h + 1))
                    for t, c in ((0, slice(0, P)), (1, slice(P, 3 * P))):
                        nc.scalar.activation(zbuf[:, h % 2, c], zbuf[:, h % 2, c], ACT.Exp,
                                             bias=rowmax[:, t, h:h + 1],
                                             accum_out=rowsum[:, t, h:h + 1]).then_inc(S["p_ready"], 1)

                def pt_copy(h):
                    act.wait_ge(S["p_turned"], h + 1)
                    if h >= 2:
                        act.wait_ge(S["pv_done"], h - 1)
                    nc.scalar.activation(ptbuf[:, h % 2, :], ps[:, 2 + h % 2, 0:3 * P], ACT.Copy).then_inc(
                        S["pt_ready"], 1)

                for m in range(8):
                    slots[2 * m + 1].append(lambda m=m: evac(m))
                for m in range(4):
                    slots[2 * m + 3].append(lambda m=m: qk_evac(m))
                slots[1].append(soft)
                slots[4].append(cols_copy)
                for q in range(4):
                    slots[4 + q].append(lambda q=q: fb_copy(q))
                for k in range(4):
                    slots[10 + k] += [lambda h=2 * k: exps(h), lambda h=2 * k + 1: exps(h)]
                    slots[11 + k] += [lambda h=2 * k: pt_copy(h), lambda h=2 * k + 1: pt_copy(h)]
                return slots

            def plan_c(n, j):
                S, c0, u0 = LS, FIRST_CHUNK[n], FIRST_UNIT[n]
                slots = {k: [] for k in range(12)}

                def evac(m):
                    for t in range(NT):
                        wait_tile(t, c0 + m, u0 + 2 * m + 1)
                        bank = ps[:, 4 + t, :]
                        r = rms[:, t:t + 1]
                        if m < 2:
                            nc.scalar.activation(nat[:, m % 2, t, :], bank, ACT.Copy, scale=r).then_inc(
                                S["nat_ready"], 1)
                        elif m < 4:
                            nc.scalar.activation(v_piece(t, m - 2, "C"), bank.rearrange("p (h n) -> p h n", h=2),
                                                 ACT.Copy, scale=r).then_inc(S["v_ready"], 1)
                        else:
                            nc.scalar.activation(gate_half(t, m - 4), bank, ACT.Silu, scale=r).then_inc(
                                S["og_ready"], 1)

                def qk_evac(m):
                    act.wait_ge(S["turned"], m + 1)
                    for b in range(2):
                        nc.scalar.activation(qkt[:, 4 * m + 2 * b:4 * m + 2 * b + 2, :],
                                             ps[:, 2 * m + b, :].rearrange("p (h n) -> p h n", h=2),
                                             ACT.Copy, scale=(GDK ** -0.5 if m == 0 else 1.0)).then_inc(
                            S["qk_ready"], 1)

                def glr_copy():
                    act.wait_ge(S["glr_turned"], 1)
                    nc.scalar.activation(glrt, ps[0:GRANK, 7, 0:SEQ], ACT.Copy).then_inc(S["glrt_ready"], 1)

                def z_bias():
                    act.wait_ge(S["z_done"], 1)
                    for h in range(GH):
                        nc.scalar.activation(ebuf[:, 1, h * SEQ:(h + 1) * SEQ],
                                             ps[:, 6 + h // 2, (h % 2) * SEQ:(h % 2 + 1) * SEQ], ACT.Identity,
                                             bias=glab[:, h:h + 1]).then_inc(S["z_ready"], 1)
                    log_sigmoid_part(S, ebuf[:, 1, :], ebuf[:, 0, :], S["z_ready"], GH)

                def decay_exp(lv):
                    act.wait_ge(S["diff_ready"], 2 * lv)
                    nc.scalar.activation(ebuf[:, lv % 2, :], ebuf[:, lv % 2, :], ACT.Exp,
                                         scale=1.0 / GTAU).then_inc(S["e_ready"], 1)

                def across_copy():
                    act.wait_ge(S["lvl_done"], GLA_LEVELS)
                    nc.scalar.activation(across[:, :, :], ps[:, 0, :].rearrange("p (h n) -> p h n", h=GH),
                                         ACT.Copy).then_inc(S["ax_ready"], 1)

                for m in range(6):
                    slots[2 * m + 1].append(lambda m=m: evac(m))
                for m in range(2):
                    slots[2 * m + 2].append(lambda m=m: qk_evac(m))
                slots[1].append(glr_copy)
                slots[2].append(z_bias)
                for lv in range(1, GLA_LEVELS):
                    slots[GLA_PE[lv] - 1].append(lambda lv=lv: decay_exp(lv))
                slots[11].append(across_copy)
                for h in range(GH):
                    slots[11].append(lambda h=h: head_square(S, h, False))
                return slots

            act.wait_ge(G["const"], 16 * 8)
            for lay in range(DEPTH):
                nc_cols = KT * GCOLS[KINDS[lay % 3]]
                nc.scalar.activation(gw_hi[:, lay, 0:nc_cols], gw_raw[:, lay, 0:nc_cols], ACT.Copy).then_inc(
                    G["gw_hi_ready"], 1)
            for u in range(AHEAD):
                split_hi(u)
            for n, (kind, j) in enumerate(SUBS):
                s = STAGE[n]
                stage_hi(s, NORM_GROUPS, range(4))
                square_rows(s)
                if n:
                    split_hi(FIRST_UNIT[n] + AHEAD - 1)
                if kind == "F":
                    ffn(n, j, n)
                    continue
                act.wait_ge(G["rms_ready"], n + 1)
                slots = {"A": plan_a, "B": plan_b, "C": plan_c}[kind](n, j)
                pu = PROJ_UNITS[kind]
                for k in range(pu):
                    for step in slots[k]:
                        step()
                    if k < pu - 1:
                        split_hi(FIRST_UNIT[n] + k + AHEAD)
                stage_hi(s + 1, MIX_GROUPS[kind], range(4))
                split_hi(FIRST_UNIT[n] + pu - 1 + AHEAD)
                for k in range(OUT_UNITS - 1):
                    split_hi(FIRST_UNIT[n] + pu + k + AHEAD)
            square_rows(N_STAGE)

        @block.vector
        def _(dve):
            def split_lo(u, count=None):
                if u >= N_UNITS:
                    return
                dve.wait_ge(G["w_hi_ready"], u + 1 if count is None else count)
                nc.vector.tensor_tensor(w_lo[:, u % SPL, :], raw[:, u % RAW, :], w_hi[:, u % SPL, :].bitcast(F32),
                                        ALU.subtract).then_inc(G["w_lo_ready"], 1)

            def stage_lo(s, groups, some):
                for g in some:
                    t, half, bank = groups[g]
                    dve.wait_ge(G["xt_hi_ready"], 4 * s + g + 1)
                    nc.vector.tensor_tensor(xt_lo[:, t, 4 * half:4 * half + 4, :],
                                            ps[:, bank, :].rearrange("p (k n) -> p k n", k=4),
                                            xt_hi[:, t, 4 * half:4 * half + 4, :].bitcast(F32),
                                            ALU.subtract).then_inc(G["xt_lo_ready"], 1)

            def wait_acc(o, t, unit):
                if t == 0:
                    dve.wait_ge(G["acc0_done"], o + 1)
                else:
                    dve.wait_ge(G["unit_used"], unit + 1)

            def new_x(n, t):
                wait_acc(n - 1, t, FIRST_UNIT[n] - 1 if n < len(SUBS) else N_UNITS - 1)
                scale = 0.5 if SUBS[n - 1][0] == "F" else 1.0
                for half in range(2):
                    part = xres[:, t, half * BANK:(half + 1) * BANK]
                    nc.vector.scalar_tensor_tensor(out=part, in0=ps[:, 2 * t + half, :], scalar=scale, in1=part,
                                                   op0=ALU.mult, op1=ALU.add).then_inc(G["x_new"], 1)

            def weigh_x(n, t):
                v = VEC[n]
                if t == 0:
                    dve.wait_ge(vec_landed[v % 2], 16 * (v // 2 + 1))
                for half in range(2):
                    c = slice(half * BANK, (half + 1) * BANK)
                    if n == 0:
                        dve.wait_ge(G["x_in"], 16 * NT)
                    else:
                        dve.wait_ge(G["x_new"], 4 * (n - 1) + 2 * t + half + 1)
                    nc.vector.tensor_tensor(src[:, t, c], xres[:, t, c], vec[:, v % 2, c], ALU.mult).then_inc(
                        G["src_ready"], 1)

            def hidden(count, first):
                for t in range(NT):
                    dve.wait_ge(G["silu_ready"], count + (t + 1))
                    nc.vector.scalar_tensor_tensor(out=hid[:, t, :], in0=ps[:, 4 + t, HC:2 * HC],
                                                   scalar=rms[:, t:t + 1], in1=silu_g[:, t, :],
                                                   op0=ALU.mult, op1=ALU.mult).then_inc(G["hid_ready"], 1)

            def hidden_lo(count):
                dve.wait_ge(G["ht_hi_ready"], count)
                nc.vector.tensor_tensor(ht_lo[:, :, :, :], ps[:, 6, :].rearrange("p (k t n) -> p k t n", k=2, t=NT),
                                        ht_hi[:, :, :, :].bitcast(F32), ALU.subtract).then_inc(G["ht_lo_ready"], 1)

            def ffn(n, j):
                u0, h0 = FIRST_UNIT[n], NCH * j
                split_lo(u0 + 3)
                hidden(2 * h0, True)
                split_lo(u0 + 4)

                def body(i):
                    for b in range(2):
                        ua = u0 + 2 + 3 * b
                        hidden_lo(i * 2 + (h0 + b + 1))
                        for q in range(3):
                            if q == 1:
                                hidden(i * 4 + 2 * (h0 + 1 + b), False)
                            v = ua + AHEAD + q
                            if in_stream(i, v):
                                split_lo(v, count=i * 6 + (v + 1))

                with dve.Fori(0, looped(n)) as i:
                    body(i)
                for i in range(looped(n), NCH // 2):
                    body(i)
                hidden_lo(h0 + NCH)

            def head_out(S, s, h, den):
                dve.wait_ge(S["rs_ready"], h + 1)
                for t in range(NT):
                    dve.wait_ge(S["ogw_ready"], NT * (h // 2) + t + 1)
                    ins = nc.vector.scalar_tensor_tensor(
                        out=src[:, t, h * MDH:(h + 1) * MDH], in0=ps[:, HEAD_BANK[h] + t, 0:MDH],
                        scalar=hrr[:, 2 * h + t:2 * h + t + 1], in1=og[:, t, h * MDH:(h + 1) * MDH],
                        op0=ALU.mult, op1=ALU.mult)
                    if h % 2:
                        ins.then_inc(G["src_ready"], 1)

            def plan_a(n, j):
                S, s = MS[j], STAGE[n]
                slots = {k: [] for k in range(16)}

                def gate_bias():
                    dve.wait_ge(S["gate_mm"], 1)
                    dve.wait_ge(G["rms_ready"], n + 1)
                    for t in range(NT):
                        nc.vector.scalar_tensor_tensor(out=gates[:, t, 0:8], in0=ps[:, 6, 16 * t:16 * t + 8],
                                                       scalar=rms[:, t:t + 1], in1=gbias[:, 2 * j + j, :],
                                                       op0=ALU.mult, op1=ALU.add).then_inc(S["gates_ready"], 1)

                def rows():
                    f, i = ps[0:MH, 7, SEQ:2 * SEQ], ps[0:MH, 7, 0:SEQ]
                    r = [rowbuf[0:MH, k, :] for k in range(6)]
                    dve.wait_ge(S["soft"], 3)
                    nc.vector.scalar_tensor_tensor(out=r[1], in0=f, scalar=0.0, in1=r[0], op0=ALU.min,
                                                   op1=ALU.subtract).then_inc(S["rows"], 1)
                    dve.wait_ge(S["rows"], 1)
                    nc.vector.tensor_tensor_scan(r[2], ones[0:MH, :], r[1], 0.0, ALU.mult, ALU.add).then_inc(
                        S["rows"], 1)
                    dve.wait_ge(S["rows"], 2)
                    nc.vector.tensor_tensor(r[3], i, r[2], ALU.subtract).then_inc(S["rows"], 1)
                    dve.wait_ge(S["rows"], 3)
                    nc.vector.tensor_tensor_scan(r[4], ones[0:MH, :], r[3], 0.0, ALU.mult, ALU.max).then_inc(
                        S["rows"], 1)
                    dve.wait_ge(S["rows"], 4)
                    nc.vector.tensor_tensor(r[5], r[2], r[4], ALU.add).then_inc(S["rows"], 1)

                def taps(m):
                    for tap in range(1, 4):
                        for c in range(4):
                            ct = 4 * m + c
                            if tap == 1:
                                dve.wait_ge(S["tap0"], 4 * m + 2 * (c // 2) + 2)
                            elif c == 0:
                                dve.wait_ge(S["taps"], 12 * m + 4 * (tap - 1))
                            bank = ps[:, 2 * (m % 2) + c // 2, (c % 2) * SEQ:(c % 2 + 1) * SEQ]
                            nc.vector.scalar_tensor_tensor(out=qkt[:, ct, tap:SEQ], in0=bank[:, 0:SEQ - tap],
                                                           scalar=convw[:, j, ct, 3 - tap:4 - tap],
                                                           in1=qkt[:, ct, tap:SEQ], op0=ALU.mult,
                                                           op1=ALU.add).then_inc(S["taps"], 1)

                def decay_args():
                    dve.wait_ge(S["cols_ready"], 1)
                    dve.wait_ge(S["mb_done"], 1)
                    for h in range(MH):
                        row = ps[:, 6 + h // 2, (h % 2) * SEQ:(h % 2 + 1) * SEQ]
                        for t, c, r in ((0, slice(0, SEQ), row), (1, slice(SEQ, SEQ + P), row[:, P:SEQ])):
                            a = cols[:, 0, 4 * t + h:4 * t + h + 1]
                            nc.vector.tensor_scalar(decay[:, h, c], r, a, a, ALU.max, ALU.subtract).then_inc(
                                S["dec_arg"], 1)

                def pm(h):
                    dve.wait_ge(S["s_done"], h + 1)
                    if h == 0:
                        dve.wait_ge(S["dec_ready"], 2)
                    nc.vector.scalar_tensor_tensor(out=probs[:, h, :], in0=ps[:, h, 0:3 * P],
                                                   scalar=MDH ** -0.5, in1=decay[:, h, :],
                                                   op0=ALU.mult, op1=ALU.mult).then_inc(S["pm_ready"], 1)

                def dens(h):
                    dve.wait_ge(S["pv_done"], h + 1)
                    c = slice(2 * h, 2 * h + 2)
                    den = ps[:, HEAD_BANK[h]:HEAD_BANK[h] + 2, MDH]
                    guard = cols[:, 1, 0:8].rearrange("p (t h) -> p h t", t=2)[:, h, :]
                    nc.vector.scalar_tensor_tensor(out=rden[:, 0, c], in0=den, scalar=-1.0, in1=guard,
                                                   op0=ALU.mult, op1=ALU.max).then_inc(S["rd_ready"], 1)
                    dve.wait_ge(S["rd_ready"], 3 * h + 1)
                    nc.vector.tensor_tensor(rden[:, 0, c], den, rden[:, 0, c], ALU.max).then_inc(S["rd_ready"], 1)
                    dve.wait_ge(S["rd_ready"], 3 * h + 2)
                    nc.vector.reciprocal(rden[:, 1, c], rden[:, 0, c]).then_inc(S["rd_ready"], 1)

                slots[0].append(gate_bias)
                slots[1].append(rows)
                slots[5].append(decay_args)
                for m in range(4):
                    slots[2 * m + 2].append(lambda m=m: taps(m))
                for h in range(MH):
                    slots[11].append(lambda h=h: pm(h))
                for h in range(3):
                    slots[13].append(lambda h=h: dens(h))
                for h in range(3):
                    slots[14 if h < 2 else 15].append(lambda h=h: head_out(S, s, h, True))
                slots[15].insert(0, lambda: dens(3))
                slots[15].append(lambda: head_out(S, s, 3, True))
                return slots

            def plan_b(n, j):
                S, s = FS, STAGE[n]
                slots = {k: [] for k in range(16)}

                def gate_bias():
                    dve.wait_ge(S["gate_mm"], 1)
                    dve.wait_ge(G["rms_ready"], n + 1)
                    for t in range(NT):
                        nc.vector.scalar_tensor_tensor(out=gates[:, t, 0:8], in0=ps[:, 6, 16 * t:16 * t + 8],
                                                       scalar=rms[:, t:t + 1], in1=gbias[:, 1, :],
                                                       op0=ALU.mult, op1=ALU.add).then_inc(S["gates_ready"], 1)

                def rows():
                    dve.wait_ge(S["soft"], 3)
                    nc.vector.scalar_tensor_tensor(out=ptbuf[0:FH, 0, 0:SEQ], in0=ps[0:FH, 7, 0:SEQ], scalar=0.0,
                                                   in1=zbuf[0:FH, 0, 0:SEQ], op0=ALU.min,
                                                   op1=ALU.subtract).then_inc(S["rows"], 1)
                    dve.wait_ge(S["rows"], 1)
                    nc.vector.tensor_tensor_scan(ptbuf[0:FH, 1, 0:SEQ], ones[0:FH, :], ptbuf[0:FH, 0, 0:SEQ], 0.0,
                                                 ALU.mult, ALU.add).then_inc(S["rows"], 1)

                def square(m):
                    for t in range(NT):
                        dve.wait_ge(S["nat_ready"], 2 * m + t + 1)
                        if m == 0 and t == 0:
                            dve.wait_ge(G["turned"], 4 * s + 4)
                        if 2 * m + t >= 2:
                            dve.wait_ge(S["red"], 2 * m + t - 1)
                        part = nat[:, m % 2, t, :]
                        nc.vector.tensor_tensor(src[:, t, 0:BANK], part, part, ALU.mult).then_inc(S["sq"], 1)
                    for t in range(NT):
                        dve.wait_ge(S["sq"], 2 * m + t + 1)
                        nc.vector.tensor_reduce(hss[:, 8 * m + 4 * t:8 * m + 4 * t + 4],
                                                src[:, t, 0:BANK].rearrange("p (h n) -> p h n", h=4), AX.X,
                                                ALU.add).then_inc(S["red"], 1)

                def normed(m):
                    dve.wait_ge(S["rn_ready"], m + 1)
                    for t in range(NT):
                        part = nat[:, m % 2, t, :].rearrange("p (h n) -> p h n", h=4)
                        r = hrs[:, 8 * m + 4 * t:8 * m + 4 * t + 4].unsqueeze(2).to_broadcast([P, 4, FDH])
                        nc.vector.tensor_tensor(part, part, r, ALU.mult).then_inc(S["natn_ready"], 1)

                def logits(h):
                    dve.wait_ge(S["s_done"], h + 1)
                    if h == 0:
                        dve.wait_ge(S["fb_ready"], 2)
                    nc.vector.scalar_tensor_tensor(out=zbuf[:, h % 2, :], in0=ps[:, h % 2, 0:3 * P],
                                                   scalar=FDH ** -0.5, in1=fbias[:, h, :], op0=ALU.mult,
                                                   op1=ALU.add).then_inc(S["z_ready"], 1)
                    dve.wait_ge(S["z_ready"], h + 1)
                    for t, c in ((0, slice(0, P)), (1, slice(P, 3 * P))):
                        nc.vector.tensor_reduce(rowmax[:, t, h:h + 1], zbuf[:, h % 2, c], AX.X, ALU.max,
                                                negate=True).then_inc(S["max_ready"], 1)

                def inverses(h):
                    dve.wait_ge(S["p_ready"], 2 * (h + 1))
                    nc.vector.reciprocal(rrow[:, :, h:h + 1], rowsum[:, :, h:h + 1]).then_inc(S["sum_inv"], 1)

                def outs(h):
                    dve.wait_ge(S["pv_done"], h // 2 * 2 + 2)
                    dve.wait_ge(S["sum_inv"], h + 1)
                    for t in range(NT):
                        dve.wait_ge(S["og_ready"], NT * (h // 4) + t + 1)
                        c = slice(h * FDH, (h + 1) * FDH)
                        q = (h % 2) * SEQ + t * P
                        ins = nc.vector.scalar_tensor_tensor(
                            out=src[:, t, c], in0=ps[:, 6 + (h // 2) % 2, q:q + P],
                            scalar=rrow[:, t, h:h + 1], in1=og[:, t, c], op0=ALU.mult, op1=ALU.mult)
                        ins.then_inc(G["src_ready"] if h % 4 == 3 else S["y_done"], 1)

                slots[0].append(gate_bias)
                slots[1].append(rows)
                for m in range(4):
                    slots[2 * m + 1].append(lambda m=m: square(m))
                    slots[2 * m + 2].append(lambda m=m: normed(m))
                for k in range(4):
                    slots[10 + k] += [lambda h=2 * k: logits(h), lambda h=2 * k + 1: logits(h)]
                    slots[11 + k] += [lambda h=2 * k: inverses(h), lambda h=2 * k + 1: inverses(h)]
                for h in range(4):
                    slots[13].append(lambda h=h: outs(h))
                for h in range(4, 8):
                    slots[14 if h < 4 else 15].append(lambda h=h: outs(h))
                return slots

            def plan_c(n, j):
                S, s = LS, STAGE[n]
                slots = {k: [] for k in range(12)}

                def glr():
                    dve.wait_ge(S["gate_mm"], 1)
                    dve.wait_ge(G["rms_ready"], n + 1)
                    for t in range(NT):
                        nc.vector.tensor_scalar(gates[:, t, :], ps[:, 6, 16 * t:16 * t + 16], rms[:, t:t + 1], None,
                                                ALU.mult).then_inc(S["glr_ready"], 1)

                def rows():
                    dve.wait_ge(S["soft"], 3)
                    nc.vector.scalar_tensor_tensor(out=ebuf[:, 0, :], in0=ebuf[:, 1, :], scalar=0.0,
                                                   in1=ebuf[:, 0, :], op0=ALU.min,
                                                   op1=ALU.subtract).then_inc(S["rows"], 1)
                    dve.wait_ge(S["rows"], 1)
                    for h in range(GH):
                        c = slice(h * SEQ, (h + 1) * SEQ)
                        nc.vector.tensor_tensor_scan(gcum[:, c], ones[:, :], ebuf[:, 0, c], 0.0, ALU.mult,
                                                     ALU.add).then_inc(S["rows"], 1)

                def diff(lv):
                    size = 1 << (lv - 1)
                    g = halves(gcum, size)
                    e = halves(ebuf[:, lv % 2, :], size)
                    ref = g[:, :, 0, size - 1:size].to_broadcast([P, 512 // size, size])
                    if lv == 1:
                        dve.wait_ge(S["rows"], 1 + GH)
                    if lv >= 3:
                        dve.wait_ge(S["ks_ready"], lv - 2)
                        dve.wait_ge(S["qs_ready"], lv - 2)
                    nc.vector.tensor_tensor(e[:, :, 1, :], g[:, :, 1, :], ref, ALU.subtract).then_inc(
                        S["diff_ready"], 1)
                    nc.vector.tensor_tensor(e[:, :, 0, :], ref, g[:, :, 0, :], ALU.subtract).then_inc(
                        S["diff_ready"], 1)

                def queries(lv):
                    size = 1 << (lv - 1)
                    dve.wait_ge(S["e_ready"], lv)
                    if lv == 1:
                        dve.wait_ge(S["qk_ready"], 4)
                        dve.wait_ge(S["ks_ready"], 1)
                    if lv >= 3:
                        dve.wait_ge(S["lvl_done"], lv - 1)
                    nc.vector.tensor_tensor(halves(qs[lv % 2], size)[:, :, 1, :],
                                            halves(qkflat[:, 0:1024], size)[:, :, 1, :],
                                            halves(ebuf[:, lv % 2, :], size)[:, :, 1, :],
                                            ALU.mult).then_inc(S["qs_ready"], 1)

                def gather(lv):
                    dve.wait_ge(S["lvl_done"], lv + 1)
                    if lv == 0:
                        dve.wait_ge(S["ks_ready"], 1)
                    else:
                        dve.wait_ge(S["a_ready"], lv)
                    b = 2 * (lv % 2)
                    nc.vector.copy_predicated(amat[:, :, :],
                                              lvl_mask[:, lv:lv + 1, :].to_broadcast([P, 8, P]),
                                              ps[:, b:b + 2, :].rearrange("p b (m n) -> p (b m) n", n=P)).then_inc(
                        S["a_ready"], 1)

                slots[0].append(glr)
                slots[2].append(rows)
                slots[4].append(lambda: diff(1))
                for lv in range(1, GLA_LEVELS):
                    k = GLA_PE[lv] - 1
                    if lv + 1 < GLA_LEVELS:
                        slots[k].append(lambda lv=lv: diff(lv + 1))
                    slots[k].append(lambda lv=lv: queries(lv))
                    slots[GLA_PE[lv - 1]].append(lambda lv=lv: gather(lv - 1)) if False else None
                return slots, gather, [lambda h=h: head_out(S, s, h, False) for h in range(GH)]

            dve.wait_ge(G["init"], 4)
            dve.wait_ge(G["const"], 16 * 8)
            nc.vector.tensor_copy(lvl_mask[:], mask_raw).then_inc(G["masks_ready"], 1)
            for lay in range(DEPTH):
                nc_cols = KT * GCOLS[KINDS[lay % 3]]
                dve.wait_ge(G["gw_hi_ready"], lay + 1)
                nc.vector.tensor_tensor(gw_lo[:, lay, 0:nc_cols], gw_raw[:, lay, 0:nc_cols],
                                        gw_hi[:, lay, 0:nc_cols].bitcast(F32), ALU.subtract).then_inc(
                    G["gw_lo_ready"], 1)
            for u in range(AHEAD):
                split_lo(u)
            for n, (kind, j) in enumerate(SUBS):
                s = STAGE[n]
                for t in range(NT):
                    if n:
                        new_x(n, t)
                    weigh_x(n, t)
                    stage_lo(s, NORM_GROUPS, (2 * t, 2 * t + 1))
                if n:
                    split_lo(FIRST_UNIT[n] + AHEAD - 1)
                if kind == "F":
                    ffn(n, j)
                    continue
                pu = PROJ_UNITS[kind]
                if kind == "C":
                    slots, gather, tail = plan_c(n, j)
                    for lv in range(GLA_LEVELS - 1):
                        slots[GLA_PE[lv]].append(lambda lv=lv: gather(lv))
                    slots[11] += tail
                else:
                    slots = {"A": plan_a, "B": plan_b}[kind](n, j)
                for k in range(pu):
                    for step in slots[k]:
                        step()
                    if k < pu - 1:
                        split_lo(FIRST_UNIT[n] + k + AHEAD)
                stage_lo(s + 1, MIX_GROUPS[kind], range(4))
                split_lo(FIRST_UNIT[n] + pu - 1 + AHEAD)
                for k in range(OUT_UNITS - 1):
                    split_lo(FIRST_UNIT[n] + pu + k + AHEAD)
            n, v = len(SUBS), N_VEC - 1
            for t in range(NT):
                new_x(n, t)
                dve.wait_ge(G["x_new"], 4 * (n - 1) + 2 * t + 2)
                nc.vector.tensor_copy(rrow[:, 0, 0:1], xres[:, t, 0:1]).then_inc(G["src_ready"], 2)
            dve.wait_ge(G["rms_ready"], n + 1)
            dve.wait_ge(vec_landed[v % 2], 16 * (v // 2 + 1))
            for t in range(NT):
                nc.vector.scalar_tensor_tensor(out=src[:, t, :], in0=xres[:, t, :], scalar=rms[:, t:t + 1],
                                               in1=vec[:, v % 2, :], op0=ALU.mult, op1=ALU.mult).then_inc(
                    G["y_final"], 1)

        @block.tensor
        def _(pe):
            def three(dst, a_hi, a_lo, slot, c, first, last):
                w = slice(c, c + BANK)
                nc.tensor.matmul(dst, a_hi, w_hi[:, slot, w], start=first, stop=False)
                nc.tensor.matmul(dst, a_hi, w_lo[:, slot, w], start=False, stop=False)
                return nc.tensor.matmul(dst, a_lo, w_hi[:, slot, w], start=False, stop=last)

            def turn(s, groups, some):
                for g in some:
                    t, half, bank = groups[g]
                    pe.wait_ge(G["src_ready"], 4 * s + g + 1)
                    for k in range(4):
                        ins = nc.tensor.transpose(ps[:, bank, k * P:(k + 1) * P],
                                                  src[:, t, half * BANK + k * P:half * BANK + (k + 1) * P], ident[:])
                    ins.then_inc(G["turned"], 1)

            def proj_tile(slot, part, t):
                for k in range(4):
                    ins = three(ps[:, 4 + t, :], xt_hi[:, t, 4 * part + k, :], xt_lo[:, t, 4 * part + k, :], slot,
                                k * BANK, part == 0 and k == 0, part == 1 and k == 3)
                return ins

            def proj_unit(u, part, count=None, read_out=None):
                pe.wait_ge(G["w_lo_ready"], u + 1 if count is None else count)
                for t in range(NT):
                    if read_out:
                        pe.wait_ge(read_out[0], read_out[1] + t + 1)
                    ins = proj_tile(u % SPL, part, t)
                    if part == 1 and t == 0:
                        ins.then_inc(G["tile0_done"], 1)
                ins.then_inc(G["unit_used"], 1)

            def first_unit(u, s):
                turn(s, NORM_GROUPS, (0, 1))
                pe.wait_ge(G["w_lo_ready"], u + 1)
                pe.wait_ge(G["xt_lo_ready"], 4 * s + 2)
                proj_tile(u % SPL, 0, 0)
                turn(s, NORM_GROUPS, (2, 3))
                pe.wait_ge(G["xt_lo_ready"], 4 * s + 4)
                proj_tile(u % SPL, 0, 1).then_inc(G["unit_used"], 1)

            def out_unit(u, a_hi, a_lo, first, last, count=None):
                pe.wait_ge(G["w_lo_ready"], u + 1 if count is None else count)
                for t in range(NT):
                    for half in range(2):
                        for k in range(2):
                            ins = three(ps[:, 2 * t + half, :], a_hi(t, k), a_lo(t, k), u % SPL,
                                        k * 2 * BANK + half * BANK, first and k == 0, last and k == 1)
                    if last and t == 0:
                        ins.then_inc(G["acc0_done"], 1)
                ins.then_inc(G["unit_used"], 1)

            def turn_hidden(count):
                pe.wait_ge(G["hid_ready"], count)
                for k in range(2):
                    for t in range(NT):
                        ins = nc.tensor.transpose(ps[:, 6, (2 * k + t) * P:(2 * k + t + 1) * P],
                                                  hid[:, t, k * P:(k + 1) * P], ident[:])
                ins.then_inc(G["ht_turned"], 1)

            def h_hi(t, k):
                return ht_hi[:, k, t, :]

            def h_lo(t, k):
                return ht_lo[:, k, t, :]

            def ffn(n, j):
                u0, h0, s = FIRST_UNIT[n], NCH * j, STAGE[n]
                first_unit(u0, s)
                proj_unit(u0 + 1, 1)
                turn_hidden(2 * h0 + 2)

                def chunk(i, b, first):
                    ua = u0 + 2 + 3 * b
                    proj_unit(ua, 0, count=i * 6 + (ua + 1))
                    proj_unit(ua + 1, 1, count=i * 6 + (ua + 2))
                    pe.wait_ge(G["ht_lo_ready"], i * 2 + (h0 + b + 1))
                    out_unit(ua + 2, h_hi, h_lo, first, False, count=i * 6 + (ua + 3))
                    turn_hidden(i * 4 + 2 * (h0 + b + 2))

                chunk(0, 0, True)
                chunk(0, 1, False)
                with pe.Fori(1, NCH // 2) as i:
                    for b in range(2):
                        chunk(i, b, False)
                pe.wait_ge(G["ht_lo_ready"], h0 + NCH)
                out_unit(u0 + FFN_UNITS - 1, h_hi, h_lo, False, True)

            def gate_products(S, lay, width):
                pe.wait_ge(G["gw_lo_ready"], lay + 1)
                for t in range(NT):
                    dst = ps[:, 6, 16 * t:16 * t + width]
                    for k in range(KT):
                        c = slice(k * width, (k + 1) * width)
                        nc.tensor.matmul(dst, xt_hi[:, t, k, :], gw_hi[:, lay, c], start=(k == 0), stop=False)
                        nc.tensor.matmul(dst, xt_hi[:, t, k, :], gw_lo[:, lay, c], start=False, stop=False)
                        ins = nc.tensor.matmul(dst, xt_lo[:, t, k, :], gw_hi[:, lay, c], start=False,
                                               stop=(k == KT - 1))
                ins.then_inc(S["gate_mm"], 1)

            def turn_nat(S, m, ready, value, banks):
                pe.wait_ge(ready, value)
                for c in range(4):
                    for t in range(NT):
                        q = (c % 2) * SEQ + t * P
                        ins = nc.tensor.transpose(ps[:, banks + c // 2, q:q + P],
                                                  nat[:, m % 2, t, c * P:(c + 1) * P], ident[:])
                ins.then_inc(S["turned"], 1)

            def spread(bank, q, row, heads, h):
                return nc.tensor.matmul(ps[:, bank, q:q + SEQ], ident[0:heads, h:h + 1].to_broadcast([heads, P]),
                                        row, start=True, stop=True)

            def plan_a(n, j):
                S = MS[j]
                slots = {k: [] for k in range(16)}

                def turn_gates():
                    pe.wait_ge(S["gates_ready"], 2)
                    for g in range(2):
                        for t in range(NT):
                            ins = nc.tensor.transpose(ps[0:MH, 7, g * SEQ + t * P:g * SEQ + (t + 1) * P],
                                                      gates[:, t, MH * g:MH * g + MH], ident[:])
                    ins.then_inc(S["gates_turned"], 1)

                def turn_rows():
                    pe.wait_ge(S["en_ready"], 1)
                    for g, r in ((0, 3), (1, 5)):
                        for t in range(NT):
                            ins = nc.tensor.transpose(ps[:, 6, 8 * g + 4 * t:8 * g + 4 * t + 4],
                                                      rowbuf[0:MH, r, t * P:(t + 1) * P], ident[0:MH, 0:MH])
                    ins.then_inc(S["cols_turned"], 1)

                def spread_m():
                    pe.wait_ge(S["cols_ready"], 1)
                    for h in range(MH):
                        ins = spread(6 + h // 2, (h % 2) * SEQ, rowbuf[0:MH, 4, :], MH, h)
                    ins.then_inc(S["mb_done"], 1)

                def turn_qk(m):
                    if m >= 2:
                        pe.wait_ge(S["taps"], 12 * (m - 1))
                    turn_nat(S, m, S["nat_ready"], 2 * (m + 1), 2 * (m % 2))

                def scores(h):
                    if h == 0:
                        pe.wait_ge(S["conv_ready"], 4)
                    for k in range(2):
                        nc.tensor.matmul(ps[:, h, 0:SEQ], qkt[:, 8 + 2 * h + k, 0:P], qkt[:, 2 * h + k, :],
                                         start=(k == 0), stop=(k == 1))
                    for k in range(2):
                        ins = nc.tensor.matmul(ps[:, h, SEQ:SEQ + P], qkt[:, 8 + 2 * h + k, P:SEQ],
                                               qkt[:, 2 * h + k, P:SEQ], start=(k == 0), stop=(k == 1))
                    ins.then_inc(S["s_done"], 1)

                def values(h):
                    pe.wait_ge(S["pm_ready"], MH)
                    pe.wait_ge(S["v_ready"], 4)
                    b = HEAD_BANK[h]
                    nc.tensor.matmul(ps[:, b, 0:MDH + 1], probs[:, h, 0:P], vaug[:, 0, h, :], start=True, stop=True)
                    nc.tensor.matmul(ps[:, b + 1, 0:MDH + 1], probs[:, h, P:SEQ], vaug[:, 0, h, :], start=True,
                                     stop=False)
                    nc.tensor.matmul(ps[:, b + 1, 0:MDH + 1], probs[:, h, SEQ:SEQ + P], vaug[:, 1, h, :],
                                     start=False, stop=True).then_inc(S["pv_done"], 1)

                def last_head():
                    pe.wait_ge(S["og_ready"], 4)
                    values(3)

                slots[0].append(lambda: gate_products(S, 3 * j, 8))
                slots[1].append(turn_gates)
                slots[3].append(turn_rows)
                slots[5].append(spread_m)
                for m in range(4):
                    slots[2 * m + 2].append(lambda m=m: turn_qk(m))
                for h in range(MH):
                    slots[11].append(lambda h=h: scores(h))
                for h in range(3):
                    slots[13].append(lambda h=h: values(h))
                slots[15].append(last_head)
                return slots

            def plan_b(n, j):
                S = FS
                slots = {k: [] for k in range(16)}

                def turn_gates():
                    pe.wait_ge(S["gates_ready"], 2)
                    for t in range(NT):
                        ins = nc.tensor.transpose(ps[0:FH, 7, t * P:(t + 1) * P], gates[:, t, 0:FH], ident[:])
                    ins.then_inc(S["gates_turned"], 1)

                def turn_rows():
                    pe.wait_ge(S["rows"], 2)
                    for t in range(NT):
                        ins = nc.tensor.transpose(ps[:, 7, FH * t:FH * (t + 1)],
                                                  ptbuf[0:FH, 1, t * P:(t + 1) * P], ident[0:FH, 0:FH])
                    ins.then_inc(S["cols_turned"], 1)

                def spread_f(q):
                    if q == 1:
                        pe.wait_ge(S["cols_ready"], 1)
                    if q >= 2:
                        pe.wait_ge(S["fb_copied"], 4 * (q - 1))
                    for h in (2 * q, 2 * q + 1):
                        ins = spread(6 + q % 2, (h % 2) * SEQ, ptbuf[0:FH, 1, 0:SEQ], FH, h)
                    ins.then_inc(S["fb_done"], 1)

                def turn_qk(m):
                    if m >= 2:
                        pe.wait_ge(S["qk_ready"], 2 * (m - 1))
                    turn_nat(S, m, S["natn_ready"], 2 * (m + 1), 2 * (m % 2))

                def scores(h):
                    if h == 0:
                        pe.wait_ge(S["qk_ready"], 8)
                    if h >= 2:
                        pe.wait_ge(S["z_ready"], h - 1)
                    q, k = qkt[:, h, :], qkt[:, FH + h, :]
                    nc.tensor.matmul(ps[:, h % 2, 0:P], q[:, 0:P], k[:, 0:P], start=True, stop=True)
                    nc.tensor.matmul(ps[:, h % 2, P:3 * P], q[:, P:SEQ], k, start=True, stop=True).then_inc(
                        S["s_done"], 1)

                def turn_probs(h):
                    pe.wait_ge(S["p_ready"], 2 * (h + 1))
                    if h >= 2:
                        pe.wait_ge(S["pt_ready"], h - 1)
                    for b in range(3):
                        ins = nc.tensor.transpose(ps[:, 2 + h % 2, b * P:(b + 1) * P],
                                                  zbuf[:, h % 2, b * P:(b + 1) * P], ident[:])
                    ins.then_inc(S["p_turned"], 1)

                def values(h):
                    pe.wait_ge(S["pt_ready"], h + 1)
                    if h == 0:
                        pe.wait_ge(S["v_ready"], 4)
                    if h == 4:
                        pe.wait_ge(S["y_done"], 3 * 2 - 2)
                    if h == 6:
                        pe.wait_ge(G["src_ready"], 4 * (STAGE[n] + 1) + 2)
                    v = [vaug[:, t, :, :].rearrange("p h n -> p (h n)")[:, h * FDH:(h + 1) * FDH] for t in range(NT)]
                    bank, q, pt = 6 + (h // 2) % 2, (h % 2) * SEQ, ptbuf[:, h % 2, :]
                    nc.tensor.matmul(ps[:, bank, q:q + P], pt[:, 0:P], v[0], start=True, stop=True)
                    nc.tensor.matmul(ps[:, bank, q + P:q + SEQ], pt[:, P:SEQ], v[0], start=True, stop=False)
                    nc.tensor.matmul(ps[:, bank, q + P:q + SEQ], pt[:, SEQ:SEQ + P], v[1], start=False,
                                     stop=True).then_inc(S["pv_done"], 1)

                slots[0].append(lambda: gate_products(S, 1, 8))
                slots[1].append(turn_gates)
                slots[4].append(turn_rows)
                for q in range(4):
                    slots[4 + q].append(lambda q=q: spread_f(q))
                for m in range(4):
                    slots[2 * m + 3].append(lambda m=m: turn_qk(m))
                for k in range(6):
                    for step, pair in ((values, k - 2), (turn_probs, k - 1), (scores, k)):
                        if 0 <= pair < 4:
                            slots[10 + k] += [lambda f=step, h=2 * pair: f(h), lambda f=step, h=2 * pair + 1: f(h)]
                return slots

            def plan_c(n, j):
                S = LS
                slots = {k: [] for k in range(12)}

                def turn_gates():
                    pe.wait_ge(S["glr_ready"], 2)
                    for t in range(NT):
                        ins = nc.tensor.transpose(ps[0:GRANK, 7, t * P:(t + 1) * P], gates[:, t, :], ident[:])
                    ins.then_inc(S["glr_turned"], 1)

                def gate_up():
                    pe.wait_ge(S["glrt_ready"], 1)
                    for h in range(GH):
                        ins = nc.tensor.matmul(ps[:, 6 + h // 2, (h % 2) * SEQ:(h % 2 + 1) * SEQ],
                                               glaup[:, h * GDK:(h + 1) * GDK], glrt, start=True, stop=True)
                    ins.then_inc(S["z_done"], 1)

                def level(lv):
                    if lv == 0:
                        pe.wait_ge(S["qk_ready"], 4)
                        q, k = qkflat[:, 0:1024], qkflat[:, 1024:2048]
                    else:
                        pe.wait_ge(S["qs_ready"], lv)
                        pe.wait_ge(S["ks_ready"], lv)
                        q, k = qs[lv % 2], ks[lv % 2]
                    if lv >= 2:
                        pe.wait_ge(S["a_ready"], lv - 1)
                    for h in range(GH):
                        base = h * SEQ
                        if lv == GLA_LEVELS - 1:
                            ins = nc.tensor.matmul(ps[:, 0, h * P:(h + 1) * P], k[:, base:base + P],
                                                   q[:, base + P:base + SEQ], start=True, stop=True)
                            continue
                        for t in range(NT):
                            m, c = 2 * h + t, slice(base + t * P, base + (t + 1) * P)
                            ins = nc.tensor.matmul(ps[:, 2 * (lv % 2) + m // 4, (m % 4) * P:(m % 4 + 1) * P],
                                                   k[:, c], q[:, c], start=True, stop=True)
                    ins.then_inc(S["lvl_done"], 1)

                def values(h):
                    b = HEAD_BANK[h]
                    if h == 0:
                        pe.wait_ge(S["v_ready"], 4)
                        pe.wait_ge(S["a_ready"], GLA_LEVELS - 1)
                        pe.wait_ge(S["ax_ready"], 1)
                    if h == 3:
                        pe.wait_ge(S["og_ready"], 4)
                    nc.tensor.matmul(ps[:, b, 0:GDV], amat[:, 2 * h, :], vaug[:, 0, h, 0:GDV], start=True, stop=True)
                    nc.tensor.matmul(ps[:, b + 1, 0:GDV], across[:, h, :], vaug[:, 0, h, 0:GDV], start=True,
                                     stop=False)
                    nc.tensor.matmul(ps[:, b + 1, 0:GDV], amat[:, 2 * h + 1, :], vaug[:, 1, h, 0:GDV], start=False,
                                     stop=True).then_inc(S["pv_done"], 1)

                slots[0].append(lambda: gate_products(S, 2, GRANK))
                slots[1].append(turn_gates)
                slots[2].append(gate_up)
                for m in range(2):
                    slots[2 * m + 2].append(lambda m=m: turn_nat(S, m, S["nat_ready"], 2 * (m + 1), 2 * m))
                for lv in range(GLA_LEVELS):
                    slots[GLA_PE[lv]].append(lambda lv=lv: level(lv))
                for h in range(GH):
                    slots[11].append(lambda h=h: values(h))
                return slots

            def mixer(n, kind, j):
                u0, s, pu = FIRST_UNIT[n], STAGE[n], PROJ_UNITS[kind]
                slots = {"A": plan_a, "B": plan_b, "C": plan_c}[kind](n, j)
                first_unit(u0, s)
                S = {"A": MS[j], "B": FS, "C": LS}[kind]
                qk = {"A": 4, "B": 4, "C": 2}[kind]
                copies = [(S["nat_ready"], 2 * m) for m in range(qk)] + \
                         [(S["v_ready"], 2 * m) for m in range(2)] + [(S["og_ready"], 2 * m) for m in range(2)]
                for k in range(pu):
                    if k:
                        proj_unit(u0 + k, k % 2, read_out=None if k % 2 else copies[k // 2 - 1])
                    for step in slots[k]:
                        step()
                turn(s + 1, MIX_GROUPS[kind], range(4))
                pe.wait_ge(G["xt_lo_ready"], 4 * (s + 1) + 4)
                for k in range(OUT_UNITS):
                    out_unit(u0 + pu + k, lambda t, q: xt_hi[:, t, 2 * k + q, :],
                             lambda t, q: xt_lo[:, t, 2 * k + q, :], k == 0, k == OUT_UNITS - 1)

            pe.wait_ge(G["const"], 16 * 8)
            for n, (kind, j) in enumerate(SUBS):
                if kind == "F":
                    ffn(n, j)
                else:
                    mixer(n, kind, j)


def kernel(**inputs):
    import numpy as np
    import concourse.bacc as bacc
    from concourse.bass_utils import run_bass_kernel_spmd as run

    a = {k: np.asarray(v) for k, v in inputs.items()}

    def in_units(w, cols):
        w = w.reshape(2, 4, P, cols // BANK, BANK).transpose(3, 0, 2, 1, 4)
        return w.reshape(-1, P, UNIT)

    def out_units(w):
        return w.reshape(-1, 2, P, D).transpose(0, 2, 1, 3).reshape(-1, P, UNIT)

    stream = np.empty((N_UNITS, P, UNIT), np.float32)
    gate = np.zeros((DEPTH, P, P), np.float32)
    vecs = np.empty((N_VEC, D), np.float32)
    gb = np.zeros((DEPTH, 8), np.float32)
    for n, (kind, j) in enumerate(SUBS):
        u, layer = FIRST_UNIT[n], n // 3
        vecs[VEC[n]] = a["norm_w"][layer, n % 3]
        if kind == "F":
            w1 = a["ffn_w_in"][j // 2, j % 2].reshape(D, 2, NCH, HC).transpose(0, 2, 1, 3).reshape(D, 2 * F)
            w1 = in_units(w1, 2 * F)
            w2 = out_units(a["ffn_w_out"][j // 2, j % 2])
            stream[u:u + 2] = w1[0:2]
            body = stream[u + 2:u + FFN_UNITS - 1].reshape(NCH - 1, 3, P, UNIT)
            body[:, 0:2] = w1[2:].reshape(NCH - 1, 2, P, UNIT)
            body[:, 2] = w2[0:NCH - 1]
            stream[u + FFN_UNITS - 1] = w2[NCH - 1]
            continue
        name = {"A": "mlstm", "B": "fox", "C": "gla"}[kind]
        w, pu, width = a[name + "_w_in"][j], PROJ_UNITS[kind], GCOLS[kind]
        main = w.shape[1] - width
        stream[u:u + pu] = in_units(w[:, 0:main], main)
        stream[u + pu:u + pu + OUT_UNITS] = out_units(a[name + "_w_out"][j])
        gate[layer, :, 0:KT * width] = w[:, main:].reshape(KT, P, width).transpose(1, 0, 2).reshape(P, KT * width)
        if kind == "A":
            gb[layer] = a["mlstm_b_gate"][j]
            vecs[VEC[n] + 1] = a["mlstm_norm_w"][j]
        if kind == "B":
            gb[layer] = a["fox_b_f"][j]
        if kind == "C":
            vecs[VEC[n] + 1] = a["gla_norm_w"][j]
    vecs[N_VEC - 1] = a["final_norm_w"]

    masks = np.zeros((P, 8, P), np.float32)
    for q in range(P):
        masks[q, 0, q] = 1
        for lv in range(1, 8):
            size = 1 << (lv - 1)
            if q // size % 2 == 0:
                t0 = (q // size + 1) * size
                masks[q, lv, t0:t0 + size] = 1

    arrays = {
        "stream": stream,
        "x": a["x"],
        "vecs": vecs,
        "gate_w": gate.transpose(1, 0, 2),
        "mg_bias": np.broadcast_to(gb[None], (P, DEPTH, 8)),
        "conv_w": a["mlstm_conv_w"].reshape(2, 4, 16, P).transpose(3, 0, 2, 1),
        "fox_b": a["fox_b_f"],
        "fox_qk": a["fox_qk_norm"][0].transpose(1, 0),
        "gla_up": a["gla_w_gate_up"][0],
        "gla_b": a["gla_b_gate"][0].reshape(GH, GDK).transpose(1, 0),
        "masks": masks,
        "ident": np.eye(P, dtype=np.float32),
    }
    nc = bacc.Bacc("TRN2", target_bir_lowering=False, num_devices=1)
    aps = []
    for name in arrays:
        arrays[name] = np.ascontiguousarray(arrays[name])
        aps.append(nc.dram_tensor("in_" + name, arrays[name].shape, mybir.dt.from_np(arrays[name].dtype),
                                  kind="ExternalInput").ap())
    out = nc.dram_tensor("out_y", (1, SEQ, D), F32, kind="ExternalOutput").ap()
    build(nc, *aps, out)
    r = run(nc, [{"in_" + k: v for k, v in arrays.items()}], core_ids=[0])
    return r.results[0]["out_y"]
```

```python
from contextlib import ExitStack

import concourse.bass as bass
from concourse import mybir

F32 = mybir.dt.float32
F32R = mybir.dt.float32r
U8 = mybir.dt.uint8
ALU = mybir.AluOpType
ACT = mybir.ActivationFunctionType
AX = mybir.AxisListType

P = 128
SEQ = 256
D = 1024
F = 2816
DEPTH = 4
EPS = 1e-6
NT = SEQ // P
KT = D // P
UNIT = 2048
BANK = 512
HC = 256
NCH = F // HC
FFN_UNITS = 3 * NCH
RAW = 6
SPL = 3
AHEAD = SPL
OUT_UNITS = 4

MH, MDH = 4, 256
FH, FDH = 8, 128
GH, GDK, GDV, GRANK, GTAU = 4, 128, 256, 16, 16.0
GCOLS = {"A": 2 * MH, "B": FH, "C": GRANK}
PROJ_UNITS = {"A": 16, "B": 16, "C": 12}
NEG = -1e30

KINDS = "ABC"
SUBS = []
for _layer in range(DEPTH):
    SUBS += [("F", 2 * _layer), (KINDS[_layer % 3], _layer // 3), ("F", 2 * _layer + 1)]

FIRST_UNIT, FIRST_CHUNK, STAGE, OUT_NO, VEC = [], [], [], [], []
_u = _c = _s = _o = _v = 0
for _kind, _ in SUBS:
    FIRST_UNIT.append(_u)
    FIRST_CHUNK.append(_c)
    STAGE.append(_s)
    OUT_NO.append(_o)
    VEC.append(_v)
    _u += FFN_UNITS if _kind == "F" else PROJ_UNITS[_kind] + OUT_UNITS
    _c += NCH if _kind == "F" else PROJ_UNITS[_kind] // 2
    _s += 1 if _kind == "F" else 2
    _o += 1
    _v += 2 if _kind in "AC" else 1
N_UNITS, N_OUT, N_STAGE, N_VEC = _u, _o, _s, _v + 1

NORM_GROUPS = [(0, 0, 6), (0, 1, 7), (1, 0, 0), (1, 1, 1)]
MIX_GROUPS = {"A": [(0, 0, 6), (1, 0, 7), (0, 1, 6), (1, 1, 7)],
              "B": [(0, 0, 0), (1, 0, 1), (0, 1, 4), (1, 1, 5)],
              "C": [(0, 0, 6), (1, 0, 7), (0, 1, 6), (1, 1, 7)]}
HEAD_BANK = [6, 0, 2, 4]

GLA_PE = {0: 6, 1: 6, 2: 7, 3: 7, 4: 8, 5: 9, 6: 10, 7: 10, 8: 11}
GLA_LEVELS = 9


def build(nc, stream, x, vecs, gate_w, mg_bias, conv_w, fox_b, fox_qk, gla_up, gla_b, masks, ident_in, out):
    with ExitStack() as ctx:
        def sb(name, shape, dt=F32):
            return ctx.enter_context(nc.sbuf_tensor(name, shape, dt))

        def sems(prefix, names):
            return {n: ctx.enter_context(nc.semaphore(prefix + n)) for n in names.split()}

        raw = sb("raw", [P, RAW, UNIT])
        w_hi = sb("w_hi", [P, SPL, UNIT], F32R)
        w_lo = sb("w_lo", [P, SPL, UNIT], F32R)
        xres = sb("xres", [P, NT, D])
        src = sb("src", [P, NT, D])
        xt_hi = sb("xt_hi", [P, NT, KT, P], F32R)
        xt_lo = sb("xt_lo", [P, NT, KT, P], F32R)
        vec = sb("vec", [P, 2, D])
        nat = sb("nat", [P, 2, NT, BANK])
        silu_g = nat[:, 0, :, 0:HC]
        hid = nat[:, 1, :, 0:HC]
        og = nat[:, :, :, :].rearrange("p a t n -> p (a t n)").rearrange("p (t n) -> p t n", t=NT)
        ht_hi = sb("ht_hi", [P, 2, NT, P], F32R)
        ht_lo = sb("ht_lo", [P, 2, NT, P], F32R)
        qkt = sb("qkt", [P, 16, SEQ])
        vaug = sb("vaug", [P, NT, MH, MDH + 1])
        scr = sb("scr", [P, 18, SEQ])
        ident = sb("ident", [P, P])
        ones = sb("ones", [P, SEQ])
        lvl_mask = sb("lvl_mask", [P, 8, P], U8)
        gw_hi = sb("gw_hi", [P, DEPTH, P], F32R)
        gw_lo = sb("gw_lo", [P, DEPTH, P], F32R)
        gw_raw = scr[:, 0:2, :].rearrange("p a n -> p (a n)").rearrange("p (l n) -> p l n", l=DEPTH)
        mask_raw = scr[:, 4:8, :].rearrange("p a n -> p (a n)").rearrange("p (l n) -> p l n", l=8)
        gbias = sb("gbias", [P, DEPTH, 8])
        convw = sb("convw", [P, 2, 16, 4])
        qkw = sb("qkw", [P, 2])
        glaup = sb("glaup", [GRANK, GH * GDK])
        glab = sb("glab", [P, GH])
        ssum = sb("ssum", [P, NT])
        msum = sb("msum", [P, NT])
        rms = sb("rms", [P, NT])
        nhalf = sb("nhalf", [P, 8])
        gates = sb("gates", [P, NT, 16])
        cols = sb("cols", [P, 2, 2 * 8])
        rden = sb("rden", [P, 2, 8])
        hss = sb("hss", [P, 32])
        hms = sb("hms", [P, 32])
        hrs = sb("hrs", [P, 32])
        hrr = sb("hrr", [P, 8])
        rowmax = sb("rowmax", [P, 2, FH])
        rowsum = sb("rowsum", [P, 2, FH])
        rrow = sb("rrow", [P, 2, FH])
        ps = ctx.enter_context(nc.psum_tensor("ps", [P, 8, BANK], F32))

        landed = [ctx.enter_context(nc.semaphore(f"landed{j}")) for j in range(RAW)]
        vec_landed = [ctx.enter_context(nc.semaphore(f"vec_landed{j}")) for j in range(2)]
        G = sems("", "const ident_in x_in out_sent w_hi_ready w_lo_ready unit_used tile0_done acc_done src_ready turned "
                     "xt_hi_ready xt_lo_ready x_new sq_ready ms_ready rms_ready silu_ready hid_ready ht_turned "
                     "ht_hi_ready ht_lo_ready gw_hi_ready gw_lo_ready init y_final masks_ready pool_chain")
        MS = [sems(f"m{j}_", "nat_ready turned tap0 taps conv_ready gate_mm gates_ready gates_turned soft rows "
                             "en_ready cols_turned cols_ready mb_done dec_arg dec_exp dec_ready s_done pm_ready "
                             "v_ready pv_done rd_ready ss_ready rs_ready og_ready ogw_ready y_done") for j in range(2)]
        FS = sems("f_", "nat_ready sq red ss_scaled rn_ready natn_ready turned qk_ready gate_mm gates_ready "
                        "gates_turned soft rows cols_turned cols_ready fb_done fb_copied fb_ready s_done z_ready "
                        "max_ready p_ready sum_inv p_turned pt_ready pv_done v_ready og_ready y_done")
        LS = sems("g_", "nat_ready turned qk_ready gate_mm glr_ready glr_turned glrt_ready z_done z_ready soft "
                        "rows diff_ready e_ready qs_ready ks_ready lvl_done a_ready ax_ready v_ready pv_done "
                        "ss_ready rs_ready og_ready ogw_ready y_done")
        block = ctx.enter_context(nc.Block())

        flat = scr[:, :, :].rearrange("p a n -> p (a n)")
        decay = flat[:, 0:1536].rearrange("p (h n) -> p h n", h=MH)
        probs = flat[:, 1536:3072].rearrange("p (h n) -> p h n", h=MH)
        rowbuf = flat[:, 3072:4608].rearrange("p (r n) -> p r n", n=SEQ)
        fbias = flat[:, 0:3072].rearrange("p (h n) -> p h n", h=FH)
        zbuf = flat[:, 3072:3840].rearrange("p (b n) -> p b n", b=2)
        ptbuf = flat[:, 3840:4608].rearrange("p (b n) -> p b n", b=2)
        gcum = flat[:, 0:1024]
        ebuf = flat[:, 1024:3072].rearrange("p (b n) -> p b n", b=2)
        amat = flat[:, 3072:4096].rearrange("p (m n) -> p m n", m=8)
        across = flat[:, 4096:4608].rearrange("p (h n) -> p h n", h=GH)
        squares = flat[:, 0:1536].rearrange("p (k n) -> p k n", n=MDH)
        glrt = flat[0:GRANK, 4096:4352]
        qkflat = qkt[:, :, :].rearrange("p a n -> p (a n)")
        srcflat = src[:, :, :].rearrange("p t n -> p (t n)")
        qs = [qkflat[:, 2048:3072], srcflat[:, 0:1024]]
        ks = [qkflat[:, 3072:4096], srcflat[:, 1024:2048]]

        def landed_at(u):
            return 16 * (u // RAW + 1)

        LOOPED = NCH // 2 - 1
        HT = NCH + 1

        def halves(ap, size):
            return ap.rearrange("p (b two s) -> p b two s", two=2, s=size)

        @block.sync
        def _(sp):
            for t in range(NT):
                sp.dma_start(xres[:, t, :], x[0, t * P:(t + 1) * P, :]).then_inc(G["x_in"], 16)
            for u in range(RAW):
                sp.dma_start(raw[:, u, :], stream[u]).then_inc(landed[u], 16)
            with sp.Fori(1, N_UNITS // RAW) as i:
                for j in range(RAW):
                    sp.wait_ge(G["w_lo_ready"], i * RAW + (j + 1 - RAW))
                    sp.dma_start(raw[:, j, :], stream[i * RAW + j]).then_inc(landed[j], 16)
            for u in range(N_UNITS // RAW * RAW, N_UNITS):
                sp.wait_ge(G["w_lo_ready"], u + 1 - RAW)
                sp.dma_start(raw[:, u % RAW, :], stream[u]).then_inc(landed[u % RAW], 16)
            for t in range(NT):
                sp.wait_ge(G["y_final"], t + 1)
                sp.dma_start(out[0, t * P:(t + 1) * P, :], src[:, t, :]).then_inc(G["out_sent"], 16)
            sp.wait_ge(G["out_sent"], 16 * NT)

        @block.gpsimd
        def _(pool):
            consts = [(mask_raw, masks), (gbias[:], mg_bias), (convw[:], conv_w),
                      (qkw[:], fox_qk), (glaup[:], gla_up), (glab[:], gla_b)]

            def load_vec(v):
                pool.dma_start(vec[:, v % 2, :], vecs[v:v + 1, :].to_broadcast([P, D])).then_inc(
                    vec_landed[v % 2], 16)

            load_vec(0)
            pool.dma_start(gw_raw, gate_w).then_inc(G["const"], 16)
            load_vec(1)
            for dst, a in consts:
                pool.dma_start(dst, a).then_inc(G["const"], 16)
            nc.gpsimd.memset(nhalf[:], -0.5).then_inc(G["init"], 1)
            nc.gpsimd.memset(ones[:], 1.0).then_inc(G["init"], 1)
            nc.gpsimd.memset(vaug[:, :, :, MDH:MDH + 1], 1.0).then_inc(G["init"], 1)
            nc.gpsimd.memset(hss[:], 1.0).then_inc(G["init"], 1)
            pool.wait_ge(G["init"], 4)
            links = [0]

            def link(ins):
                links[0] += 1
                ins.then_inc(G["pool_chain"], 1)
                pool.wait_ge(G["pool_chain"], links[0])

            def input_rms(k):
                pool.wait_ge(G["sq_ready"], NT * (k + 1))
                nc.gpsimd.tensor_scalar(msum[:], ssum[:], 1.0 / D, EPS, ALU.mult, ALU.add).then_inc(G["ms_ready"], 1)
                pool.wait_ge(G["ms_ready"], k + 1)
                nc.gpsimd.tensor_tensor(rms[:], msum[:], nhalf[:, 0:NT], ALU.pow).then_inc(G["rms_ready"], 1)

            def weigh_gate(S, v, half):
                if half == 0:
                    pool.wait_ge(vec_landed[v % 2], 16 * (v // 2 + 1))
                for t in range(NT):
                    pool.wait_ge(S["og_ready"], NT * half + t + 1)
                    part = og[:, t, half * BANK:(half + 1) * BANK]
                    nc.gpsimd.tensor_tensor(part, part, vec[:, v % 2, half * BANK:(half + 1) * BANK],
                                            ALU.mult).then_inc(S["ogw_ready"], 1)

            def head_rms(S, h, den):
                pool.wait_ge(S["ss_ready"], 2 * (h + 1))
                c = slice(2 * h, 2 * h + 2)
                link(nc.gpsimd.tensor_scalar(hms[:, c], hss[:, c], 1.0 / MDH, EPS, ALU.mult, ALU.add))
                if not den:
                    nc.gpsimd.tensor_tensor(hrr[:, c], hms[:, c], nhalf[:, 0:2], ALU.pow).then_inc(S["rs_ready"], 1)
                    return
                link(nc.gpsimd.tensor_tensor(hrs[:, c], hms[:, c], nhalf[:, 0:2], ALU.pow))
                nc.gpsimd.tensor_tensor(hrr[:, c], hrs[:, c], rden[:, 1, c], ALU.mult).then_inc(S["rs_ready"], 1)

            norm_no = 0
            for n, (kind, j) in enumerate(SUBS):
                input_rms(norm_no)
                norm_no += 1
                if VEC[n] + 2 < N_VEC:
                    pool.wait_ge(G["src_ready"], 4 * STAGE[n] + 4)
                    load_vec(VEC[n] + 2)
                if kind == "A":
                    S = MS[j]
                    pool.wait_ge(S["dec_exp"], 1)
                    for part in (decay[:, :, 0:P], decay[:, :, 2 * P:3 * P]):
                        nc.gpsimd.affine_select(out=part, in_=part, compare_op=ALU.is_ge, fill=0.0, base=0,
                                                pattern=[[0, MH], [1, P]], channel_multiplier=-1).then_inc(
                            S["dec_ready"], 1)
                    weigh_gate(S, VEC[n] + 1, 0)
                    for h in range(3):
                        head_rms(S, h, True)
                    weigh_gate(S, VEC[n] + 1, 1)
                    pool.wait_ge(S["ogw_ready"], 4)
                    if VEC[n] + 3 < N_VEC:
                        load_vec(VEC[n] + 3)
                    head_rms(S, 3, True)
                if kind == "B":
                    for m in range(4):
                        pool.wait_ge(FS["red"], 2 * (m + 1))
                        c = slice(8 * m, 8 * m + 8)
                        nc.gpsimd.tensor_scalar(hms[:, c], hss[:, c], 1.0 / FDH, EPS, ALU.mult, ALU.add).then_inc(
                            FS["ss_scaled"], 1)
                        pool.wait_ge(FS["ss_scaled"], m + 1)
                        nc.gpsimd.tensor_tensor(hrs[:, c], hms[:, c], nhalf[:, 0:8], ALU.pow).then_inc(
                            FS["rn_ready"], 1)
                    pool.wait_ge(FS["fb_copied"], 2 * FH)
                    for part, base in ((fbias[:, :, 0:P], 0), (fbias[:, :, 2 * P:3 * P], 0)):
                        nc.gpsimd.affine_select(out=part, in_=part, compare_op=ALU.is_ge, fill=NEG, base=base,
                                                pattern=[[0, FH], [-1, P]], channel_multiplier=1).then_inc(
                            FS["fb_ready"], 1)
                if kind == "C":
                    S = LS
                    pool.wait_ge(G["turned"], 4 * STAGE[n] + 4)
                    link(nc.gpsimd.memset(qs[0], 0.0))
                    link(nc.gpsimd.memset(ks[0], 0.0))
                    link(nc.gpsimd.memset(srcflat[:, :], 0.0))
                    link(nc.gpsimd.memset(amat[:, :, :], 0.0))
                    for lv in range(1, GLA_LEVELS):
                        size = 1 << (lv - 1)
                        if lv == 1:
                            pool.wait_ge(S["qk_ready"], 4)
                        pool.wait_ge(S["e_ready"], lv)
                        if lv >= 3:
                            pool.wait_ge(S["lvl_done"], lv - 1)
                        nc.gpsimd.tensor_tensor(halves(ks[lv % 2], size)[:, :, 0, :],
                                                halves(qkflat[:, 1024:2048], size)[:, :, 0, :],
                                                halves(ebuf[:, lv % 2, :], size)[:, :, 0, :],
                                                ALU.mult).then_inc(S["ks_ready"], 1)
                    for half in range(2):
                        weigh_gate(S, VEC[n] + 1, half)
                    pool.wait_ge(S["ogw_ready"], 4)
                    if VEC[n] + 3 < N_VEC:
                        load_vec(VEC[n] + 3)
                    for h in range(GH):
                        head_rms(S, h, False)
            for t in range(NT):
                pool.wait_ge(G["sq_ready"], NT * norm_no + t + 1)
                c = slice(t, t + 1)
                nc.gpsimd.tensor_scalar(msum[:, c], ssum[:, c], 1.0 / D, EPS, ALU.mult, ALU.add).then_inc(
                    G["ms_ready"], 1)
                pool.wait_ge(G["ms_ready"], norm_no + t + 1)
                nc.gpsimd.tensor_tensor(rms[:, c], msum[:, c], nhalf[:, c], ALU.pow).then_inc(G["rms_ready"], 1)

        @block.scalar
        def _(act):
            def split_hi(u, at=None, used=None):
                if u >= N_UNITS:
                    return
                act.wait_ge(landed[u % RAW], landed_at(u) if at is None else at)
                if u >= SPL:
                    act.wait_ge(G["unit_used"], u - SPL + 1 if used is None else used)
                nc.scalar.activation(w_hi[:, u % SPL, :], raw[:, u % RAW, :], ACT.Copy).then_inc(G["w_hi_ready"], 1)

            def stage_hi(s, groups, some):
                for g in some:
                    t, half, bank = groups[g]
                    act.wait_ge(G["turned"], 4 * s + g + 1)
                    nc.scalar.activation(xt_hi[:, t, 4 * half:4 * half + 4, :],
                                         ps[:, bank, :].rearrange("p (k n) -> p k n", k=4),
                                         ACT.Copy).then_inc(G["xt_hi_ready"], 1)

            def square_rows(s, t):
                act.wait_ge(G["src_ready"], 4 * s + 2 * t + 2)
                nc.scalar.activation(nat[:, t, :, :].rearrange("p t n -> p (t n)"), xres[:, t, :], ACT.Square,
                                     accum_out=ssum[:, t:t + 1]).then_inc(G["sq_ready"], 1)

            def wait_tile(t, chunk, unit):
                if t == 0:
                    act.wait_ge(G["tile0_done"], chunk + 1)
                else:
                    act.wait_ge(G["unit_used"], unit + 1)

            def ffn_chunk(chunk, ua, first):
                for t in range(NT):
                    wait_tile(t, chunk, ua + 1)
                    if first:
                        act.wait_ge(G["rms_ready"], first)
                    nc.scalar.activation(silu_g[:, t, :], ps[:, 4 + t, 0:HC], ACT.Silu,
                                         scale=rms[:, t:t + 1]).then_inc(G["silu_ready"], 1)

            def hidden_hi(count):
                act.wait_ge(G["ht_turned"], count)
                nc.scalar.activation(ht_hi[:, :, :, :], ps[:, 6, :].rearrange("p (k t n) -> p k t n", k=2, t=NT),
                                     ACT.Copy).then_inc(G["ht_hi_ready"], 1)

            def ffn(n, j, norm_no):
                u0, c0, h0 = FIRST_UNIT[n], FIRST_CHUNK[n], HT * j
                ffn_chunk(c0, u0, norm_no + 1)
                split_hi(u0 + 3)
                split_hi(u0 + 4)

                def body(i):
                    for b in range(2):
                        ua = u0 + 2 + 3 * b
                        hidden_hi(i * 2 + (h0 + b + 1))
                        for q in range(3):
                            if q == 1:
                                ffn_chunk(i * 2 + (c0 + 1 + b), i * 6 + ua, 0)
                            v = ua + AHEAD + q
                            if not isinstance(i, int):
                                split_hi(v, at=i * 16 + landed_at(v), used=i * 6 + (v - SPL + 1))
                            elif not (b and q == 2):
                                split_hi(6 * i + v)

                with act.Fori(0, LOOPED) as i:
                    body(i)
                body(LOOPED)
                for t in range(NT):
                    act.wait_ge(G["ht_turned"], h0 + NCH + t)
                    if t:
                        act.wait_ge(G["unit_used"], u0 + FFN_UNITS - 1)
                    nc.scalar.activation(ht_hi[:, :, t, :], ps[:, 6 + t, 0:2 * P].rearrange("p (k n) -> p k n", k=2),
                                         ACT.Copy).then_inc(G["ht_hi_ready"], 1)

            def head_square(S, h, den):
                act.wait_ge(S["pv_done"], h + 1)
                if den:
                    act.wait_ge(S["rd_ready"], 3 * (h + 1))
                for t in range(NT):
                    k = 2 * h + t
                    q = k % 6
                    if k >= 6:
                        act.wait_ge(S["ss_ready"], k - 5)
                    nc.scalar.activation(squares[:, q, :], ps[:, HEAD_BANK[h] + t, 0:MDH],
                                         ACT.Square, scale=rden[:, 1, k:k + 1] if den else 1.0,
                                         accum_out=hss[:, k:k + 1]).then_inc(S["ss_ready"], 1)

            def log_sigmoid_part(S, gate_ap, tmp, ready, value):
                act.wait_ge(ready, value)
                nc.scalar.activation(tmp, gate_ap, ACT.Abs).then_inc(S["soft"], 1)
                act.wait_ge(S["soft"], 1)
                nc.scalar.activation(tmp, tmp, ACT.Exp, scale=-1.0).then_inc(S["soft"], 1)
                act.wait_ge(S["soft"], 2)
                nc.scalar.activation(tmp, tmp, ACT.Ln, bias=1.0).then_inc(S["soft"], 1)

            def v_piece(t, m, kind):
                if kind == "B":
                    return vaug[:, t, :, :].rearrange("p h n -> p (h n)")[:, m * BANK:(m + 1) * BANK]
                return vaug[:, t, 2 * m:2 * m + 2, 0:MDH]

            def gate_half(t, m):
                return og[:, t, m * BANK:(m + 1) * BANK]

            def plan_a(n, j):
                S, c0, u0, s = MS[j], FIRST_CHUNK[n], FIRST_UNIT[n], STAGE[n]
                slots = {k: [] for k in range(16)}

                def evac(m):
                    for t in range(NT):
                        evac_tile(m, t)

                def evac_tile(m, t):
                    if True:
                        wait_tile(t, c0 + m, u0 + 2 * m + 1)
                        bank = ps[:, 4 + t, :]
                        r = rms[:, t:t + 1]
                        if m < 4:
                            nc.scalar.activation(nat[:, m % 2, t, :], bank, ACT.Copy, scale=r).then_inc(
                                S["nat_ready"], 1)
                        elif m < 6:
                            nc.scalar.activation(v_piece(t, m - 4, "A"), bank.rearrange("p (h n) -> p h n", h=2),
                                                 ACT.Copy, scale=r).then_inc(S["v_ready"], 1)
                        else:
                            if m == 6 and t == 0:
                                act.wait_ge(S["turned"], 4)
                            nc.scalar.activation(gate_half(t, m - 6), bank, ACT.Sigmoid, scale=r).then_inc(
                                S["og_ready"], 1)

                def first_tap(m):
                    act.wait_ge(S["turned"], m + 1)
                    for c in range(4):
                        ct = 4 * m + c
                        nc.scalar.activation(qkt[:, ct, :], ps[:, 2 * (m % 2) + c // 2, (c % 2) * SEQ:(c % 2 + 1) * SEQ],
                                             ACT.Copy, scale=convw[:, j, ct, 3:4]).then_inc(S["tap0"], 1)

                def conv_silu(m):
                    act.wait_ge(S["taps"], 12 * (m + 1))
                    part = qkt[:, 4 * m:4 * m + 4, :]
                    nc.scalar.activation(part, part, ACT.Silu).then_inc(S["conv_ready"], 1)

                def soft():
                    log_sigmoid_part(S, ps[0:MH, 7, SEQ:2 * SEQ], rowbuf[0:MH, 0, :], S["gates_turned"], 1)

                def en():
                    act.wait_ge(S["rows"], 5)
                    nc.scalar.activation(rowbuf[0:MH, 5, :], rowbuf[0:MH, 5, :], ACT.Exp, scale=-1.0).then_inc(
                        S["en_ready"], 1)

                def cols_copy():
                    act.wait_ge(S["cols_turned"], 1)
                    nc.scalar.activation(cols[:, :, 0:8], ps[:, 6, 0:16].rearrange("p (a n) -> p a n", a=2),
                                         ACT.Copy).then_inc(S["cols_ready"], 1)

                def dec_exp():
                    act.wait_ge(S["dec_arg"], 8)
                    nc.scalar.activation(decay[:, :, :], decay[:, :, :], ACT.Exp, scale=-1.0).then_inc(S["dec_exp"], 1)

                for m in range(7):
                    slots[2 * m + 1].append(lambda m=m: evac(m))
                for m in range(4):
                    slots[2 * m + 2].append(lambda m=m: first_tap(m))
                    slots[2 * m + 3].append(lambda m=m: conv_silu(m))
                slots[1].append(soft)
                slots[2].append(en)
                slots[3].append(cols_copy)
                slots[6].append(dec_exp)
                for k in (2, 4, 6, 8):
                    slots[k].insert(0, None)
                for h in range(3):
                    slots[13].append(lambda h=h: head_square(S, h, True))
                slots[15] = [lambda: evac_tile(7, 0), lambda: stage_hi(s + 1, MIX_GROUPS["A"], (0, 1)),
                             lambda: evac_tile(7, 1), None, lambda: head_square(S, 3, True),
                             lambda: stage_hi(s + 1, MIX_GROUPS["A"], (2, 3))]
                return slots

            def plan_b(n, j):
                S, c0, u0, s = FS, FIRST_CHUNK[n], FIRST_UNIT[n], STAGE[n]
                slots = {k: [] for k in range(16)}

                def evac(m):
                    for t in range(NT):
                        evac_tile(m, t)

                def evac_tile(m, t):
                    if True:
                        wait_tile(t, c0 + m, u0 + 2 * m + 1)
                        bank = ps[:, 4 + t, :]
                        r = rms[:, t:t + 1]
                        if m < 4:
                            nc.scalar.activation(nat[:, m % 2, t, :], bank, ACT.Copy, scale=r).then_inc(
                                S["nat_ready"], 1)
                        elif m < 6:
                            nc.scalar.activation(v_piece(t, m - 4, "B"), bank, ACT.Copy, scale=r).then_inc(
                                S["v_ready"], 1)
                        else:
                            if m == 6 and t == 0:
                                act.wait_ge(S["turned"], 4)
                            nc.scalar.activation(gate_half(t, m - 6), bank, ACT.Sigmoid, scale=r).then_inc(
                                S["og_ready"], 1)

                def qk_evac(m):
                    act.wait_ge(S["turned"], m + 1)
                    for b in range(2):
                        nc.scalar.activation(qkt[:, 4 * m + 2 * b:4 * m + 2 * b + 2, :],
                                             ps[:, 2 * (m % 2) + b, :].rearrange("p (h n) -> p h n", h=2),
                                             ACT.Copy, scale=qkw[:, m // 2:m // 2 + 1]).then_inc(S["qk_ready"], 1)

                def soft():
                    log_sigmoid_part(S, ps[0:FH, 7, 0:SEQ], zbuf[0:FH, 0, 0:SEQ], S["gates_turned"], 1)

                def cols_copy():
                    act.wait_ge(S["cols_turned"], 1)
                    nc.scalar.activation(cols[:, 0, :], ps[:, 7, 0:16], ACT.Copy).then_inc(S["cols_ready"], 1)

                def fb_copy(q):
                    act.wait_ge(S["fb_done"], q + 1)
                    if q == 0:
                        act.wait_ge(S["cols_ready"], 1)
                    for h in (2 * q, 2 * q + 1):
                        row = ps[:, 6 + q % 2, (h % 2) * SEQ:(h % 2 + 1) * SEQ]
                        nc.scalar.activation(fbias[:, h, 0:P], row[:, 0:P], ACT.Identity, scale=-1.0,
                                             bias=cols[:, 0, h:h + 1]).then_inc(S["fb_copied"], 1)
                        nc.scalar.activation(fbias[:, h, P:3 * P], row, ACT.Identity, scale=-1.0,
                                             bias=cols[:, 0, FH + h:FH + h + 1]).then_inc(S["fb_copied"], 1)

                def exps(h):
                    act.wait_ge(S["max_ready"], 2 * (h + 1))
                    for t, c in ((0, slice(0, P)), (1, slice(P, 3 * P))):
                        nc.scalar.activation(zbuf[:, h % 2, c], zbuf[:, h % 2, c], ACT.Exp,
                                             bias=rowmax[:, t, h:h + 1],
                                             accum_out=rowsum[:, t, h:h + 1]).then_inc(S["p_ready"], 1)

                def pt_copy(h):
                    act.wait_ge(S["p_turned"], h + 1)
                    if h >= 2:
                        act.wait_ge(S["pv_done"], h - 1)
                    nc.scalar.activation(ptbuf[:, h % 2, :], ps[:, 2 + h % 2, 0:3 * P], ACT.Copy).then_inc(
                        S["pt_ready"], 1)

                for m in range(7):
                    slots[2 * m + 1].append(lambda m=m: evac(m))
                for m in range(4):
                    slots[2 * m + 3].append(lambda m=m: qk_evac(m))
                slots[1].append(soft)
                slots[4].append(cols_copy)
                for q in range(4):
                    slots[4 + q].append(lambda q=q: fb_copy(q))
                for k in range(4):
                    slots[10 + k] += [lambda h=2 * k: exps(h), lambda h=2 * k + 1: exps(h)]
                    slots[11 + k] += [lambda h=2 * k: pt_copy(h), lambda h=2 * k + 1: pt_copy(h)]
                slots[15] = [lambda: evac_tile(7, 0), lambda: stage_hi(s + 1, MIX_GROUPS["B"], (0, 1)),
                             lambda: evac_tile(7, 1), None, lambda: stage_hi(s + 1, MIX_GROUPS["B"], (2, 3))]
                return slots

            def plan_c(n, j):
                S, c0, u0, s = LS, FIRST_CHUNK[n], FIRST_UNIT[n], STAGE[n]
                slots = {k: [] for k in range(12)}

                def evac(m):
                    for t in range(NT):
                        evac_tile(m, t)

                def evac_tile(m, t):
                    if True:
                        wait_tile(t, c0 + m, u0 + 2 * m + 1)
                        bank = ps[:, 4 + t, :]
                        r = rms[:, t:t + 1]
                        if m < 2:
                            nc.scalar.activation(nat[:, m % 2, t, :], bank, ACT.Copy, scale=r).then_inc(
                                S["nat_ready"], 1)
                        elif m < 4:
                            nc.scalar.activation(v_piece(t, m - 2, "C"), bank.rearrange("p (h n) -> p h n", h=2),
                                                 ACT.Copy, scale=r).then_inc(S["v_ready"], 1)
                        else:
                            nc.scalar.activation(gate_half(t, m - 4), bank, ACT.Silu, scale=r).then_inc(
                                S["og_ready"], 1)

                def qk_evac(m):
                    act.wait_ge(S["turned"], m + 1)
                    for b in range(2):
                        nc.scalar.activation(qkt[:, 4 * m + 2 * b:4 * m + 2 * b + 2, :],
                                             ps[:, 2 * m + b, :].rearrange("p (h n) -> p h n", h=2),
                                             ACT.Copy, scale=(GDK ** -0.5 if m == 0 else 1.0)).then_inc(
                            S["qk_ready"], 1)

                def glr_copy():
                    act.wait_ge(S["glr_turned"], 1)
                    nc.scalar.activation(glrt, ps[0:GRANK, 7, 0:SEQ], ACT.Copy).then_inc(S["glrt_ready"], 1)

                def z_bias():
                    act.wait_ge(S["z_done"], 1)
                    for h in range(GH):
                        nc.scalar.activation(ebuf[:, 1, h * SEQ:(h + 1) * SEQ],
                                             ps[:, 6 + h // 2, (h % 2) * SEQ:(h % 2 + 1) * SEQ], ACT.Identity,
                                             bias=glab[:, h:h + 1]).then_inc(S["z_ready"], 1)
                    log_sigmoid_part(S, ebuf[:, 1, :], ebuf[:, 0, :], S["z_ready"], GH)

                def decay_exp(lv):
                    act.wait_ge(S["diff_ready"], 2 * lv)
                    nc.scalar.activation(ebuf[:, lv % 2, :], ebuf[:, lv % 2, :], ACT.Exp,
                                         scale=1.0 / GTAU).then_inc(S["e_ready"], 1)

                def across_copy():
                    act.wait_ge(S["lvl_done"], GLA_LEVELS)
                    nc.scalar.activation(across[:, :, :], ps[:, 0, :].rearrange("p (h n) -> p h n", h=GH),
                                         ACT.Copy).then_inc(S["ax_ready"], 1)

                for m in range(6):
                    slots[2 * m + 1].append(lambda m=m: evac(m))
                for m in range(2):
                    slots[2 * m + 2].append(lambda m=m: qk_evac(m))
                slots[1].append(glr_copy)
                slots[2].append(z_bias)
                for lv in range(1, GLA_LEVELS):
                    slots[GLA_PE[lv] - 1].append(lambda lv=lv: decay_exp(lv))
                slots[2].insert(0, None)
                slots[11].append(across_copy)
                for h in range(3):
                    slots[11].append(lambda h=h: head_square(S, h, False))
                slots[11] += [lambda: stage_hi(s + 1, MIX_GROUPS["C"], (0, 1)), lambda: head_square(S, 3, False),
                              None, lambda: stage_hi(s + 1, MIX_GROUPS["C"], (2, 3))]
                return slots

            act.dma_start(ident[:], ident_in).then_inc(G["ident_in"], 16)
            split_hi(0)

            def gate_weights():
                act.wait_ge(G["const"], 16 * 7)
                for lay in range(DEPTH):
                    width = KT * GCOLS[KINDS[lay % 3]]
                    nc.scalar.activation(gw_hi[:, lay, 0:width], gw_raw[:, lay, 0:width], ACT.Copy).then_inc(
                        G["gw_hi_ready"], 1)

            for n, (kind, j) in enumerate(SUBS):
                s, u0 = STAGE[n], FIRST_UNIT[n]
                stage_hi(s, NORM_GROUPS, (0, 1))
                split_hi(u0 + 1)
                square_rows(s, 0)
                stage_hi(s, NORM_GROUPS, (2,))
                square_rows(s, 1)
                stage_hi(s, NORM_GROUPS, (3,))
                split_hi(u0 + 2)
                if kind == "F":
                    ffn(n, j, n)
                    if n == 0:
                        gate_weights()
                    continue
                act.wait_ge(G["rms_ready"], n + 1)
                slots = {"A": plan_a, "B": plan_b, "C": plan_c}[kind](n, j)
                pu = PROJ_UNITS[kind]
                for k in range(pu):
                    if None not in slots[k]:
                        slots[k].append(None)
                    for step in slots[k]:
                        if step:
                            step()
                        else:
                            split_hi(u0 + k + AHEAD)
                for k in range(OUT_UNITS - 2):
                    split_hi(u0 + pu + k + AHEAD)
            for t in range(NT):
                square_rows(N_STAGE, t)

        @block.vector
        def _(dve):
            def split_lo(u, count=None):
                if u >= N_UNITS:
                    return
                dve.wait_ge(G["w_hi_ready"], u + 1 if count is None else count)
                nc.vector.tensor_tensor(w_lo[:, u % SPL, :], raw[:, u % RAW, :], w_hi[:, u % SPL, :].bitcast(F32),
                                        ALU.subtract).then_inc(G["w_lo_ready"], 1)

            def stage_lo(s, groups, some):
                for g in some:
                    t, half, bank = groups[g]
                    dve.wait_ge(G["xt_hi_ready"], 4 * s + g + 1)
                    nc.vector.tensor_tensor(xt_lo[:, t, 4 * half:4 * half + 4, :],
                                            ps[:, bank, :].rearrange("p (k n) -> p k n", k=4),
                                            xt_hi[:, t, 4 * half:4 * half + 4, :].bitcast(F32),
                                            ALU.subtract).then_inc(G["xt_lo_ready"], 1)

            def new_x(n, t, half):
                if t and half:
                    dve.wait_ge(G["unit_used"], FIRST_UNIT[n] if n < len(SUBS) else N_UNITS)
                else:
                    dve.wait_ge(G["acc_done"], 3 * (n - 1) + 2 * t + half + 1)
                scale = 0.5 if SUBS[n - 1][0] == "F" else 1.0
                part = xres[:, t, half * BANK:(half + 1) * BANK]
                nc.vector.scalar_tensor_tensor(out=part, in0=ps[:, 2 * t + half, :], scalar=scale, in1=part,
                                               op0=ALU.mult, op1=ALU.add).then_inc(G["x_new"], 1)

            def weigh_x(n, t, half):
                v = VEC[n]
                if t + half == 0:
                    dve.wait_ge(vec_landed[v % 2], 16 * (v // 2 + 1))
                c = slice(half * BANK, (half + 1) * BANK)
                if n == 0:
                    dve.wait_ge(G["x_in"], 16 * NT)
                else:
                    dve.wait_ge(G["x_new"], 4 * (n - 1) + 2 * t + half + 1)
                nc.vector.tensor_tensor(src[:, t, c], xres[:, t, c], vec[:, v % 2, c], ALU.mult).then_inc(
                    G["src_ready"], 1)

            def hidden(count):
                for t in range(NT):
                    dve.wait_ge(G["silu_ready"], count + (t + 1))
                    nc.vector.scalar_tensor_tensor(out=hid[:, t, :], in0=ps[:, 4 + t, HC:2 * HC],
                                                   scalar=rms[:, t:t + 1], in1=silu_g[:, t, :],
                                                   op0=ALU.mult, op1=ALU.mult).then_inc(G["hid_ready"], 1)

            def hidden_lo(count):
                dve.wait_ge(G["ht_hi_ready"], count)
                nc.vector.tensor_tensor(ht_lo[:, :, :, :], ps[:, 6, :].rearrange("p (k t n) -> p k t n", k=2, t=NT),
                                        ht_hi[:, :, :, :].bitcast(F32), ALU.subtract).then_inc(G["ht_lo_ready"], 1)

            def ffn(n, j):
                u0, h0, hid0 = FIRST_UNIT[n], HT * j, NT * NCH * j
                hidden(hid0)
                split_lo(u0 + 3)
                split_lo(u0 + 4)

                def body(i):
                    for b in range(2):
                        ua = u0 + 2 + 3 * b
                        hidden_lo(i * 2 + (h0 + b + 1))
                        for q in range(3):
                            if q == 1:
                                hidden(i * 4 + (hid0 + 2 + 2 * b))
                            v = ua + AHEAD + q
                            if not isinstance(i, int):
                                split_lo(v, count=i * 6 + (v + 1))
                            elif not (b and q == 2):
                                split_lo(6 * i + v)

                with dve.Fori(0, LOOPED) as i:
                    body(i)
                body(LOOPED)
                for t in range(NT):
                    dve.wait_ge(G["ht_hi_ready"], h0 + NCH + t)
                    nc.vector.tensor_tensor(ht_lo[:, :, t, :], ps[:, 6 + t, 0:2 * P].rearrange("p (k n) -> p k n", k=2),
                                            ht_hi[:, :, t, :].bitcast(F32), ALU.subtract).then_inc(
                        G["ht_lo_ready"], 1)

            def head_out(S, s, h, den):
                dve.wait_ge(S["rs_ready"], h + 1)
                for t in range(NT):
                    dve.wait_ge(S["ogw_ready"], NT * (h // 2) + t + 1)
                    ins = nc.vector.scalar_tensor_tensor(
                        out=src[:, t, h * MDH:(h + 1) * MDH], in0=ps[:, HEAD_BANK[h] + t, 0:MDH],
                        scalar=hrr[:, 2 * h + t:2 * h + t + 1], in1=og[:, t, h * MDH:(h + 1) * MDH],
                        op0=ALU.mult, op1=ALU.mult)
                    ins.then_inc(G["src_ready"] if h % 2 else S["y_done"], 1)

            def plan_a(n, j):
                S, s = MS[j], STAGE[n]
                slots = {k: [] for k in range(16)}

                def gate_bias():
                    dve.wait_ge(S["gate_mm"], 1)
                    dve.wait_ge(G["rms_ready"], n + 1)
                    for t in range(NT):
                        nc.vector.scalar_tensor_tensor(out=gates[:, t, 0:8], in0=ps[:, 6, 16 * t:16 * t + 8],
                                                       scalar=rms[:, t:t + 1], in1=gbias[:, 2 * j + j, :],
                                                       op0=ALU.mult, op1=ALU.add).then_inc(S["gates_ready"], 1)

                def rows():
                    f, i = ps[0:MH, 7, SEQ:2 * SEQ], ps[0:MH, 7, 0:SEQ]
                    r = [rowbuf[0:MH, k, :] for k in range(6)]
                    dve.wait_ge(S["soft"], 3)
                    nc.vector.scalar_tensor_tensor(out=r[1], in0=f, scalar=0.0, in1=r[0], op0=ALU.min,
                                                   op1=ALU.subtract).then_inc(S["rows"], 1)
                    dve.wait_ge(S["rows"], 1)
                    nc.vector.tensor_tensor_scan(r[2], ones[0:MH, :], r[1], 0.0, ALU.mult, ALU.add).then_inc(
                        S["rows"], 1)
                    dve.wait_ge(S["rows"], 2)
                    nc.vector.tensor_tensor(r[3], i, r[2], ALU.subtract).then_inc(S["rows"], 1)
                    dve.wait_ge(S["rows"], 3)
                    nc.vector.tensor_tensor_scan(r[4], ones[0:MH, :], r[3], 0.0, ALU.mult, ALU.max).then_inc(
                        S["rows"], 1)
                    dve.wait_ge(S["rows"], 4)
                    nc.vector.tensor_tensor(r[5], r[2], r[4], ALU.add).then_inc(S["rows"], 1)

                def taps(m):
                    for tap in range(1, 4):
                        for c in range(4):
                            ct = 4 * m + c
                            if tap == 1:
                                dve.wait_ge(S["tap0"], 4 * m + 2 * (c // 2) + 2)
                            elif c == 0:
                                dve.wait_ge(S["taps"], 12 * m + 4 * (tap - 1))
                            bank = ps[:, 2 * (m % 2) + c // 2, (c % 2) * SEQ:(c % 2 + 1) * SEQ]
                            nc.vector.scalar_tensor_tensor(out=qkt[:, ct, tap:SEQ], in0=bank[:, 0:SEQ - tap],
                                                           scalar=convw[:, j, ct, 3 - tap:4 - tap],
                                                           in1=qkt[:, ct, tap:SEQ], op0=ALU.mult,
                                                           op1=ALU.add).then_inc(S["taps"], 1)

                def decay_args():
                    dve.wait_ge(S["cols_ready"], 1)
                    dve.wait_ge(S["mb_done"], 1)
                    for h in range(MH):
                        row = ps[:, 6 + h // 2, (h % 2) * SEQ:(h % 2 + 1) * SEQ]
                        for t, c, r in ((0, slice(0, SEQ), row), (1, slice(SEQ, SEQ + P), row[:, P:SEQ])):
                            a = cols[:, 0, 4 * t + h:4 * t + h + 1]
                            nc.vector.tensor_scalar(decay[:, h, c], r, a, a, ALU.max, ALU.subtract).then_inc(
                                S["dec_arg"], 1)

                def pm(h):
                    dve.wait_ge(S["s_done"], h + 1)
                    if h == 0:
                        dve.wait_ge(S["dec_ready"], 2)
                    nc.vector.scalar_tensor_tensor(out=probs[:, h, :], in0=ps[:, h, 0:3 * P],
                                                   scalar=MDH ** -0.5, in1=decay[:, h, :],
                                                   op0=ALU.mult, op1=ALU.mult).then_inc(S["pm_ready"], 1)

                def dens(h):
                    dve.wait_ge(S["pv_done"], h + 1)
                    c = slice(2 * h, 2 * h + 2)
                    den = ps[:, HEAD_BANK[h]:HEAD_BANK[h] + 2, MDH]
                    guard = cols[:, 1, 0:8].rearrange("p (t h) -> p h t", t=2)[:, h, :]
                    nc.vector.scalar_tensor_tensor(out=rden[:, 0, c], in0=den, scalar=-1.0, in1=guard,
                                                   op0=ALU.mult, op1=ALU.max).then_inc(S["rd_ready"], 1)
                    dve.wait_ge(S["rd_ready"], 3 * h + 1)
                    nc.vector.tensor_tensor(rden[:, 0, c], den, rden[:, 0, c], ALU.max).then_inc(S["rd_ready"], 1)
                    dve.wait_ge(S["rd_ready"], 3 * h + 2)
                    nc.vector.reciprocal(rden[:, 1, c], rden[:, 0, c]).then_inc(S["rd_ready"], 1)

                slots[0].append(gate_bias)
                slots[1].append(rows)
                slots[5].append(decay_args)
                for m in range(4):
                    slots[2 * m + 2].append(lambda m=m: taps(m))
                for h in range(MH):
                    slots[11].append(lambda h=h: pm(h))
                for h in range(3):
                    slots[13].append(lambda h=h: dens(h))
                for k in (2, 4, 6, 8):
                    slots[k].insert(0, None)
                for h in range(2):
                    slots[14].append(lambda h=h: head_out(S, s, h, True))
                slots[15] = [lambda: stage_lo(s + 1, MIX_GROUPS["A"], (0, 1)), None,
                             lambda: head_out(S, s, 2, True), lambda: dens(3), lambda: head_out(S, s, 3, True),
                             lambda: stage_lo(s + 1, MIX_GROUPS["A"], (2, 3))]
                return slots

            def plan_b(n, j):
                S, s = FS, STAGE[n]
                slots = {k: [] for k in range(16)}

                def gate_bias():
                    dve.wait_ge(S["gate_mm"], 1)
                    dve.wait_ge(G["rms_ready"], n + 1)
                    for t in range(NT):
                        nc.vector.scalar_tensor_tensor(out=gates[:, t, 0:8], in0=ps[:, 6, 16 * t:16 * t + 8],
                                                       scalar=rms[:, t:t + 1], in1=gbias[:, 1, :],
                                                       op0=ALU.mult, op1=ALU.add).then_inc(S["gates_ready"], 1)

                def rows():
                    dve.wait_ge(S["soft"], 3)
                    nc.vector.scalar_tensor_tensor(out=ptbuf[0:FH, 0, 0:SEQ], in0=ps[0:FH, 7, 0:SEQ], scalar=0.0,
                                                   in1=zbuf[0:FH, 0, 0:SEQ], op0=ALU.min,
                                                   op1=ALU.subtract).then_inc(S["rows"], 1)
                    dve.wait_ge(S["rows"], 1)
                    nc.vector.tensor_tensor_scan(ptbuf[0:FH, 1, 0:SEQ], ones[0:FH, :], ptbuf[0:FH, 0, 0:SEQ], 0.0,
                                                 ALU.mult, ALU.add).then_inc(S["rows"], 1)

                def square(m):
                    for t in range(NT):
                        dve.wait_ge(S["nat_ready"], 2 * m + t + 1)
                        if m == 0 and t == 0:
                            dve.wait_ge(G["turned"], 4 * s + 4)
                        if 2 * m + t >= 2:
                            dve.wait_ge(S["red"], 2 * m + t - 1)
                        part = nat[:, m % 2, t, :]
                        nc.vector.tensor_tensor(src[:, t, 0:BANK], part, part, ALU.mult).then_inc(S["sq"], 1)
                    for t in range(NT):
                        dve.wait_ge(S["sq"], 2 * m + t + 1)
                        nc.vector.tensor_reduce(hss[:, 8 * m + 4 * t:8 * m + 4 * t + 4],
                                                src[:, t, 0:BANK].rearrange("p (h n) -> p h n", h=4), AX.X,
                                                ALU.add).then_inc(S["red"], 1)

                def normed(m):
                    dve.wait_ge(S["rn_ready"], m + 1)
                    for t in range(NT):
                        part = nat[:, m % 2, t, :].rearrange("p (h n) -> p h n", h=4)
                        r = hrs[:, 8 * m + 4 * t:8 * m + 4 * t + 4].unsqueeze(2).to_broadcast([P, 4, FDH])
                        nc.vector.tensor_tensor(part, part, r, ALU.mult).then_inc(S["natn_ready"], 1)

                def logits(h):
                    dve.wait_ge(S["s_done"], h + 1)
                    if h == 0:
                        dve.wait_ge(S["fb_ready"], 2)
                    nc.vector.scalar_tensor_tensor(out=zbuf[:, h % 2, :], in0=ps[:, h % 2, 0:3 * P],
                                                   scalar=FDH ** -0.5, in1=fbias[:, h, :], op0=ALU.mult,
                                                   op1=ALU.add).then_inc(S["z_ready"], 1)
                    dve.wait_ge(S["z_ready"], h + 1)
                    for t, c in ((0, slice(0, P)), (1, slice(P, 3 * P))):
                        nc.vector.tensor_reduce(rowmax[:, t, h:h + 1], zbuf[:, h % 2, c], AX.X, ALU.max,
                                                negate=True).then_inc(S["max_ready"], 1)

                def inverses(h):
                    dve.wait_ge(S["p_ready"], 2 * (h + 1))
                    nc.vector.reciprocal(rrow[:, :, h:h + 1], rowsum[:, :, h:h + 1]).then_inc(S["sum_inv"], 1)

                def outs(h):
                    dve.wait_ge(S["pv_done"], h // 2 * 2 + 2)
                    dve.wait_ge(S["sum_inv"], h + 1)
                    for t in range(NT):
                        dve.wait_ge(S["og_ready"], NT * (h // 4) + t + 1)
                        c = slice(h * FDH, (h + 1) * FDH)
                        q = (h % 2) * SEQ + t * P
                        ins = nc.vector.scalar_tensor_tensor(
                            out=src[:, t, c], in0=ps[:, 6 + (h // 2) % 2, q:q + P],
                            scalar=rrow[:, t, h:h + 1], in1=og[:, t, c], op0=ALU.mult, op1=ALU.mult)
                        ins.then_inc(G["src_ready"] if h % 4 == 3 else S["y_done"], 1)

                slots[0].append(gate_bias)
                slots[1].append(rows)
                for m in range(4):
                    slots[2 * m + 1].append(lambda m=m: square(m))
                    slots[2 * m + 2].append(lambda m=m: normed(m))
                for k in range(4):
                    slots[10 + k] += [lambda h=2 * k: logits(h), lambda h=2 * k + 1: logits(h)]
                    slots[11 + k] += [lambda h=2 * k: inverses(h), lambda h=2 * k + 1: inverses(h)]
                for h in range(4):
                    slots[13].append(lambda h=h: outs(h))
                slots[15] = [lambda: stage_lo(s + 1, MIX_GROUPS["B"], (0, 1)), lambda: outs(4), lambda: outs(5),
                             None, lambda: outs(6), lambda: outs(7),
                             lambda: stage_lo(s + 1, MIX_GROUPS["B"], (2, 3))]
                return slots

            def plan_c(n, j):
                S, s = LS, STAGE[n]
                slots = {k: [] for k in range(12)}

                def glr():
                    dve.wait_ge(S["gate_mm"], 1)
                    dve.wait_ge(G["rms_ready"], n + 1)
                    for t in range(NT):
                        nc.vector.tensor_scalar(gates[:, t, :], ps[:, 6, 16 * t:16 * t + 16], rms[:, t:t + 1], None,
                                                ALU.mult).then_inc(S["glr_ready"], 1)

                def rows():
                    dve.wait_ge(S["soft"], 3)
                    nc.vector.scalar_tensor_tensor(out=ebuf[:, 0, :], in0=ebuf[:, 1, :], scalar=0.0,
                                                   in1=ebuf[:, 0, :], op0=ALU.min,
                                                   op1=ALU.subtract).then_inc(S["rows"], 1)
                    dve.wait_ge(S["rows"], 1)
                    for h in range(GH):
                        c = slice(h * SEQ, (h + 1) * SEQ)
                        nc.vector.tensor_tensor_scan(gcum[:, c], ones[:, :], ebuf[:, 0, c], 0.0, ALU.mult,
                                                     ALU.add).then_inc(S["rows"], 1)

                def diff(lv):
                    size = 1 << (lv - 1)
                    g = halves(gcum, size)
                    e = halves(ebuf[:, lv % 2, :], size)
                    ref = g[:, :, 0, size - 1:size].to_broadcast([P, 512 // size, size])
                    if lv == 1:
                        dve.wait_ge(S["rows"], 1 + GH)
                    if lv >= 3:
                        dve.wait_ge(S["ks_ready"], lv - 2)
                        dve.wait_ge(S["qs_ready"], lv - 2)
                    nc.vector.tensor_tensor(e[:, :, 1, :], g[:, :, 1, :], ref, ALU.subtract).then_inc(
                        S["diff_ready"], 1)
                    nc.vector.tensor_tensor(e[:, :, 0, :], ref, g[:, :, 0, :], ALU.subtract).then_inc(
                        S["diff_ready"], 1)

                def queries(lv):
                    size = 1 << (lv - 1)
                    dve.wait_ge(S["e_ready"], lv)
                    if lv == 1:
                        dve.wait_ge(S["qk_ready"], 4)
                        dve.wait_ge(S["ks_ready"], 1)
                    if lv >= 3:
                        dve.wait_ge(S["lvl_done"], lv - 1)
                    nc.vector.tensor_tensor(halves(qs[lv % 2], size)[:, :, 1, :],
                                            halves(qkflat[:, 0:1024], size)[:, :, 1, :],
                                            halves(ebuf[:, lv % 2, :], size)[:, :, 1, :],
                                            ALU.mult).then_inc(S["qs_ready"], 1)

                def gather(lv):
                    dve.wait_ge(S["lvl_done"], lv + 1)
                    if lv == 0:
                        dve.wait_ge(S["ks_ready"], 1)
                    else:
                        dve.wait_ge(S["a_ready"], lv)
                    b = 2 * (lv % 2)
                    nc.vector.copy_predicated(amat[:, :, :],
                                              lvl_mask[:, lv:lv + 1, :].to_broadcast([P, 8, P]),
                                              ps[:, b:b + 2, :].rearrange("p b (m n) -> p (b m) n", n=P)).then_inc(
                        S["a_ready"], 1)

                slots[0].append(glr)
                slots[2].append(rows)
                slots[4].append(lambda: diff(1))
                slots[2].insert(0, None)
                for lv in range(1, GLA_LEVELS):
                    k = GLA_PE[lv] - 1
                    if lv + 1 < GLA_LEVELS:
                        slots[k].append(lambda lv=lv: diff(lv + 1))
                    slots[k].append(lambda lv=lv: queries(lv))
                for lv in range(GLA_LEVELS - 1):
                    slots[GLA_PE[lv]].append(lambda lv=lv: gather(lv))
                slots[11] += [lambda: head_out(S, s, 0, False), lambda: head_out(S, s, 1, False),
                              lambda: stage_lo(s + 1, MIX_GROUPS["C"], (0, 1)), lambda: head_out(S, s, 2, False),
                              None, lambda: head_out(S, s, 3, False),
                              lambda: stage_lo(s + 1, MIX_GROUPS["C"], (2, 3))]
                return slots

            def gate_weights():
                dve.wait_ge(G["const"], 16 * 7)
                nc.vector.tensor_copy(lvl_mask[:], mask_raw).then_inc(G["masks_ready"], 1)
                for lay in range(DEPTH):
                    width = KT * GCOLS[KINDS[lay % 3]]
                    dve.wait_ge(G["gw_hi_ready"], lay + 1)
                    nc.vector.tensor_tensor(gw_lo[:, lay, 0:width], gw_raw[:, lay, 0:width],
                                            gw_hi[:, lay, 0:width].bitcast(F32), ALU.subtract).then_inc(
                        G["gw_lo_ready"], 1)

            split_lo(0)
            dve.wait_ge(G["init"], 4)
            for n, (kind, j) in enumerate(SUBS):
                s, u0 = STAGE[n], FIRST_UNIT[n]

                def piece(t, half):
                    if n:
                        new_x(n, t, half)
                    weigh_x(n, t, half)

                piece(0, 0)
                piece(0, 1)
                stage_lo(s, NORM_GROUPS, (0, 1))
                piece(1, 0)
                split_lo(u0 + 1)
                piece(1, 1)
                stage_lo(s, NORM_GROUPS, (2, 3))
                split_lo(u0 + 2)
                if kind == "F":
                    ffn(n, j)
                    if n == 0:
                        gate_weights()
                    continue
                pu = PROJ_UNITS[kind]
                slots = {"A": plan_a, "B": plan_b, "C": plan_c}[kind](n, j)
                for k in range(pu):
                    if None not in slots[k]:
                        slots[k].append(None)
                    for step in slots[k]:
                        if step:
                            step()
                        else:
                            split_lo(u0 + k + AHEAD)
                for k in range(OUT_UNITS - 2):
                    split_lo(u0 + pu + k + AHEAD)
            n, v = len(SUBS), N_VEC - 1
            for t in range(NT):
                for half in range(2):
                    new_x(n, t, half)
                dve.wait_ge(G["x_new"], 4 * (n - 1) + 2 * t + 2)
                nc.vector.tensor_copy(rrow[:, 0, t:t + 1], xres[:, t, 0:1]).then_inc(G["src_ready"], 2)
            dve.wait_ge(vec_landed[v % 2], 16 * (v // 2 + 1))
            for t in range(NT):
                dve.wait_ge(G["rms_ready"], n + 1 + t)
                nc.vector.scalar_tensor_tensor(out=src[:, t, :], in0=xres[:, t, :], scalar=rms[:, t:t + 1],
                                               in1=vec[:, v % 2, :], op0=ALU.mult, op1=ALU.mult).then_inc(
                    G["y_final"], 1)

        @block.tensor
        def _(pe):
            def three(dst, a_hi, a_lo, slot, c, first, last):
                w = slice(c, c + BANK)
                nc.tensor.matmul(dst, a_hi, w_hi[:, slot, w], start=first, stop=False)
                nc.tensor.matmul(dst, a_hi, w_lo[:, slot, w], start=False, stop=False)
                return nc.tensor.matmul(dst, a_lo, w_hi[:, slot, w], start=False, stop=last)

            def turn(s, groups, some):
                for g in some:
                    t, half, bank = groups[g]
                    pe.wait_ge(G["src_ready"], 4 * s + g + 1)
                    for k in range(4):
                        ins = nc.tensor.transpose(ps[:, bank, k * P:(k + 1) * P],
                                                  src[:, t, half * BANK + k * P:half * BANK + (k + 1) * P], ident[:])
                    ins.then_inc(G["turned"], 1)

            def proj_tile(slot, part, t):
                for k in range(4):
                    ins = three(ps[:, 4 + t, :], xt_hi[:, t, 4 * part + k, :], xt_lo[:, t, 4 * part + k, :], slot,
                                k * BANK, part == 0 and k == 0, part == 1 and k == 3)
                return ins

            def proj_unit(u, part, count=None, read_out=None, weave=None):
                pe.wait_ge(G["w_lo_ready"], u + 1 if count is None else count)
                for t in range(NT):
                    if read_out and read_out[t]:
                        pe.wait_ge(*read_out[t])
                    ins = proj_tile(u % SPL, part, t)
                    if part == 1 and t == 0:
                        ins.then_inc(G["tile0_done"], 1)
                    if t == 0 and weave:
                        weave()
                ins.then_inc(G["unit_used"], 1)

            def entry(n, between=None):
                u, s = FIRST_UNIT[n], STAGE[n]
                if n == 0:
                    turn(s, NORM_GROUPS, (0, 1))
                pe.wait_ge(G["w_lo_ready"], u + 1)
                pe.wait_ge(G["xt_lo_ready"], 4 * s + 1)
                proj_tile(u % SPL, 0, 0)
                turn(s, NORM_GROUPS, (2,))
                pe.wait_ge(G["w_lo_ready"], u + 2)
                pe.wait_ge(G["xt_lo_ready"], 4 * s + 2)
                proj_tile((u + 1) % SPL, 1, 0).then_inc(G["tile0_done"], 1)
                turn(s, NORM_GROUPS, (3,))
                pe.wait_ge(G["xt_lo_ready"], 4 * s + 3)
                proj_tile(u % SPL, 0, 1).then_inc(G["unit_used"], 1)
                pe.wait_ge(G["xt_lo_ready"], 4 * s + 4)
                if between:
                    between()
                proj_tile((u + 1) % SPL, 1, 1).then_inc(G["unit_used"], 1)

            def out_tile(u, t, a_hi, a_lo, first, last, weave=None):
                for half in range(2):
                    for k in range(2):
                        ins = three(ps[:, 2 * t + half, :], a_hi(t, k), a_lo(t, k), u % SPL,
                                    k * 2 * BANK + half * BANK, first and k == 0, last and k == 1)
                    if last and not (t and half):
                        ins.then_inc(G["acc_done"], 1)
                    if weave and (t, half) in weave:
                        weave[t, half]()
                if t:
                    ins.then_inc(G["unit_used"], 1)

            def out_unit(u, a_hi, a_lo, first, last, count=None, weave=None, ready=None):
                pe.wait_ge(G["w_lo_ready"], u + 1 if count is None else count)
                for t in range(NT):
                    if ready:
                        pe.wait_ge(ready[0], ready[1] + t)
                    out_tile(u, t, a_hi, a_lo, first, last, weave)

            def next_norm(n):
                if n + 1 == len(SUBS):
                    return None
                return {(0, 1): lambda: turn(STAGE[n + 1], NORM_GROUPS, (0,)),
                        (1, 0): lambda: turn(STAGE[n + 1], NORM_GROUPS, (1,))}

            def turn_hidden(count):
                pe.wait_ge(G["hid_ready"], count)
                for k in range(2):
                    for t in range(NT):
                        ins = nc.tensor.transpose(ps[:, 6, (2 * k + t) * P:(2 * k + t + 1) * P],
                                                  hid[:, t, k * P:(k + 1) * P], ident[:])
                ins.then_inc(G["ht_turned"], 1)

            def turn_hidden_tile(count, t):
                pe.wait_ge(G["hid_ready"], count + t)
                for k in range(2):
                    ins = nc.tensor.transpose(ps[:, 6 + t, k * P:(k + 1) * P], hid[:, t, k * P:(k + 1) * P], ident[:])
                ins.then_inc(G["ht_turned"], 1)

            def h_hi(t, k):
                return ht_hi[:, k, t, :]

            def h_lo(t, k):
                return ht_lo[:, k, t, :]

            def ffn(n, j):
                u0, h0, hid0 = FIRST_UNIT[n], HT * j, NT * NCH * j
                entry(n)

                def chunk(i, b, first=False, weave=None):
                    ua = u0 + 2 + 3 * b
                    proj_unit(ua, 0, count=i * 6 + (ua + 1),
                              read_out=[(G["hid_ready"], i * 4 + (hid0 + 2 * b + 1)), None],
                              weave=lambda: turn_hidden(i * 4 + (hid0 + 2 * b + 2)))
                    proj_unit(ua + 1, 1, count=i * 6 + (ua + 2))
                    pe.wait_ge(G["ht_lo_ready"], i * 2 + (h0 + b + 1))
                    out_unit(ua + 2, h_hi, h_lo, first, False, count=i * 6 + (ua + 3), weave=weave)

                chunk(0, 0, first=True)
                chunk(0, 1)
                with pe.Fori(1, LOOPED) as i:
                    for b in range(2):
                        chunk(i, b)
                last = hid0 + 2 * NCH - 1
                chunk(LOOPED, 0)
                chunk(LOOPED, 1, weave={(0, 1): lambda: turn_hidden_tile(last, 0),
                                        (1, 0): lambda: turn_hidden_tile(last, 1)})
                out_unit(u0 + FFN_UNITS - 1, h_hi, h_lo, False, True, weave=next_norm(n),
                         ready=(G["ht_lo_ready"], h0 + NCH))

            def gate_products(S, lay, width):
                pe.wait_ge(G["gw_lo_ready"], lay + 1)
                for t in range(NT):
                    dst = ps[:, 6, 16 * t:16 * t + width]
                    for k in range(KT):
                        c = slice(k * width, (k + 1) * width)
                        nc.tensor.matmul(dst, xt_hi[:, t, k, :], gw_hi[:, lay, c], start=(k == 0), stop=False)
                        nc.tensor.matmul(dst, xt_hi[:, t, k, :], gw_lo[:, lay, c], start=False, stop=False)
                        ins = nc.tensor.matmul(dst, xt_lo[:, t, k, :], gw_hi[:, lay, c], start=False,
                                               stop=(k == KT - 1))
                ins.then_inc(S["gate_mm"], 1)

            def turn_nat(S, m, ready, value, banks):
                pe.wait_ge(ready, value)
                for c in range(4):
                    for t in range(NT):
                        q = (c % 2) * SEQ + t * P
                        ins = nc.tensor.transpose(ps[:, banks + c // 2, q:q + P],
                                                  nat[:, m % 2, t, c * P:(c + 1) * P], ident[:])
                ins.then_inc(S["turned"], 1)

            def spread(bank, q, row, heads, h):
                return nc.tensor.matmul(ps[:, bank, q:q + SEQ], ident[0:heads, h:h + 1].to_broadcast([heads, P]),
                                        row, start=True, stop=True)

            def plan_a(n, j):
                S = MS[j]
                slots = {k: [] for k in range(16)}

                def turn_gates():
                    pe.wait_ge(S["gates_ready"], 2)
                    for g in range(2):
                        for t in range(NT):
                            ins = nc.tensor.transpose(ps[0:MH, 7, g * SEQ + t * P:g * SEQ + (t + 1) * P],
                                                      gates[:, t, MH * g:MH * g + MH], ident[:])
                    ins.then_inc(S["gates_turned"], 1)

                def turn_rows():
                    pe.wait_ge(S["en_ready"], 1)
                    for g, r in ((0, 3), (1, 5)):
                        for t in range(NT):
                            ins = nc.tensor.transpose(ps[:, 6, 8 * g + 4 * t:8 * g + 4 * t + 4],
                                                      rowbuf[0:MH, r, t * P:(t + 1) * P], ident[0:MH, 0:MH])
                    ins.then_inc(S["cols_turned"], 1)

                def spread_m():
                    pe.wait_ge(S["cols_ready"], 1)
                    for h in range(MH):
                        ins = spread(6 + h // 2, (h % 2) * SEQ, rowbuf[0:MH, 4, :], MH, h)
                    ins.then_inc(S["mb_done"], 1)

                def turn_qk(m):
                    if m >= 2:
                        pe.wait_ge(S["taps"], 12 * (m - 1))
                    turn_nat(S, m, S["nat_ready"], 2 * (m + 1), 2 * (m % 2))

                def scores(h):
                    if h == 0:
                        pe.wait_ge(S["conv_ready"], 4)
                    for k in range(2):
                        nc.tensor.matmul(ps[:, h, 0:SEQ], qkt[:, 8 + 2 * h + k, 0:P], qkt[:, 2 * h + k, :],
                                         start=(k == 0), stop=(k == 1))
                    for k in range(2):
                        ins = nc.tensor.matmul(ps[:, h, SEQ:SEQ + P], qkt[:, 8 + 2 * h + k, P:SEQ],
                                               qkt[:, 2 * h + k, P:SEQ], start=(k == 0), stop=(k == 1))
                    ins.then_inc(S["s_done"], 1)

                def values(h):
                    pe.wait_ge(S["pm_ready"], MH)
                    pe.wait_ge(S["v_ready"], 4)
                    b = HEAD_BANK[h]
                    nc.tensor.matmul(ps[:, b, 0:MDH + 1], probs[:, h, 0:P], vaug[:, 0, h, :], start=True, stop=True)
                    nc.tensor.matmul(ps[:, b + 1, 0:MDH + 1], probs[:, h, P:SEQ], vaug[:, 0, h, :], start=True,
                                     stop=False)
                    nc.tensor.matmul(ps[:, b + 1, 0:MDH + 1], probs[:, h, SEQ:SEQ + P], vaug[:, 1, h, :],
                                     start=False, stop=True).then_inc(S["pv_done"], 1)

                def last_head():
                    pe.wait_ge(S["og_ready"], 4)
                    values(3)

                slots[0].append(lambda: gate_products(S, 3 * j, 8))
                slots[1].append(turn_gates)
                slots[3].append(turn_rows)
                slots[5].append(spread_m)
                for m in range(4):
                    slots[2 * m + 2].append(lambda m=m: turn_qk(m))
                for h in range(MH):
                    slots[11].append(lambda h=h: scores(h))
                for h in range(3):
                    slots[13].append(lambda h=h: values(h))
                return slots, last_head

            def plan_b(n, j):
                S = FS
                slots = {k: [] for k in range(16)}

                def turn_gates():
                    pe.wait_ge(S["gates_ready"], 2)
                    for t in range(NT):
                        ins = nc.tensor.transpose(ps[0:FH, 7, t * P:(t + 1) * P], gates[:, t, 0:FH], ident[:])
                    ins.then_inc(S["gates_turned"], 1)

                def turn_rows():
                    pe.wait_ge(S["rows"], 2)
                    for t in range(NT):
                        ins = nc.tensor.transpose(ps[:, 7, FH * t:FH * (t + 1)],
                                                  ptbuf[0:FH, 1, t * P:(t + 1) * P], ident[0:FH, 0:FH])
                    ins.then_inc(S["cols_turned"], 1)

                def spread_f(q):
                    if q == 1:
                        pe.wait_ge(S["cols_ready"], 1)
                    if q >= 2:
                        pe.wait_ge(S["fb_copied"], 4 * (q - 1))
                    for h in (2 * q, 2 * q + 1):
                        ins = spread(6 + q % 2, (h % 2) * SEQ, ptbuf[0:FH, 1, 0:SEQ], FH, h)
                    ins.then_inc(S["fb_done"], 1)

                def turn_qk(m):
                    if m >= 2:
                        pe.wait_ge(S["qk_ready"], 2 * (m - 1))
                    turn_nat(S, m, S["natn_ready"], 2 * (m + 1), 2 * (m % 2))

                def scores(h):
                    if h == 0:
                        pe.wait_ge(S["qk_ready"], 8)
                    if h >= 2:
                        pe.wait_ge(S["z_ready"], h - 1)
                    q, k = qkt[:, h, :], qkt[:, FH + h, :]
                    nc.tensor.matmul(ps[:, h % 2, 0:P], q[:, 0:P], k[:, 0:P], start=True, stop=True)
                    nc.tensor.matmul(ps[:, h % 2, P:3 * P], q[:, P:SEQ], k, start=True, stop=True).then_inc(
                        S["s_done"], 1)

                def turn_probs(h):
                    pe.wait_ge(S["p_ready"], 2 * (h + 1))
                    if h >= 2:
                        pe.wait_ge(S["pt_ready"], h - 1)
                    for b in range(3):
                        ins = nc.tensor.transpose(ps[:, 2 + h % 2, b * P:(b + 1) * P],
                                                  zbuf[:, h % 2, b * P:(b + 1) * P], ident[:])
                    ins.then_inc(S["p_turned"], 1)

                def values(h):
                    pe.wait_ge(S["pt_ready"], h + 1)
                    if h == 0:
                        pe.wait_ge(S["v_ready"], 4)
                    if h == 4:
                        pe.wait_ge(S["y_done"], 3 * 2 - 2)
                    if h == 6:
                        pe.wait_ge(G["src_ready"], 4 * (STAGE[n] + 1) + 2)
                    v = [vaug[:, t, :, :].rearrange("p h n -> p (h n)")[:, h * FDH:(h + 1) * FDH] for t in range(NT)]
                    bank, q, pt = 6 + (h // 2) % 2, (h % 2) * SEQ, ptbuf[:, h % 2, :]
                    nc.tensor.matmul(ps[:, bank, q:q + P], pt[:, 0:P], v[0], start=True, stop=True)
                    nc.tensor.matmul(ps[:, bank, q + P:q + SEQ], pt[:, P:SEQ], v[0], start=True, stop=False)
                    nc.tensor.matmul(ps[:, bank, q + P:q + SEQ], pt[:, SEQ:SEQ + P], v[1], start=False,
                                     stop=True).then_inc(S["pv_done"], 1)

                slots[0].append(lambda: gate_products(S, 1, 8))
                slots[1].append(turn_gates)
                slots[4].append(turn_rows)
                for q in range(4):
                    slots[4 + q].append(lambda q=q: spread_f(q))
                for m in range(4):
                    slots[2 * m + 3].append(lambda m=m: turn_qk(m))
                for k in range(6):
                    for step, pair in ((values, k - 2), (turn_probs, k - 1), (scores, k)):
                        if 0 <= pair < 4:
                            slots[10 + k] += [lambda f=step, h=2 * pair: f(h), lambda f=step, h=2 * pair + 1: f(h)]
                return slots, None

            def plan_c(n, j):
                S = LS
                slots = {k: [] for k in range(12)}

                def turn_gates():
                    pe.wait_ge(S["glr_ready"], 2)
                    for t in range(NT):
                        ins = nc.tensor.transpose(ps[0:GRANK, 7, t * P:(t + 1) * P], gates[:, t, :], ident[:])
                    ins.then_inc(S["glr_turned"], 1)

                def gate_up():
                    pe.wait_ge(S["glrt_ready"], 1)
                    for h in range(GH):
                        ins = nc.tensor.matmul(ps[:, 6 + h // 2, (h % 2) * SEQ:(h % 2 + 1) * SEQ],
                                               glaup[:, h * GDK:(h + 1) * GDK], glrt, start=True, stop=True)
                    ins.then_inc(S["z_done"], 1)

                def level(lv):
                    if lv == 0:
                        pe.wait_ge(S["qk_ready"], 4)
                        q, k = qkflat[:, 0:1024], qkflat[:, 1024:2048]
                    else:
                        pe.wait_ge(S["qs_ready"], lv)
                        pe.wait_ge(S["ks_ready"], lv)
                        q, k = qs[lv % 2], ks[lv % 2]
                    if lv >= 2:
                        pe.wait_ge(S["a_ready"], lv - 1)
                    for h in range(GH):
                        base = h * SEQ
                        if lv == GLA_LEVELS - 1:
                            ins = nc.tensor.matmul(ps[:, 0, h * P:(h + 1) * P], k[:, base:base + P],
                                                   q[:, base + P:base + SEQ], start=True, stop=True)
                            continue
                        for t in range(NT):
                            m, c = 2 * h + t, slice(base + t * P, base + (t + 1) * P)
                            ins = nc.tensor.matmul(ps[:, 2 * (lv % 2) + m // 4, (m % 4) * P:(m % 4 + 1) * P],
                                                   k[:, c], q[:, c], start=True, stop=True)
                    ins.then_inc(S["lvl_done"], 1)

                def values(h):
                    b = HEAD_BANK[h]
                    if h == 0:
                        pe.wait_ge(S["v_ready"], 4)
                        pe.wait_ge(S["a_ready"], GLA_LEVELS - 1)
                        pe.wait_ge(S["ax_ready"], 1)
                    if h == 3:
                        pe.wait_ge(S["og_ready"], 4)
                    nc.tensor.matmul(ps[:, b, 0:GDV], amat[:, 2 * h, :], vaug[:, 0, h, 0:GDV], start=True, stop=True)
                    nc.tensor.matmul(ps[:, b + 1, 0:GDV], across[:, h, :], vaug[:, 0, h, 0:GDV], start=True,
                                     stop=False)
                    nc.tensor.matmul(ps[:, b + 1, 0:GDV], amat[:, 2 * h + 1, :], vaug[:, 1, h, 0:GDV], start=False,
                                     stop=True).then_inc(S["pv_done"], 1)

                slots[0].append(lambda: gate_products(S, 2, GRANK))
                slots[1].append(turn_gates)
                slots[2].append(gate_up)
                for m in range(2):
                    slots[2 * m + 2].append(lambda m=m: turn_nat(S, m, S["nat_ready"], 2 * (m + 1), 2 * m))
                for lv in range(GLA_LEVELS):
                    slots[GLA_PE[lv]].append(lambda lv=lv: level(lv))
                for h in range(3):
                    slots[11].append(lambda h=h: values(h))
                slots[11] += [lambda: turn(STAGE[n] + 1, MIX_GROUPS["C"], (0, 1)), lambda: values(3)]
                return slots, None

            def mixer(n, kind, j):
                u0, s, pu = FIRST_UNIT[n], STAGE[n], PROJ_UNITS[kind]
                slots, late = {"A": plan_a, "B": plan_b, "C": plan_c}[kind](n, j)
                S = {"A": MS[j], "B": FS, "C": LS}[kind]
                qk = {"A": 4, "B": 4, "C": 2}[kind]
                copies = [(S["nat_ready"], 2 * m) for m in range(qk)] + \
                         [(S["v_ready"], 2 * m) for m in range(2)] + [(S["og_ready"], 2 * m) for m in range(2)]

                def turn_half():
                    turn(s + 1, MIX_GROUPS[kind], (0, 1))

                entry(n, slots[0][0])
                for k in range(1, pu):
                    if k > 1:
                        read = None
                        if k % 2 == 0:
                            done, before = copies[k // 2 - 1]
                            read = [(done, before + 1), (done, before + 2)]
                        proj_unit(u0 + k, k % 2, read_out=read,
                                  weave=turn_half if k == pu - 1 and kind != "C" else None)
                    for step in slots[k]:
                        step()

                def rows_of(q):
                    return (lambda t, k: xt_hi[:, t, 2 * q + k, :]), (lambda t, k: xt_lo[:, t, 2 * q + k, :])

                pe.wait_ge(G["xt_lo_ready"], 4 * (s + 1) + 2)
                pe.wait_ge(G["w_lo_ready"], u0 + pu + 1)
                out_tile(u0 + pu, 0, *rows_of(0), True, False)
                if late:
                    late()
                if kind != "B":
                    pe.wait_ge(S["y_done"], 4)
                out_tile(u0 + pu, 1, *rows_of(0), True, False)
                out_unit(u0 + pu + 1, *rows_of(1), False, False)
                turn(s + 1, MIX_GROUPS[kind], (2, 3))
                pe.wait_ge(G["xt_lo_ready"], 4 * (s + 1) + 4)
                out_unit(u0 + pu + 2, *rows_of(2), False, False)
                out_unit(u0 + pu + 3, *rows_of(3), False, True, weave=next_norm(n))

            pe.wait_ge(G["ident_in"], 16)
            for n, (kind, j) in enumerate(SUBS):
                if kind == "F":
                    ffn(n, j)
                else:
                    mixer(n, kind, j)


def kernel(**inputs):
    import numpy as np
    import concourse.bacc as bacc
    from concourse.bass_utils import run_bass_kernel_spmd as run

    a = {k: np.asarray(v) for k, v in inputs.items()}

    def in_units(w, cols):
        w = w.reshape(2, 4, P, cols // BANK, BANK).transpose(3, 0, 2, 1, 4)
        return w.reshape(-1, P, UNIT)

    def out_units(w):
        return w.reshape(-1, 2, P, D).transpose(0, 2, 1, 3).reshape(-1, P, UNIT)

    stream = np.empty((N_UNITS, P, UNIT), np.float32)
    gate = np.zeros((DEPTH, P, P), np.float32)
    vecs = np.empty((N_VEC, D), np.float32)
    gb = np.zeros((DEPTH, 8), np.float32)
    for n, (kind, j) in enumerate(SUBS):
        u, layer = FIRST_UNIT[n], n // 3
        vecs[VEC[n]] = a["norm_w"][layer, n % 3]
        if kind == "F":
            w1 = a["ffn_w_in"][j // 2, j % 2].reshape(D, 2, NCH, HC).transpose(0, 2, 1, 3).reshape(D, 2 * F)
            w1 = in_units(w1, 2 * F)
            w2 = out_units(a["ffn_w_out"][j // 2, j % 2])
            stream[u:u + 2] = w1[0:2]
            body = stream[u + 2:u + FFN_UNITS - 1].reshape(NCH - 1, 3, P, UNIT)
            body[:, 0:2] = w1[2:].reshape(NCH - 1, 2, P, UNIT)
            body[:, 2] = w2[0:NCH - 1]
            stream[u + FFN_UNITS - 1] = w2[NCH - 1]
            continue
        name = {"A": "mlstm", "B": "fox", "C": "gla"}[kind]
        w, pu, width = a[name + "_w_in"][j], PROJ_UNITS[kind], GCOLS[kind]
        main = w.shape[1] - width
        stream[u:u + pu] = in_units(w[:, 0:main], main)
        stream[u + pu:u + pu + OUT_UNITS] = out_units(a[name + "_w_out"][j])
        gate[layer, :, 0:KT * width] = w[:, main:].reshape(KT, P, width).transpose(1, 0, 2).reshape(P, KT * width)
        if kind == "A":
            gb[layer] = a["mlstm_b_gate"][j]
            vecs[VEC[n] + 1] = a["mlstm_norm_w"][j]
        if kind == "B":
            gb[layer] = a["fox_b_f"][j]
        if kind == "C":
            vecs[VEC[n] + 1] = a["gla_norm_w"][j]
    vecs[N_VEC - 1] = a["final_norm_w"]

    masks = np.zeros((P, 8, P), np.float32)
    for q in range(P):
        masks[q, 0, q] = 1
        for lv in range(1, 8):
            size = 1 << (lv - 1)
            if q // size % 2 == 0:
                t0 = (q // size + 1) * size
                masks[q, lv, t0:t0 + size] = 1

    arrays = {
        "stream": stream,
        "x": a["x"],
        "vecs": vecs,
        "gate_w": gate.transpose(1, 0, 2),
        "mg_bias": np.broadcast_to(gb[None], (P, DEPTH, 8)),
        "conv_w": a["mlstm_conv_w"].reshape(2, 4, 16, P).transpose(3, 0, 2, 1),
        "fox_b": a["fox_b_f"],
        "fox_qk": a["fox_qk_norm"][0].transpose(1, 0),
        "gla_up": a["gla_w_gate_up"][0],
        "gla_b": a["gla_b_gate"][0].reshape(GH, GDK).transpose(1, 0),
        "masks": masks,
        "ident": np.eye(P, dtype=np.float32),
    }
    nc = bacc.Bacc("TRN2", target_bir_lowering=False, num_devices=1)
    aps = []
    for name in arrays:
        arrays[name] = np.ascontiguousarray(arrays[name])
        aps.append(nc.dram_tensor("in_" + name, arrays[name].shape, mybir.dt.from_np(arrays[name].dtype),
                                  kind="ExternalInput").ap())
    out = nc.dram_tensor("out_y", (1, SEQ, D), F32, kind="ExternalOutput").ap()
    build(nc, *aps, out)
    r = run(nc, [{"in_" + k: v for k, v in arrays.items()}], core_ids=[0])
    return r.results[0]["out_y"]
```

```python
from contextlib import ExitStack

import concourse.bass as bass
from concourse import mybir


F32 = mybir.dt.float32
F32R = mybir.dt.float32r
U8 = mybir.dt.uint8
ALU = mybir.AluOpType
ACT = mybir.ActivationFunctionType
AX = mybir.AxisListType

P = 128
SEQ = 256
D = 1024
F = 2816
DEPTH = 4
EPS = 1e-6
NT = SEQ // P
KT = D // P
UNIT = 2048
BANK = 512
HC = 256
NCH = F // HC
FFN_UNITS = 3 * NCH
RAW = 6
SPL = 3
AHEAD = SPL
OUT_UNITS = 4

MH, MDH = 4, 256
FH, FDH = 8, 128
GH, GDK, GDV, GRANK, GTAU = 4, 128, 256, 16, 16.0
GCOLS = {"A": 2 * MH, "B": FH, "C": GRANK}
PROJ_UNITS = {"A": 16, "B": 16, "C": 12}
NEG = -1e30

KINDS = "ABC"
SUBS = []
for _layer in range(DEPTH):
    SUBS += [("F", 2 * _layer), (KINDS[_layer % 3], _layer // 3), ("F", 2 * _layer + 1)]

FIRST_UNIT, FIRST_CHUNK, STAGE, OUT_NO, VEC = [], [], [], [], []
_u = _c = _s = _o = _v = 0
for _kind, _ in SUBS:
    FIRST_UNIT.append(_u)
    FIRST_CHUNK.append(_c)
    STAGE.append(_s)
    OUT_NO.append(_o)
    VEC.append(_v)
    _u += FFN_UNITS if _kind == "F" else PROJ_UNITS[_kind] + OUT_UNITS
    _c += NCH if _kind == "F" else PROJ_UNITS[_kind] // 2
    _s += 1 if _kind == "F" else 2
    _o += 1
    _v += 2 if _kind in "AC" else 1
N_UNITS, N_OUT, N_STAGE, N_VEC = _u, _o, _s, _v + 1

NORM_GROUPS = [(0, 0, 6), (0, 1, 7), (1, 0, 0), (1, 1, 1)]
MIX_GROUPS = {"A": [(0, 0, 6), (1, 0, 7), (0, 1, 6), (1, 1, 7)],
              "B": [(0, 0, 0), (1, 0, 1), (0, 1, 4), (1, 1, 5)],
              "C": [(0, 0, 6), (1, 0, 7), (0, 1, 6), (1, 1, 7)]}
HEAD_BANK = [6, 0, 2, 4]

GLA_PE = {0: 6, 1: 7, 2: 7, 3: 8, 4: 8, 5: 9, 6: 10, 7: 10, 8: 11}
GLA_LEVELS = 9


def build(nc, stream, x, vecs, gate_w, gate_sel, conv_w, fox_qk, gla_up, gla_b, masks, ident_in, out):
    with ExitStack() as ctx:
        def sb(name, shape, dt=F32):
            return ctx.enter_context(nc.sbuf_tensor(name, shape, dt))

        def sems(prefix, names):
            return {n: ctx.enter_context(nc.semaphore(prefix + n)) for n in names.split()}

        raw = sb("raw", [P, RAW, UNIT])
        w_hi = sb("w_hi", [P, SPL, UNIT], F32R)
        w_lo = sb("w_lo", [P, SPL, UNIT], F32R)
        xres = sb("xres", [P, NT, D])
        src = sb("src", [P, NT, D])
        xt_hi = sb("xt_hi", [P, NT, KT, P], F32R)
        xt_lo = sb("xt_lo", [P, NT, KT, P], F32R)
        vec = sb("vec", [P, 2, D])
        nat = sb("nat", [P, 2, NT, BANK])
        silu_g = nat[:, 0, :, 0:HC]
        hid = nat[:, 1, :, 0:HC]
        og = nat[:, :, :, :].rearrange("p a t n -> p (a t n)").rearrange("p (t n) -> p t n", t=NT)
        ht_hi = sb("ht_hi", [P, 2, NT, P], F32R)
        ht_lo = sb("ht_lo", [P, 2, NT, P], F32R)
        qkt = sb("qkt", [P, 16, SEQ])
        vaug = sb("vaug", [P, NT, MH, MDH + 1])
        scr = sb("scr", [P, 18, SEQ])
        ident = sb("ident", [P, P])
        ones = sb("ones", [P, SEQ])
        lvl_mask = sb("lvl_mask", [P, 8, P], U8)
        gw_hi = sb("gw_hi", [P, DEPTH, P], F32R)
        gw_lo = sb("gw_lo", [P, DEPTH, P], F32R)
        gw_raw = scr[:, 0:2, :].rearrange("p a n -> p (a n)").rearrange("p (l n) -> p l n", l=DEPTH)
        mask_raw = scr[:, 4:8, :].rearrange("p a n -> p (a n)").rearrange("p (l n) -> p l n", l=8)
        convw = sb("convw", [P, 2, 16, 4])
        qkw = sb("qkw", [P, 2])
        glaup = sb("glaup", [GRANK, GH * GDK])
        glab = sb("glab", [P, GH])
        ssum = sb("ssum", [P, NT])
        msum = sb("msum", [P, NT])
        rms = sb("rms", [P, NT])
        nhalf = sb("nhalf", [P, 8])
        grow = sb("grow", [33, SEQ])
        rrows = sb("rrows", [32, SEQ])
        gsel = sb("gsel", [33, DEPTH, 16])
        cols = sb("cols", [P, 2, 2 * 8])
        rden = sb("rden", [P, 2, 8])
        hss = sb("hss", [P, 32])
        hms = sb("hms", [P, 32])
        hrs = sb("hrs", [P, 32])
        hrr = sb("hrr", [P, 8])
        rowmax = sb("rowmax", [P, 2, FH])
        rowsum = sb("rowsum", [P, 2, FH])
        rrow = sb("rrow", [P, 2, FH])
        ps = ctx.enter_context(nc.psum_tensor("ps", [P, 8, BANK], F32))

        landed = [ctx.enter_context(nc.semaphore(f"landed{j}")) for j in range(RAW)]
        vec_landed = [ctx.enter_context(nc.semaphore(f"vec_landed{j}")) for j in range(2)]
        G = sems("", "const vec0_in half_unit_in w_hi_half ident_in x_in x_in1 gw_spread w_lo_half out_sent w_hi_ready w_lo_ready unit_used tile0_done acc_done src_ready turned "
                     "xt_hi_ready xt_lo_ready x_new sq_ready rms_ready silu_ready hid_ready ht_turned "
                     "ht_hi_ready ht_lo_ready gw_hi_ready gw_lo_ready init y_final pool_chain")
        MS = [sems(f"m{j}_", "nat_ready turned tap0 taps conv_ready gate_mm rms_turned rms_rows gates_ready gates_turned soft rows "
                             "en_ready cols_turned cols_ready mb_done dec_arg dec_exp dec_ready s_done pm_ready "
                             "v_ready pv_done rd_ready ss_ready rs_ready og_ready ogw_ready y_done") for j in range(2)]
        FS = sems("f_", "nat_ready sq red rn_ready natn_ready turned qk_ready gate_mm rms_turned rms_rows gates_ready "
                        "gates_turned soft rows cols_turned cols_ready fb_done fb_copied fb_ready s_done z_ready "
                        "max_ready p_ready sum_inv p_turned pt_ready pv_done v_ready og_ready y_done")
        LS = sems("g_", "nat_ready turned qk_ready gate_mm gates_ready rms_turned rms_rows gates_turned glrt_ready z_done z_ready soft "
                        "rows diff_ready e_ready qs_ready ks_ready lvl_done a_ready ax_ready v_ready pv_done "
                        "ss_ready rs_ready og_ready ogw_ready y_done")
        block = ctx.enter_context(nc.Block())

        flat = scr[:, :, :].rearrange("p a n -> p (a n)")
        decay = flat[:, 0:1536].rearrange("p (h n) -> p h n", h=MH)
        probs = flat[:, 1536:3072].rearrange("p (h n) -> p h n", h=MH)
        rowbuf = flat[:, 3072:4608].rearrange("p (r n) -> p r n", n=SEQ)
        fbias = flat[:, 0:3072].rearrange("p (h n) -> p h n", h=FH)
        zbuf = flat[:, 3072:3840].rearrange("p (b n) -> p b n", b=2)
        ptbuf = flat[:, 3840:4608].rearrange("p (b n) -> p b n", b=2)
        gcum = flat[:, 0:1024]
        ebuf = flat[:, 1024:3072].rearrange("p (b n) -> p b n", b=2)
        amat = flat[:, 3072:4096].rearrange("p (m n) -> p m n", m=8)
        across = flat[:, 4096:4608].rearrange("p (h n) -> p h n", h=GH)
        squares = flat[:, 0:1536].rearrange("p (k n) -> p k n", n=MDH)
        glrt = flat[0:GRANK, 4096:4352]
        qkflat = qkt[:, :, :].rearrange("p a n -> p (a n)")
        srcflat = src[:, :, :].rearrange("p t n -> p (t n)")
        qs = [qkflat[:, 2048:3072], srcflat[:, 0:1024]]
        ks = [qkflat[:, 3072:4096], srcflat[:, 1024:2048]]

        def landed_at(u):
            return 16 * (u // RAW + 1)

        def vec_there(v):
            return (G["vec0_in"], 16) if v == 0 else (vec_landed[v % 2], 16 * ((v + 1) // 2))

        LOOPED = NCH // 2 - 1
        HT = NCH + 1

        def halves(ap, size):
            return ap.rearrange("p (b two s) -> p b two s", two=2, s=size)

        @block.sync
        def _(sp):
            sp.dma_start(ident[:], ident_in).then_inc(G["ident_in"], 16)
            sp.dma_start(xres[:, 0, :], x[0, 0:P, :]).then_inc(G["x_in"], 16)
            sp.dma_start(vec[:, 0, :], vecs[0:1, :].to_broadcast([P, D])).then_inc(G["vec0_in"], 16)
            for half, there in ((0, G["half_unit_in"]), (1, landed[0])):
                c = slice(half * UNIT // 2, (half + 1) * UNIT // 2)
                sp.dma_start(raw[:, 0, c], stream[0, :, c]).then_inc(there, 16)
            sp.dma_start(raw[:, 1, :], stream[1]).then_inc(landed[1], 16)
            sp.dma_start(xres[:, 1, :], x[0, P:2 * P, :]).then_inc(G["x_in1"], 16)
            for u in range(2, RAW):
                sp.dma_start(raw[:, u, :], stream[u]).then_inc(landed[u], 16)
            with sp.Fori(1, N_UNITS // RAW) as i:
                for j in range(RAW):
                    sp.wait_ge(G["w_lo_ready"], i * RAW + (j + 1 - RAW))
                    sp.dma_start(raw[:, j, :], stream[i * RAW + j]).then_inc(landed[j], 16)
            for u in range(N_UNITS // RAW * RAW, N_UNITS):
                sp.wait_ge(G["w_lo_ready"], u + 1 - RAW)
                sp.dma_start(raw[:, u % RAW, :], stream[u]).then_inc(landed[u % RAW], 16)
            for t in range(NT):
                sp.wait_ge(G["y_final"], t + 1)
                sp.dma_start(out[0, t * P:(t + 1) * P, :], src[:, t, :]).then_inc(G["out_sent"], 16)
            sp.wait_ge(G["out_sent"], 16 * NT)

        @block.gpsimd
        def _(pool):
            consts = [(mask_raw, masks), (gsel[:], gate_sel), (convw[:], conv_w),
                      (qkw[:], fox_qk), (glaup[:], gla_up), (glab[:], gla_b)]

            def load_vec(v):
                pool.dma_start(vec[:, v % 2, :], vecs[v:v + 1, :].to_broadcast([P, D])).then_inc(
                    vec_landed[v % 2], 16)

            nc.gpsimd.memset(nhalf[:], -0.5).then_inc(G["init"], 1)
            nc.gpsimd.memset(ones[:], 1.0).then_inc(G["init"], 1)
            nc.gpsimd.memset(vaug[:, :, :, MDH:MDH + 1], 1.0).then_inc(G["init"], 1)
            nc.gpsimd.memset(hss[:], 1.0).then_inc(G["init"], 1)
            nc.gpsimd.memset(grow[:], 1.0).then_inc(G["init"], 1)
            pool.dma_start(gw_raw, gate_w).then_inc(G["const"], 16)
            load_vec(1)
            for dst, a in consts:
                pool.dma_start(dst, a).then_inc(G["const"], 16)
            pool.wait_ge(G["init"], 5)
            links = [0]

            def link(ins):
                links[0] += 1
                ins.then_inc(G["pool_chain"], 1)
                pool.wait_ge(G["pool_chain"], links[0])

            def input_rms(k):
                pool.wait_ge(G["sq_ready"], NT * (k + 1))
                link(nc.gpsimd.tensor_scalar(msum[:], ssum[:], 1.0 / D, EPS, ALU.mult, ALU.add))
                nc.gpsimd.tensor_tensor(rms[:], msum[:], nhalf[:, 0:NT], ALU.pow).then_inc(G["rms_ready"], 1)

            def weigh_gate(S, v, half):
                if half == 0:
                    pool.wait_ge(*vec_there(v))
                for t in range(NT):
                    pool.wait_ge(S["og_ready"], NT * half + t + 1)
                    part = og[:, t, half * BANK:(half + 1) * BANK]
                    nc.gpsimd.tensor_tensor(part, part, vec[:, v % 2, half * BANK:(half + 1) * BANK],
                                            ALU.mult).then_inc(S["ogw_ready"], 1)

            def head_rms(S, h, den):
                pool.wait_ge(S["ss_ready"], 2 * (h + 1))
                c = slice(2 * h, 2 * h + 2)
                link(nc.gpsimd.tensor_scalar(hms[:, c], hss[:, c], 1.0 / MDH, EPS, ALU.mult, ALU.add))
                if not den:
                    nc.gpsimd.tensor_tensor(hrr[:, c], hms[:, c], nhalf[:, 0:2], ALU.pow).then_inc(S["rs_ready"], 1)
                    return
                link(nc.gpsimd.tensor_tensor(hrs[:, c], hms[:, c], nhalf[:, 0:2], ALU.pow))
                nc.gpsimd.tensor_tensor(hrr[:, c], hrs[:, c], rden[:, 1, c], ALU.mult).then_inc(S["rs_ready"], 1)

            norm_no = 0
            for n, (kind, j) in enumerate(SUBS):
                input_rms(norm_no)
                norm_no += 1
                if VEC[n] + 2 < N_VEC:
                    pool.wait_ge(G["src_ready"], 4 * STAGE[n] + 4)
                    load_vec(VEC[n] + 2)
                if kind != "F":
                    lay, w = n // 3, GCOLS[kind]
                    pool.wait_ge(G["gw_lo_ready"], DEPTH)
                    link(nc.gpsimd.memset(ht_hi[:, :, :, :].bitcast(F32), 0.0))
                    link(nc.gpsimd.memset(ht_lo[:, :, :, :].bitcast(F32), 0.0))
                    for q, tile in enumerate((ht_hi, ht_lo)):
                        rows4 = tile[:, :, :, :].rearrange("p a b n -> p (a b) n")
                        for r, part in enumerate((gw_hi, gw_lo)):
                            nc.gpsimd.tensor_copy(
                                rows4[:, :, r * w:(r + 1) * w],
                                part[:, lay, 4 * q * w:4 * (q + 1) * w].bitcast(F32).rearrange(
                                    "p (k n) -> p k n", k=4)).then_inc(G["gw_spread"], 1)
                if kind == "A":
                    S = MS[j]
                    pool.wait_ge(S["dec_exp"], 1)
                    for part in (decay[:, :, 0:P], decay[:, :, 2 * P:3 * P]):
                        nc.gpsimd.affine_select(out=part, in_=part, compare_op=ALU.is_ge, fill=0.0, base=0,
                                                pattern=[[0, MH], [1, P]], channel_multiplier=-1).then_inc(
                            S["dec_ready"], 1)
                    weigh_gate(S, VEC[n] + 1, 0)
                    for h in range(3):
                        head_rms(S, h, True)
                    pool.wait_ge(S["ogw_ready"], 4)
                    if VEC[n] + 3 < N_VEC:
                        load_vec(VEC[n] + 3)
                    head_rms(S, 3, True)
                if kind == "B":
                    for m in range(4):
                        pool.wait_ge(FS["red"], 2 * (m + 1))
                        c = slice(8 * m, 8 * m + 8)
                        link(nc.gpsimd.tensor_scalar(hms[:, c], hss[:, c], 1.0 / FDH, EPS, ALU.mult, ALU.add))
                        nc.gpsimd.tensor_tensor(hrs[:, c], hms[:, c], nhalf[:, 0:8], ALU.pow).then_inc(
                            FS["rn_ready"], 1)
                    pool.wait_ge(FS["fb_copied"], 2 * FH)
                    for part, base in ((fbias[:, :, 0:P], 0), (fbias[:, :, 2 * P:3 * P], 0)):
                        nc.gpsimd.affine_select(out=part, in_=part, compare_op=ALU.is_ge, fill=NEG, base=base,
                                                pattern=[[0, FH], [-1, P]], channel_multiplier=1).then_inc(
                            FS["fb_ready"], 1)
                if kind == "C":
                    S = LS
                    pool.wait_ge(G["turned"], 4 * STAGE[n] + 4)
                    link(nc.gpsimd.memset(qs[0], 0.0))
                    link(nc.gpsimd.memset(ks[0], 0.0))
                    link(nc.gpsimd.memset(srcflat[:, :], 0.0))
                    link(nc.gpsimd.memset(amat[:, :, :], 0.0))
                    for lv in range(1, GLA_LEVELS):
                        size = 1 << (lv - 1)
                        if lv == 1:
                            pool.wait_ge(S["qk_ready"], 4)
                        pool.wait_ge(S["e_ready"], lv)
                        if lv >= 3:
                            pool.wait_ge(S["lvl_done"], lv - 1)
                        nc.gpsimd.tensor_tensor(halves(ks[lv % 2], size)[:, :, 0, :],
                                                halves(qkflat[:, 1024:2048], size)[:, :, 0, :],
                                                halves(ebuf[:, lv % 2, :], size)[:, :, 0, :],
                                                ALU.mult).then_inc(S["ks_ready"], 1)
                    for half in range(2):
                        weigh_gate(S, VEC[n] + 1, half)
                    pool.wait_ge(S["ogw_ready"], 4)
                    if VEC[n] + 3 < N_VEC:
                        load_vec(VEC[n] + 3)
                    for h in range(GH):
                        head_rms(S, h, False)
            for t in range(NT):
                pool.wait_ge(G["sq_ready"], NT * norm_no + t + 1)
                c = slice(t, t + 1)
                link(nc.gpsimd.tensor_scalar(msum[:, c], ssum[:, c], 1.0 / D, EPS, ALU.mult, ALU.add))
                nc.gpsimd.tensor_tensor(rms[:, c], msum[:, c], nhalf[:, c], ALU.pow).then_inc(G["rms_ready"], 1)

        @block.scalar
        def _(act):
            def split_hi(u, at=None, used=None):
                if u >= N_UNITS:
                    return
                act.wait_ge(landed[u % RAW], landed_at(u) if at is None else at)
                if u >= SPL:
                    act.wait_ge(G["unit_used"], u - SPL + 1 if used is None else used)
                nc.scalar.activation(w_hi[:, u % SPL, :], raw[:, u % RAW, :], ACT.Copy).then_inc(G["w_hi_ready"], 1)

            def stage_hi(s, groups, some):
                for g in some:
                    t, half, bank = groups[g]
                    act.wait_ge(G["turned"], 4 * s + g + 1)
                    nc.scalar.activation(xt_hi[:, t, 4 * half:4 * half + 4, :],
                                         ps[:, bank, :].rearrange("p (k n) -> p k n", k=4),
                                         ACT.Copy).then_inc(G["xt_hi_ready"], 1)

            def square_rows(s, t):
                act.wait_ge(G["src_ready"], 4 * s + 2 * t + 2)
                nc.scalar.activation(nat[:, t, :, :].rearrange("p t n -> p (t n)"), xres[:, t, :], ACT.Square,
                                     accum_out=ssum[:, t:t + 1]).then_inc(G["sq_ready"], 1)

            def wait_tile(t, chunk, unit):
                if t == 0:
                    act.wait_ge(G["tile0_done"], chunk + 1)
                else:
                    act.wait_ge(G["unit_used"], unit + 1)

            def ffn_chunk(chunk, ua, norms=0):
                for t in range(NT):
                    wait_tile(t, chunk, ua + 1)
                    if norms:
                        act.wait_ge(G["rms_ready"], norms)
                    nc.scalar.activation(silu_g[:, t, :], ps[:, 4 + t, 0:HC], ACT.Silu,
                                         scale=rms[:, t:t + 1]).then_inc(G["silu_ready"], 1)

            def hidden_hi(count):
                act.wait_ge(G["ht_turned"], count)
                nc.scalar.activation(ht_hi[:, :, :, :], ps[:, 6, :].rearrange("p (k t n) -> p k t n", k=2, t=NT),
                                     ACT.Copy).then_inc(G["ht_hi_ready"], 1)

            def ffn(n, j, norm_no):
                u0, c0, h0 = FIRST_UNIT[n], FIRST_CHUNK[n], HT * j
                ffn_chunk(c0, u0, norm_no + 1)
                split_hi(u0 + 3)
                split_hi(u0 + 4)

                def body(i):
                    for b in range(2):
                        ua = u0 + 2 + 3 * b
                        hidden_hi(i * 2 + (h0 + b + 1))
                        for q in range(3):
                            if q == 1:
                                ffn_chunk(i * 2 + (c0 + 1 + b), i * 6 + ua)
                            v = ua + AHEAD + q
                            if not isinstance(i, int):
                                split_hi(v, at=i * 16 + landed_at(v), used=i * 6 + (v - SPL + 1))
                            elif not (b and q == 2):
                                split_hi(6 * i + v)

                with act.Fori(0, LOOPED) as i:
                    body(i)
                body(LOOPED)
                for t in range(NT):
                    act.wait_ge(G["ht_turned"], h0 + NCH + t)
                    if t:
                        act.wait_ge(G["unit_used"], u0 + FFN_UNITS - 1)
                    nc.scalar.activation(ht_hi[:, :, t, :], ps[:, 6 + t, 0:2 * P].rearrange("p (k n) -> p k n", k=2),
                                         ACT.Copy).then_inc(G["ht_hi_ready"], 1)

            def head_square(S, h, den):
                act.wait_ge(S["pv_done"], h + 1)
                if den:
                    act.wait_ge(S["rd_ready"], 3 * (h + 1))
                for t in range(NT):
                    k = 2 * h + t
                    q = k % 6
                    if k >= 6:
                        act.wait_ge(S["ss_ready"], k - 5)
                    nc.scalar.activation(squares[:, q, :], ps[:, HEAD_BANK[h] + t, 0:MDH],
                                         ACT.Square, scale=rden[:, 1, k:k + 1] if den else 1.0,
                                         accum_out=hss[:, k:k + 1]).then_inc(S["ss_ready"], 1)

            def rms_copy(S):
                act.wait_ge(S["rms_turned"], 1)
                nc.scalar.activation(rrows[:, :], ps[0:32, 7, 0:SEQ], ACT.Copy).then_inc(S["rms_rows"], 1)

            def log_sigmoid_part(S, gate_ap, tmp, ready, value):
                act.wait_ge(ready, value)
                nc.scalar.activation(tmp, gate_ap, ACT.Abs).then_inc(S["soft"], 1)
                act.wait_ge(S["soft"], 1)
                nc.scalar.activation(tmp, tmp, ACT.Exp, scale=-1.0).then_inc(S["soft"], 1)
                act.wait_ge(S["soft"], 2)
                nc.scalar.activation(tmp, tmp, ACT.Ln, bias=1.0).then_inc(S["soft"], 1)

            def v_piece(t, m, kind):
                if kind == "B":
                    return vaug[:, t, :, :].rearrange("p h n -> p (h n)")[:, m * BANK:(m + 1) * BANK]
                return vaug[:, t, 2 * m:2 * m + 2, 0:MDH]

            def gate_half(t, m):
                return og[:, t, m * BANK:(m + 1) * BANK]

            def plan_a(n, j):
                S, c0, u0, s = MS[j], FIRST_CHUNK[n], FIRST_UNIT[n], STAGE[n]
                slots = {k: [] for k in range(16)}

                def evac(m):
                    for t in range(NT):
                        evac_tile(m, t)

                def evac_tile(m, t):
                    wait_tile(t, c0 + m, u0 + 2 * m + 1)
                    bank = ps[:, 4 + t, :]
                    r = rms[:, t:t + 1]
                    if m < 4:
                        nc.scalar.activation(nat[:, m % 2, t, :], bank, ACT.Copy, scale=r).then_inc(
                            S["nat_ready"], 1)
                    elif m < 6:
                        nc.scalar.activation(v_piece(t, m - 4, "A"), bank.rearrange("p (h n) -> p h n", h=2),
                                             ACT.Copy, scale=r).then_inc(S["v_ready"], 1)
                    else:
                        if m == 6 and t == 0:
                            act.wait_ge(S["turned"], 4)
                        nc.scalar.activation(gate_half(t, m - 6), bank, ACT.Sigmoid, scale=r).then_inc(
                            S["og_ready"], 1)

                def first_tap(m):
                    act.wait_ge(S["turned"], m + 1)
                    for c in range(4):
                        ct = 4 * m + c
                        nc.scalar.activation(qkt[:, ct, :], ps[:, 2 * (m % 2) + c // 2, (c % 2) * SEQ:(c % 2 + 1) * SEQ],
                                             ACT.Copy, scale=convw[:, j, ct, 3:4]).then_inc(S["tap0"], 1)

                def conv_silu(m):
                    act.wait_ge(S["taps"], 12 * (m + 1))
                    part = qkt[:, 4 * m:4 * m + 4, :]
                    nc.scalar.activation(part, part, ACT.Silu).then_inc(S["conv_ready"], 1)

                def soft():
                    log_sigmoid_part(S, ps[0:MH, 7, SEQ:2 * SEQ], rowbuf[0:MH, 0, :], S["gates_turned"], 1)

                def en():
                    act.wait_ge(S["rows"], 5)
                    nc.scalar.activation(rowbuf[0:MH, 5, :], rowbuf[0:MH, 5, :], ACT.Exp, scale=-1.0).then_inc(
                        S["en_ready"], 1)

                def cols_copy():
                    act.wait_ge(S["cols_turned"], 1)
                    nc.scalar.activation(cols[:, :, 0:8], ps[:, 6, 0:16].rearrange("p (a n) -> p a n", a=2),
                                         ACT.Copy).then_inc(S["cols_ready"], 1)

                def dec_exp():
                    act.wait_ge(S["dec_arg"], 8)
                    nc.scalar.activation(decay[:, :, :], decay[:, :, :], ACT.Exp, scale=-1.0).then_inc(S["dec_exp"], 1)

                for m in range(7):
                    slots[2 * m + 1].append(lambda m=m: evac(m))
                for k in (3, 5, 7):
                    slots[k].append(None)
                for m in range(4):
                    slots[2 * m + 2].append(lambda m=m: first_tap(m))
                slots[5] += [en, lambda: conv_silu(0)]
                for m in range(1, 4):
                    slots[2 * m + 3].append(lambda m=m: conv_silu(m))
                slots[1].append(lambda: rms_copy(S))
                slots[3].append(soft)
                slots[6].append(cols_copy)
                slots[9] += [None, dec_exp]
                for k in (2, 4, 6, 8):
                    slots[k].insert(0, None)
                for h in range(3):
                    slots[13].append(lambda h=h: head_square(S, h, True))
                slots[15] = [lambda: evac_tile(7, 0), lambda: stage_hi(s + 1, MIX_GROUPS["A"], (0, 1)),
                             lambda: evac_tile(7, 1), None, lambda: head_square(S, 3, True),
                             lambda: stage_hi(s + 1, MIX_GROUPS["A"], (2, 3))]
                return slots

            def plan_b(n, j):
                S, c0, u0, s = FS, FIRST_CHUNK[n], FIRST_UNIT[n], STAGE[n]
                slots = {k: [] for k in range(16)}

                def evac(m):
                    for t in range(NT):
                        evac_tile(m, t)

                def evac_tile(m, t):
                    wait_tile(t, c0 + m, u0 + 2 * m + 1)
                    bank = ps[:, 4 + t, :]
                    r = rms[:, t:t + 1]
                    if m < 4:
                        nc.scalar.activation(nat[:, m % 2, t, :], bank, ACT.Copy, scale=r).then_inc(
                            S["nat_ready"], 1)
                    elif m < 6:
                        nc.scalar.activation(v_piece(t, m - 4, "B"), bank, ACT.Copy, scale=r).then_inc(
                            S["v_ready"], 1)
                    else:
                        if m == 6 and t == 0:
                            act.wait_ge(S["turned"], 4)
                        nc.scalar.activation(gate_half(t, m - 6), bank, ACT.Sigmoid, scale=r).then_inc(
                            S["og_ready"], 1)

                def qk_evac(m):
                    act.wait_ge(S["turned"], m + 1)
                    for b in range(2):
                        nc.scalar.activation(qkt[:, 4 * m + 2 * b:4 * m + 2 * b + 2, :],
                                             ps[:, 2 * (m % 2) + b, :].rearrange("p (h n) -> p h n", h=2),
                                             ACT.Copy, scale=qkw[:, m // 2:m // 2 + 1]).then_inc(S["qk_ready"], 1)

                def soft():
                    log_sigmoid_part(S, ps[0:FH, 7, 0:SEQ], zbuf[0:FH, 0, 0:SEQ], S["gates_turned"], 1)

                def cols_copy():
                    act.wait_ge(S["cols_turned"], 1)
                    nc.scalar.activation(cols[:, 0, :], ps[:, 7, 0:16], ACT.Copy).then_inc(S["cols_ready"], 1)

                def fb_copy(q):
                    act.wait_ge(S["fb_done"], q + 1)
                    if q == 0:
                        act.wait_ge(S["cols_ready"], 1)
                    for h in (2 * q, 2 * q + 1):
                        row = ps[:, 6 + q % 2, (h % 2) * SEQ:(h % 2 + 1) * SEQ]
                        nc.scalar.activation(fbias[:, h, 0:P], row[:, 0:P], ACT.Identity, scale=-1.0,
                                             bias=cols[:, 0, h:h + 1]).then_inc(S["fb_copied"], 1)
                        nc.scalar.activation(fbias[:, h, P:3 * P], row, ACT.Identity, scale=-1.0,
                                             bias=cols[:, 0, FH + h:FH + h + 1]).then_inc(S["fb_copied"], 1)

                def exps(h):
                    act.wait_ge(S["max_ready"], 2 * (h + 1))
                    for t, c in ((0, slice(0, P)), (1, slice(P, 3 * P))):
                        nc.scalar.activation(zbuf[:, h % 2, c], zbuf[:, h % 2, c], ACT.Exp,
                                             bias=rowmax[:, t, h:h + 1],
                                             accum_out=rowsum[:, t, h:h + 1]).then_inc(S["p_ready"], 1)

                def pt_copy(h):
                    act.wait_ge(S["p_turned"], h + 1)
                    if h >= 2:
                        act.wait_ge(S["pv_done"], h - 1)
                    nc.scalar.activation(ptbuf[:, h % 2, :], ps[:, 2 + h % 2, 0:3 * P], ACT.Copy).then_inc(
                        S["pt_ready"], 1)

                for m in range(7):
                    slots[2 * m + 1].append(lambda m=m: evac(m))
                for m in range(4):
                    slots[2 * m + 3].append(lambda m=m: qk_evac(m))
                slots[1].append(lambda: rms_copy(S))
                slots[2] += [None, soft]
                slots[4].append(cols_copy)
                for q in range(4):
                    slots[4 + q].append(lambda q=q: fb_copy(q))
                for k in range(4):
                    slots[10 + k] += [lambda h=2 * k: exps(h), lambda h=2 * k + 1: exps(h)]
                    slots[11 + k] += [lambda h=2 * k: pt_copy(h), lambda h=2 * k + 1: pt_copy(h)]
                slots[15] = [lambda: evac_tile(7, 0), lambda: stage_hi(s + 1, MIX_GROUPS["B"], (0, 1)),
                             lambda: evac_tile(7, 1), None, lambda: stage_hi(s + 1, MIX_GROUPS["B"], (2, 3))]
                return slots

            def plan_c(n, j):
                S, c0, u0, s = LS, FIRST_CHUNK[n], FIRST_UNIT[n], STAGE[n]
                slots = {k: [] for k in range(12)}

                def evac(m):
                    for t in range(NT):
                        evac_tile(m, t)

                def evac_tile(m, t):
                    wait_tile(t, c0 + m, u0 + 2 * m + 1)
                    bank = ps[:, 4 + t, :]
                    r = rms[:, t:t + 1]
                    if m < 2:
                        nc.scalar.activation(nat[:, m % 2, t, :], bank, ACT.Copy, scale=r).then_inc(
                            S["nat_ready"], 1)
                    elif m < 4:
                        nc.scalar.activation(v_piece(t, m - 2, "C"), bank.rearrange("p (h n) -> p h n", h=2),
                                             ACT.Copy, scale=r).then_inc(S["v_ready"], 1)
                    else:
                        nc.scalar.activation(gate_half(t, m - 4), bank, ACT.Silu, scale=r).then_inc(
                            S["og_ready"], 1)

                def qk_evac(m):
                    act.wait_ge(S["turned"], m + 1)
                    for b in range(2):
                        nc.scalar.activation(qkt[:, 4 * m + 2 * b:4 * m + 2 * b + 2, :],
                                             ps[:, 2 * m + b, :].rearrange("p (h n) -> p h n", h=2),
                                             ACT.Copy, scale=(GDK ** -0.5 if m == 0 else 1.0)).then_inc(
                            S["qk_ready"], 1)

                def glr_copy():
                    act.wait_ge(S["gates_turned"], 1)
                    nc.scalar.activation(glrt, ps[0:GRANK, 7, 0:SEQ], ACT.Copy).then_inc(S["glrt_ready"], 1)

                def z_bias():
                    act.wait_ge(S["z_done"], 1)
                    for h in range(GH):
                        nc.scalar.activation(ebuf[:, 1, h * SEQ:(h + 1) * SEQ],
                                             ps[:, 6 + h // 2, (h % 2) * SEQ:(h % 2 + 1) * SEQ], ACT.Identity,
                                             bias=glab[:, h:h + 1]).then_inc(S["z_ready"], 1)

                def soft():
                    log_sigmoid_part(S, ebuf[:, 1, :], ebuf[:, 0, :], S["z_ready"], GH)

                def decay_exp(lv):
                    act.wait_ge(S["diff_ready"], 2 * lv)
                    nc.scalar.activation(ebuf[:, lv % 2, :], ebuf[:, lv % 2, :], ACT.Exp,
                                         scale=1.0 / GTAU).then_inc(S["e_ready"], 1)

                def across_copy():
                    act.wait_ge(S["lvl_done"], GLA_LEVELS)
                    nc.scalar.activation(across[:, :, :], ps[:, 0, :].rearrange("p (h n) -> p h n", h=GH),
                                         ACT.Copy).then_inc(S["ax_ready"], 1)

                for m in range(6):
                    slots[2 * m + 1].append(lambda m=m: evac(m))
                for m in range(2):
                    slots[2 * m + 2].append(lambda m=m: qk_evac(m))
                slots[1].append(lambda: rms_copy(S))
                slots[2].append(glr_copy)
                slots[3] += [None, z_bias, soft]
                for lv in range(1, GLA_LEVELS):
                    slots[GLA_PE[lv] - 1].append(lambda lv=lv: decay_exp(lv))
                slots[2].insert(0, None)
                slots[11] = [lambda: evac_tile(5, 0), across_copy, lambda: evac_tile(5, 1)]
                for h in range(3):
                    slots[11].append(lambda h=h: head_square(S, h, False))
                slots[11] += [lambda: stage_hi(s + 1, MIX_GROUPS["C"], (0, 1)), lambda: head_square(S, 3, False),
                              None, lambda: stage_hi(s + 1, MIX_GROUPS["C"], (2, 3))]
                return slots

            def first_unit_hi(there, c, done):
                act.wait_ge(there, 16)
                nc.scalar.activation(w_hi[:, 0, c], raw[:, 0, c], ACT.Copy).then_inc(done, 1)

            def gate_weights():
                act.wait_ge(G["const"], 16 * 7)
                for lay in range(DEPTH):
                    width = KT * GCOLS[KINDS[lay % 3]]
                    nc.scalar.activation(gw_hi[:, lay, 0:width], gw_raw[:, lay, 0:width], ACT.Copy).then_inc(
                        G["gw_hi_ready"], 1)

            for n, (kind, j) in enumerate(SUBS):
                s, u0 = STAGE[n], FIRST_UNIT[n]
                if n == 0:
                    first_unit_hi(G["half_unit_in"], slice(0, UNIT // 2), G["w_hi_half"])
                stage_hi(s, NORM_GROUPS, (0,))
                if n == 0:
                    first_unit_hi(landed[0], slice(UNIT // 2, UNIT), G["w_hi_ready"])
                stage_hi(s, NORM_GROUPS, (1,))
                split_hi(u0 + 1)
                square_rows(s, 0)
                stage_hi(s, NORM_GROUPS, (2,))
                square_rows(s, 1)
                stage_hi(s, NORM_GROUPS, (3,))
                split_hi(u0 + 2)
                if kind == "F":
                    ffn(n, j, n)
                    if n == 0:
                        gate_weights()
                    continue
                act.wait_ge(G["rms_ready"], n + 1)
                slots = {"A": plan_a, "B": plan_b, "C": plan_c}[kind](n, j)
                pu = PROJ_UNITS[kind]
                for k in range(pu):
                    if None not in slots[k]:
                        slots[k].append(None)
                    for step in slots[k]:
                        if step:
                            step()
                        else:
                            split_hi(u0 + k + AHEAD)
                for k in range(OUT_UNITS - 2):
                    split_hi(u0 + pu + k + AHEAD)
            for t in range(NT):
                square_rows(N_STAGE, t)

        @block.vector
        def _(dve):
            def split_lo(u, count=None):
                if u >= N_UNITS:
                    return
                dve.wait_ge(G["w_hi_ready"], u + 1 if count is None else count)
                nc.vector.tensor_tensor(w_lo[:, u % SPL, :], raw[:, u % RAW, :], w_hi[:, u % SPL, :].bitcast(F32),
                                        ALU.subtract).then_inc(G["w_lo_ready"], 1)

            def split_lo_halves(u):
                dve.wait_ge(G["w_hi_ready"], u + 1)
                for half, done in ((0, G["w_lo_half"]), (1, G["w_lo_ready"])):
                    c = slice(half * UNIT // 2, (half + 1) * UNIT // 2)
                    nc.vector.tensor_tensor(w_lo[:, u % SPL, c], raw[:, u % RAW, c], w_hi[:, u % SPL, c].bitcast(F32),
                                            ALU.subtract).then_inc(done, 1)

            def stage_lo(s, groups, some):
                for g in some:
                    t, half, bank = groups[g]
                    dve.wait_ge(G["xt_hi_ready"], 4 * s + g + 1)
                    nc.vector.tensor_tensor(xt_lo[:, t, 4 * half:4 * half + 4, :],
                                            ps[:, bank, :].rearrange("p (k n) -> p k n", k=4),
                                            xt_hi[:, t, 4 * half:4 * half + 4, :].bitcast(F32),
                                            ALU.subtract).then_inc(G["xt_lo_ready"], 1)

            def new_x(n, t, half):
                if t and half:
                    dve.wait_ge(G["unit_used"], FIRST_UNIT[n] if n < len(SUBS) else N_UNITS)
                else:
                    dve.wait_ge(G["acc_done"], 3 * (n - 1) + 2 * t + half + 1)
                scale = 0.5 if SUBS[n - 1][0] == "F" else 1.0
                part = xres[:, t, half * BANK:(half + 1) * BANK]
                nc.vector.scalar_tensor_tensor(out=part, in0=ps[:, 2 * t + half, :], scalar=scale, in1=part,
                                               op0=ALU.mult, op1=ALU.add).then_inc(G["x_new"], 1)

            def weigh_x(n, t, half):
                v = VEC[n]
                if t + half == 0:
                    dve.wait_ge(*vec_there(v))
                c = slice(half * BANK, (half + 1) * BANK)
                if n == 0:
                    dve.wait_ge(G["x_in1"] if t else G["x_in"], 16)
                else:
                    dve.wait_ge(G["x_new"], 4 * (n - 1) + 2 * t + half + 1)
                nc.vector.tensor_tensor(src[:, t, c], xres[:, t, c], vec[:, v % 2, c], ALU.mult).then_inc(
                    G["src_ready"], 1)

            def hidden(count):
                for t in range(NT):
                    dve.wait_ge(G["silu_ready"], count + (t + 1))
                    nc.vector.scalar_tensor_tensor(out=hid[:, t, :], in0=ps[:, 4 + t, HC:2 * HC],
                                                   scalar=rms[:, t:t + 1], in1=silu_g[:, t, :],
                                                   op0=ALU.mult, op1=ALU.mult).then_inc(G["hid_ready"], 1)

            def hidden_lo(count):
                dve.wait_ge(G["ht_hi_ready"], count)
                nc.vector.tensor_tensor(ht_lo[:, :, :, :], ps[:, 6, :].rearrange("p (k t n) -> p k t n", k=2, t=NT),
                                        ht_hi[:, :, :, :].bitcast(F32), ALU.subtract).then_inc(G["ht_lo_ready"], 1)

            def ffn(n, j):
                u0, h0, hid0 = FIRST_UNIT[n], HT * j, NT * NCH * j
                hidden(hid0)
                split_lo(u0 + 3)
                split_lo(u0 + 4)

                def body(i):
                    for b in range(2):
                        ua = u0 + 2 + 3 * b
                        hidden_lo(i * 2 + (h0 + b + 1))
                        for q in range(3):
                            if q == 1:
                                hidden(i * 4 + (hid0 + 2 + 2 * b))
                            v = ua + AHEAD + q
                            if not isinstance(i, int):
                                split_lo(v, count=i * 6 + (v + 1))
                            elif not (b and q == 2):
                                split_lo(6 * i + v)

                with dve.Fori(0, LOOPED) as i:
                    body(i)
                body(LOOPED)
                for t in range(NT):
                    dve.wait_ge(G["ht_hi_ready"], h0 + NCH + t)
                    nc.vector.tensor_tensor(ht_lo[:, :, t, :], ps[:, 6 + t, 0:2 * P].rearrange("p (k n) -> p k n", k=2),
                                            ht_hi[:, :, t, :].bitcast(F32), ALU.subtract).then_inc(
                        G["ht_lo_ready"], 1)

            def weigh_gate(S, v):
                dve.wait_ge(*vec_there(v))
                for t in range(NT):
                    dve.wait_ge(S["og_ready"], NT + t + 1)
                    dve.wait_ge(S["ogw_ready"], NT + t)
                    part = og[:, t, BANK:2 * BANK]
                    nc.vector.tensor_tensor(part, part, vec[:, v % 2, BANK:2 * BANK], ALU.mult).then_inc(
                        S["ogw_ready"], 1)

            def head_out(S, s, h, den):
                dve.wait_ge(S["rs_ready"], h + 1)
                for t in range(NT):
                    dve.wait_ge(S["ogw_ready"], NT * (h // 2) + t + 1)
                    ins = nc.vector.scalar_tensor_tensor(
                        out=src[:, t, h * MDH:(h + 1) * MDH], in0=ps[:, HEAD_BANK[h] + t, 0:MDH],
                        scalar=hrr[:, 2 * h + t:2 * h + t + 1], in1=og[:, t, h * MDH:(h + 1) * MDH],
                        op0=ALU.mult, op1=ALU.mult)
                    ins.then_inc(G["src_ready"] if h % 2 else S["y_done"], 1)

            def scale_gates(S, width):
                dve.wait_ge(S["gate_mm"], 1)
                dve.wait_ge(S["rms_rows"], 1)
                nc.vector.tensor_tensor(grow[0:2 * width, :], ps[0:2 * width, 6, 0:SEQ], rrows[0:2 * width, :],
                                        ALU.mult).then_inc(S["gates_ready"], 1)

            def plan_a(n, j):
                S, s = MS[j], STAGE[n]
                slots = {k: [] for k in range(16)}

                def rows():
                    f, i = ps[0:MH, 7, SEQ:2 * SEQ], ps[0:MH, 7, 0:SEQ]
                    r = [rowbuf[0:MH, k, :] for k in range(6)]
                    dve.wait_ge(S["soft"], 3)
                    nc.vector.scalar_tensor_tensor(out=r[1], in0=f, scalar=0.0, in1=r[0], op0=ALU.min,
                                                   op1=ALU.subtract).then_inc(S["rows"], 1)
                    dve.wait_ge(S["rows"], 1)
                    nc.vector.tensor_tensor_scan(r[2], ones[0:MH, :], r[1], 0.0, ALU.mult, ALU.add).then_inc(
                        S["rows"], 1)
                    dve.wait_ge(S["rows"], 2)
                    nc.vector.tensor_tensor(r[3], i, r[2], ALU.subtract).then_inc(S["rows"], 1)
                    dve.wait_ge(S["rows"], 3)
                    nc.vector.tensor_tensor_scan(r[4], ones[0:MH, :], r[3], 0.0, ALU.mult, ALU.max).then_inc(
                        S["rows"], 1)
                    dve.wait_ge(S["rows"], 4)
                    nc.vector.tensor_tensor(r[5], r[2], r[4], ALU.add).then_inc(S["rows"], 1)

                def taps(m):
                    for tap in range(1, 4):
                        for c in range(4):
                            ct = 4 * m + c
                            if tap == 1:
                                dve.wait_ge(S["tap0"], 4 * m + 2 * (c // 2) + 2)
                            elif c == 0:
                                dve.wait_ge(S["taps"], 12 * m + 4 * (tap - 1))
                            bank = ps[:, 2 * (m % 2) + c // 2, (c % 2) * SEQ:(c % 2 + 1) * SEQ]
                            nc.vector.scalar_tensor_tensor(out=qkt[:, ct, tap:SEQ], in0=bank[:, 0:SEQ - tap],
                                                           scalar=convw[:, j, ct, 3 - tap:4 - tap],
                                                           in1=qkt[:, ct, tap:SEQ], op0=ALU.mult,
                                                           op1=ALU.add).then_inc(S["taps"], 1)

                def decay_args():
                    dve.wait_ge(S["cols_ready"], 1)
                    dve.wait_ge(S["mb_done"], 1)
                    for h in range(MH):
                        row = ps[:, 6 + h // 2, (h % 2) * SEQ:(h % 2 + 1) * SEQ]
                        for t, c, r in ((0, slice(0, SEQ), row), (1, slice(SEQ, SEQ + P), row[:, P:SEQ])):
                            a = cols[:, 0, 4 * t + h:4 * t + h + 1]
                            nc.vector.tensor_scalar(decay[:, h, c], r, a, a, ALU.max, ALU.subtract).then_inc(
                                S["dec_arg"], 1)

                def pm(h):
                    dve.wait_ge(S["s_done"], h + 1)
                    if h == 0:
                        dve.wait_ge(S["dec_ready"], 2)
                    nc.vector.scalar_tensor_tensor(out=probs[:, h, :], in0=ps[:, h, 0:3 * P],
                                                   scalar=MDH ** -0.5, in1=decay[:, h, :],
                                                   op0=ALU.mult, op1=ALU.mult).then_inc(S["pm_ready"], 1)

                def dens(h):
                    dve.wait_ge(S["pv_done"], h + 1)
                    c = slice(2 * h, 2 * h + 2)
                    den = ps[:, HEAD_BANK[h]:HEAD_BANK[h] + 2, MDH]
                    guard = cols[:, 1, 0:8].rearrange("p (t h) -> p h t", t=2)[:, h, :]
                    nc.vector.scalar_tensor_tensor(out=rden[:, 0, c], in0=den, scalar=-1.0, in1=guard,
                                                   op0=ALU.mult, op1=ALU.max).then_inc(S["rd_ready"], 1)
                    dve.wait_ge(S["rd_ready"], 3 * h + 1)
                    nc.vector.tensor_tensor(rden[:, 0, c], den, rden[:, 0, c], ALU.max).then_inc(S["rd_ready"], 1)
                    dve.wait_ge(S["rd_ready"], 3 * h + 2)
                    nc.vector.reciprocal(rden[:, 1, c], rden[:, 0, c]).then_inc(S["rd_ready"], 1)

                slots[1].append(lambda: scale_gates(S, 8))
                slots[3] += [None, rows]
                slots[7] += [None, decay_args]
                for m in range(4):
                    slots[2 * m + 2].append(lambda m=m: taps(m))
                for h in range(MH):
                    slots[11].append(lambda h=h: pm(h))
                for h in range(3):
                    slots[13].append(lambda h=h: dens(h))
                for k in (2, 4, 6, 8):
                    slots[k].insert(0, None)
                for h in range(2):
                    slots[14].append(lambda h=h: head_out(S, s, h, True))
                slots[15] = [lambda: stage_lo(s + 1, MIX_GROUPS["A"], (0, 1)), lambda: weigh_gate(S, VEC[n] + 1),
                             lambda: head_out(S, s, 2, True), None, lambda: dens(3), lambda: head_out(S, s, 3, True),
                             lambda: stage_lo(s + 1, MIX_GROUPS["A"], (2, 3))]
                return slots

            def plan_b(n, j):
                S, s = FS, STAGE[n]
                slots = {k: [] for k in range(16)}

                def rows():
                    dve.wait_ge(S["soft"], 3)
                    nc.vector.scalar_tensor_tensor(out=ptbuf[0:FH, 0, 0:SEQ], in0=ps[0:FH, 7, 0:SEQ], scalar=0.0,
                                                   in1=zbuf[0:FH, 0, 0:SEQ], op0=ALU.min,
                                                   op1=ALU.subtract).then_inc(S["rows"], 1)
                    dve.wait_ge(S["rows"], 1)
                    nc.vector.tensor_tensor_scan(ptbuf[0:FH, 1, 0:SEQ], ones[0:FH, :], ptbuf[0:FH, 0, 0:SEQ], 0.0,
                                                 ALU.mult, ALU.add).then_inc(S["rows"], 1)

                def square(m):
                    for t in range(NT):
                        dve.wait_ge(S["nat_ready"], 2 * m + t + 1)
                        if m == 0 and t == 0:
                            dve.wait_ge(G["turned"], 4 * s + 4)
                        if 2 * m + t >= 2:
                            dve.wait_ge(S["red"], 2 * m + t - 1)
                        part = nat[:, m % 2, t, :]
                        nc.vector.tensor_tensor(src[:, t, 0:BANK], part, part, ALU.mult).then_inc(S["sq"], 1)
                    for t in range(NT):
                        dve.wait_ge(S["sq"], 2 * m + t + 1)
                        nc.vector.tensor_reduce(hss[:, 8 * m + 4 * t:8 * m + 4 * t + 4],
                                                src[:, t, 0:BANK].rearrange("p (h n) -> p h n", h=4), AX.X,
                                                ALU.add).then_inc(S["red"], 1)

                def normed(m):
                    dve.wait_ge(S["rn_ready"], m + 1)
                    for t in range(NT):
                        part = nat[:, m % 2, t, :].rearrange("p (h n) -> p h n", h=4)
                        r = hrs[:, 8 * m + 4 * t:8 * m + 4 * t + 4].unsqueeze(2).to_broadcast([P, 4, FDH])
                        nc.vector.tensor_tensor(part, part, r, ALU.mult).then_inc(S["natn_ready"], 1)

                def logits(h):
                    dve.wait_ge(S["s_done"], h + 1)
                    if h == 0:
                        dve.wait_ge(S["fb_ready"], 2)
                    nc.vector.scalar_tensor_tensor(out=zbuf[:, h % 2, :], in0=ps[:, h % 2, 0:3 * P],
                                                   scalar=FDH ** -0.5, in1=fbias[:, h, :], op0=ALU.mult,
                                                   op1=ALU.add).then_inc(S["z_ready"], 1)
                    dve.wait_ge(S["z_ready"], h + 1)
                    for t, c in ((0, slice(0, P)), (1, slice(P, 3 * P))):
                        nc.vector.tensor_reduce(rowmax[:, t, h:h + 1], zbuf[:, h % 2, c], AX.X, ALU.max,
                                                negate=True).then_inc(S["max_ready"], 1)

                def inverses(h):
                    dve.wait_ge(S["p_ready"], 2 * (h + 1))
                    nc.vector.reciprocal(rrow[:, :, h:h + 1], rowsum[:, :, h:h + 1]).then_inc(S["sum_inv"], 1)

                def outs(h):
                    dve.wait_ge(S["pv_done"], h // 2 * 2 + 2)
                    dve.wait_ge(S["sum_inv"], h + 1)
                    for t in range(NT):
                        dve.wait_ge(S["og_ready"], NT * (h // 4) + t + 1)
                        c = slice(h * FDH, (h + 1) * FDH)
                        q = (h % 2) * SEQ + t * P
                        ins = nc.vector.scalar_tensor_tensor(
                            out=src[:, t, c], in0=ps[:, 6 + (h // 2) % 2, q:q + P],
                            scalar=rrow[:, t, h:h + 1], in1=og[:, t, c], op0=ALU.mult, op1=ALU.mult)
                        ins.then_inc(G["src_ready"] if h % 4 == 3 else S["y_done"], 1)

                for m in range(4):
                    slots[2 * m + 1].append(lambda m=m: square(m))
                    slots[2 * m + 2].append(lambda m=m: normed(m))
                slots[1].append(lambda: scale_gates(S, 8))
                slots[2] += [None, rows]
                for k in range(4):
                    slots[10 + k] += [lambda h=2 * k: logits(h), lambda h=2 * k + 1: logits(h)]
                    slots[11 + k] += [lambda h=2 * k: inverses(h), lambda h=2 * k + 1: inverses(h)]
                for h in range(4):
                    slots[13].append(lambda h=h: outs(h))
                slots[15] = [lambda: stage_lo(s + 1, MIX_GROUPS["B"], (0, 1)), lambda: outs(4), lambda: outs(5),
                             None, lambda: outs(6), lambda: outs(7),
                             lambda: stage_lo(s + 1, MIX_GROUPS["B"], (2, 3))]
                return slots

            def plan_c(n, j):
                S, s = LS, STAGE[n]
                slots = {k: [] for k in range(12)}

                def rows():
                    dve.wait_ge(S["soft"], 3)
                    nc.vector.scalar_tensor_tensor(out=ebuf[:, 0, :], in0=ebuf[:, 1, :], scalar=0.0,
                                                   in1=ebuf[:, 0, :], op0=ALU.min,
                                                   op1=ALU.subtract).then_inc(S["rows"], 1)
                    dve.wait_ge(S["rows"], 1)
                    for h in range(GH):
                        c = slice(h * SEQ, (h + 1) * SEQ)
                        nc.vector.tensor_tensor_scan(gcum[:, c], ones[:, :], ebuf[:, 0, c], 0.0, ALU.mult,
                                                     ALU.add).then_inc(S["rows"], 1)

                def diff(lv):
                    size = 1 << (lv - 1)
                    g = halves(gcum, size)
                    e = halves(ebuf[:, lv % 2, :], size)
                    ref = g[:, :, 0, size - 1:size].to_broadcast([P, 512 // size, size])
                    if lv == 1:
                        dve.wait_ge(S["rows"], 1 + GH)
                    if lv >= 3:
                        dve.wait_ge(S["ks_ready"], lv - 2)
                        dve.wait_ge(S["qs_ready"], lv - 2)
                    nc.vector.tensor_tensor(e[:, :, 1, :], g[:, :, 1, :], ref, ALU.subtract).then_inc(
                        S["diff_ready"], 1)
                    nc.vector.tensor_tensor(e[:, :, 0, :], ref, g[:, :, 0, :], ALU.subtract).then_inc(
                        S["diff_ready"], 1)

                def queries(lv):
                    size = 1 << (lv - 1)
                    dve.wait_ge(S["e_ready"], lv)
                    if lv == 1:
                        dve.wait_ge(S["qk_ready"], 4)
                        dve.wait_ge(S["ks_ready"], 1)
                    if lv >= 3:
                        dve.wait_ge(S["lvl_done"], lv - 1)
                    nc.vector.tensor_tensor(halves(qs[lv % 2], size)[:, :, 1, :],
                                            halves(qkflat[:, 0:1024], size)[:, :, 1, :],
                                            halves(ebuf[:, lv % 2, :], size)[:, :, 1, :],
                                            ALU.mult).then_inc(S["qs_ready"], 1)

                def gather(lv):
                    dve.wait_ge(S["lvl_done"], lv + 1)
                    if lv == 0:
                        dve.wait_ge(S["ks_ready"], 1)
                    else:
                        dve.wait_ge(S["a_ready"], lv)
                    b = 2 * (lv % 2)
                    nc.vector.copy_predicated(amat[:, :, :],
                                              lvl_mask[:, lv:lv + 1, :].to_broadcast([P, 8, P]),
                                              ps[:, b:b + 2, :].rearrange("p b (m n) -> p (b m) n", n=P)).then_inc(
                        S["a_ready"], 1)

                slots[1].append(lambda: scale_gates(S, GRANK))
                slots[4] += [None, rows]
                slots[5].append(lambda: diff(1))
                for lv in range(1, GLA_LEVELS):
                    k = GLA_PE[lv] - 1
                    if lv + 1 < GLA_LEVELS:
                        slots[k].append(lambda lv=lv: diff(lv + 1))
                    slots[k].append(lambda lv=lv: queries(lv))
                for lv in range(GLA_LEVELS - 1):
                    slots[GLA_PE[lv]].append(lambda lv=lv: gather(lv))
                slots[11] += [lambda: head_out(S, s, 0, False), lambda: head_out(S, s, 1, False),
                              lambda: stage_lo(s + 1, MIX_GROUPS["C"], (0, 1)), lambda: head_out(S, s, 2, False),
                              None, lambda: head_out(S, s, 3, False),
                              lambda: stage_lo(s + 1, MIX_GROUPS["C"], (2, 3))]
                return slots

            def gate_weights():
                dve.wait_ge(G["const"], 16 * 7)
                nc.vector.tensor_copy(lvl_mask[:], mask_raw)
                for lay in range(DEPTH):
                    width = KT * GCOLS[KINDS[lay % 3]]
                    dve.wait_ge(G["gw_hi_ready"], lay + 1)
                    nc.vector.tensor_tensor(gw_lo[:, lay, 0:width], gw_raw[:, lay, 0:width],
                                            gw_hi[:, lay, 0:width].bitcast(F32), ALU.subtract).then_inc(
                        G["gw_lo_ready"], 1)

            def first_unit_lo(there, c, done):
                dve.wait_ge(there, 1)
                nc.vector.tensor_tensor(w_lo[:, 0, c], raw[:, 0, c], w_hi[:, 0, c].bitcast(F32),
                                        ALU.subtract).then_inc(done, 1)

            for n, (kind, j) in enumerate(SUBS):
                s, u0 = STAGE[n], FIRST_UNIT[n]

                def piece(t, half):
                    if n:
                        new_x(n, t, half)
                    weigh_x(n, t, half)

                piece(0, 0)
                piece(0, 1)
                if n == 0:
                    first_unit_lo(G["w_hi_half"], slice(0, UNIT // 2), G["w_lo_half"])
                stage_lo(s, NORM_GROUPS, (0,))
                if n == 0:
                    first_unit_lo(G["w_hi_ready"], slice(UNIT // 2, UNIT), G["w_lo_ready"])
                    dve.wait_ge(G["init"], 5)
                stage_lo(s, NORM_GROUPS, (1,))
                piece(1, 0)
                split_lo_halves(u0 + 1)
                piece(1, 1)
                stage_lo(s, NORM_GROUPS, (2, 3))
                split_lo(u0 + 2)
                if kind == "F":
                    ffn(n, j)
                    if n == 0:
                        gate_weights()
                    continue
                pu = PROJ_UNITS[kind]
                slots = {"A": plan_a, "B": plan_b, "C": plan_c}[kind](n, j)
                for k in range(pu):
                    if None not in slots[k]:
                        slots[k].append(None)
                    for step in slots[k]:
                        if step:
                            step()
                        else:
                            split_lo(u0 + k + AHEAD)
                for k in range(OUT_UNITS - 2):
                    split_lo(u0 + pu + k + AHEAD)
            n, v = len(SUBS), N_VEC - 1
            for t in range(NT):
                for half in range(2):
                    new_x(n, t, half)
                dve.wait_ge(G["x_new"], 4 * (n - 1) + 2 * t + 2)
                nc.vector.tensor_copy(rrow[:, 0, t:t + 1], xres[:, t, 0:1]).then_inc(G["src_ready"], 2)
            dve.wait_ge(*vec_there(v))
            for t in range(NT):
                dve.wait_ge(G["rms_ready"], n + 1 + t)
                nc.vector.scalar_tensor_tensor(out=src[:, t, :], in0=xres[:, t, :], scalar=rms[:, t:t + 1],
                                               in1=vec[:, v % 2, :], op0=ALU.mult, op1=ALU.mult).then_inc(
                    G["y_final"], 1)

        @block.tensor
        def _(pe):
            def three(dst, a_hi, a_lo, slot, c, first, last):
                w = slice(c, c + BANK)
                nc.tensor.matmul(dst, a_hi, w_hi[:, slot, w], start=first, stop=False)
                nc.tensor.matmul(dst, a_hi, w_lo[:, slot, w], start=False, stop=False)
                return nc.tensor.matmul(dst, a_lo, w_hi[:, slot, w], start=False, stop=last)

            def turn(s, groups, some):
                for g in some:
                    t, half, bank = groups[g]
                    pe.wait_ge(G["src_ready"], 4 * s + g + 1)
                    for k in range(4):
                        ins = nc.tensor.transpose(ps[:, bank, k * P:(k + 1) * P],
                                                  src[:, t, half * BANK + k * P:half * BANK + (k + 1) * P], ident[:])
                    ins.then_inc(G["turned"], 1)

            def proj_tile(slot, part, t, ready=None):
                for k in range(4):
                    if ready and k == 2:
                        pe.wait_ge(G["w_lo_ready"], ready)
                    ins = three(ps[:, 4 + t, :], xt_hi[:, t, 4 * part + k, :], xt_lo[:, t, 4 * part + k, :], slot,
                                k * BANK, part == 0 and k == 0, part == 1 and k == 3)
                return ins

            def proj_unit(u, part, count=None, read_out=None, weave=None):
                pe.wait_ge(G["w_lo_ready"], u + 1 if count is None else count)
                for t in range(NT):
                    if read_out and read_out[t]:
                        pe.wait_ge(*read_out[t])
                    ins = proj_tile(u % SPL, part, t)
                    if part == 1 and t == 0:
                        ins.then_inc(G["tile0_done"], 1)
                    if t == 0 and weave:
                        weave()
                ins.then_inc(G["unit_used"], 1)

            def entry(n):
                u, s = FIRST_UNIT[n], STAGE[n]
                if n == 0:
                    turn(s, NORM_GROUPS, (0, 1))
                    pe.wait_ge(G["w_lo_half"], 1)
                else:
                    pe.wait_ge(G["w_lo_ready"], u + 1)
                pe.wait_ge(G["xt_lo_ready"], 4 * s + 1)
                proj_tile(u % SPL, 0, 0, ready=None if n else u + 1)
                turn(s, NORM_GROUPS, (2,))
                pe.wait_ge(G["w_lo_half"], n + 2)
                pe.wait_ge(G["xt_lo_ready"], 4 * s + 2)
                proj_tile((u + 1) % SPL, 1, 0, ready=u + 2).then_inc(G["tile0_done"], 1)
                turn(s, NORM_GROUPS, (3,))
                pe.wait_ge(G["xt_lo_ready"], 4 * s + 3)
                proj_tile(u % SPL, 0, 1).then_inc(G["unit_used"], 1)
                pe.wait_ge(G["xt_lo_ready"], 4 * s + 4)
                proj_tile((u + 1) % SPL, 1, 1).then_inc(G["unit_used"], 1)

            def out_tile(u, t, a_hi, a_lo, first, last, weave=None):
                for half in range(2):
                    for k in range(2):
                        ins = three(ps[:, 2 * t + half, :], a_hi(t, k), a_lo(t, k), u % SPL,
                                    k * 2 * BANK + half * BANK, first and k == 0, last and k == 1)
                        if weave and (t, half, k) in weave:
                            weave[t, half, k]()
                    if last and not (t and half):
                        ins.then_inc(G["acc_done"], 1)
                    if weave and (t, half) in weave:
                        weave[t, half]()
                if t:
                    ins.then_inc(G["unit_used"], 1)

            def out_unit(u, a_hi, a_lo, first, last, count=None, weave=None, ready=None):
                pe.wait_ge(G["w_lo_ready"], u + 1 if count is None else count)
                for t in range(NT):
                    if ready:
                        pe.wait_ge(ready[0], ready[1] + t)
                    out_tile(u, t, a_hi, a_lo, first, last, weave)

            def next_norm(n):
                if n + 1 == len(SUBS):
                    return None
                return {(1, 0, 0): lambda: turn(STAGE[n + 1], NORM_GROUPS, (0,)),
                        (1, 0): lambda: turn(STAGE[n + 1], NORM_GROUPS, (1,))}

            def turn_hidden(count):
                pe.wait_ge(G["hid_ready"], count)
                for k in range(2):
                    for t in range(NT):
                        ins = nc.tensor.transpose(ps[:, 6, (2 * k + t) * P:(2 * k + t + 1) * P],
                                                  hid[:, t, k * P:(k + 1) * P], ident[:])
                ins.then_inc(G["ht_turned"], 1)

            def turn_hidden_tile(count, t):
                pe.wait_ge(G["hid_ready"], count + t)
                for k in range(2):
                    ins = nc.tensor.transpose(ps[:, 6 + t, k * P:(k + 1) * P], hid[:, t, k * P:(k + 1) * P], ident[:])
                ins.then_inc(G["ht_turned"], 1)

            def h_hi(t, k):
                return ht_hi[:, k, t, :]

            def h_lo(t, k):
                return ht_lo[:, k, t, :]

            def ffn(n, j):
                u0, h0, hid0 = FIRST_UNIT[n], HT * j, NT * NCH * j
                entry(n)

                def chunk(i, b, first=False, weave=None):
                    ua = u0 + 2 + 3 * b
                    proj_unit(ua, 0, count=i * 6 + (ua + 1),
                              read_out=[(G["hid_ready"], i * 4 + (hid0 + 2 * b + 1)), None],
                              weave=lambda: turn_hidden(i * 4 + (hid0 + 2 * b + 2)))
                    proj_unit(ua + 1, 1, count=i * 6 + (ua + 2))
                    pe.wait_ge(G["ht_lo_ready"], i * 2 + (h0 + b + 1))
                    out_unit(ua + 2, h_hi, h_lo, first, False, count=i * 6 + (ua + 3), weave=weave)

                chunk(0, 0, first=True)
                chunk(0, 1)
                with pe.Fori(1, LOOPED) as i:
                    for b in range(2):
                        chunk(i, b)
                last = hid0 + 2 * NCH - 1
                chunk(LOOPED, 0)
                chunk(LOOPED, 1, weave={(0, 1): lambda: turn_hidden_tile(last, 0),
                                        (1, 0): lambda: turn_hidden_tile(last, 1)})
                out_unit(u0 + FFN_UNITS - 1, h_hi, h_lo, False, True, weave=next_norm(n),
                         ready=(G["ht_lo_ready"], h0 + NCH))

            def gate_products(S, mixer_no):
                pe.wait_ge(G["gw_spread"], 4 * (mixer_no + 1))
                for k in range(KT):
                    w = (ht_hi, ht_lo)[k // 4][:, :, :, :].rearrange("p a b n -> p (a b) n")[:, k % 4, :]
                    nc.tensor.matmul(ps[:, 6, 0:SEQ], w, xt_hi[:, :, k, :], start=(k == 0), stop=False)
                    ins = nc.tensor.matmul(ps[:, 6, 0:SEQ], w, xt_lo[:, :, k, :], start=False, stop=(k == KT - 1))
                ins.then_inc(S["gate_mm"], 1)

            def rms_rows(S, n):
                pe.wait_ge(G["rms_ready"], n + 1)
                for t in range(NT):
                    ins = nc.tensor.matmul(ps[0:32, 7, t * P:(t + 1) * P], rms[:, t:t + 1].to_broadcast([P, 32]),
                                           ident[:], start=True, stop=True)
                ins.then_inc(S["rms_turned"], 1)

            def gate_rows(S, lay, outs):
                pe.wait_ge(S["gates_ready"], 1)
                for m, c in enumerate(outs):
                    ins = nc.tensor.matmul(ps[0:c.stop - c.start, 7, m * SEQ:(m + 1) * SEQ],
                                           gsel[:, lay, c], grow[:, :], start=True, stop=True)
                ins.then_inc(S["gates_turned"], 1)

            def turn_nat(S, m, ready, value, banks):
                pe.wait_ge(ready, value)
                for c in range(4):
                    for t in range(NT):
                        q = (c % 2) * SEQ + t * P
                        ins = nc.tensor.transpose(ps[:, banks + c // 2, q:q + P],
                                                  nat[:, m % 2, t, c * P:(c + 1) * P], ident[:])
                ins.then_inc(S["turned"], 1)

            def spread(bank, q, row, heads, h):
                return nc.tensor.matmul(ps[:, bank, q:q + SEQ], ident[0:heads, h:h + 1].to_broadcast([heads, P]),
                                        row, start=True, stop=True)

            def plan_a(n, j):
                S = MS[j]
                slots = {k: [] for k in range(16)}

                def turn_rows():
                    pe.wait_ge(S["en_ready"], 1)
                    for g, r in ((0, 3), (1, 5)):
                        for t in range(NT):
                            ins = nc.tensor.transpose(ps[:, 6, 8 * g + 4 * t:8 * g + 4 * t + 4],
                                                      rowbuf[0:MH, r, t * P:(t + 1) * P], ident[0:MH, 0:MH])
                    ins.then_inc(S["cols_turned"], 1)

                def spread_m():
                    pe.wait_ge(S["cols_ready"], 1)
                    for h in range(MH):
                        ins = spread(6 + h // 2, (h % 2) * SEQ, rowbuf[0:MH, 4, :], MH, h)
                    ins.then_inc(S["mb_done"], 1)

                def turn_qk(m):
                    if m >= 2:
                        pe.wait_ge(S["taps"], 12 * (m - 1))
                    turn_nat(S, m, S["nat_ready"], 2 * (m + 1), 2 * (m % 2))

                def scores(h):
                    if h == 0:
                        pe.wait_ge(S["conv_ready"], 4)
                    for k in range(2):
                        nc.tensor.matmul(ps[:, h, 0:SEQ], qkt[:, 8 + 2 * h + k, 0:P], qkt[:, 2 * h + k, :],
                                         start=(k == 0), stop=(k == 1))
                    for k in range(2):
                        ins = nc.tensor.matmul(ps[:, h, SEQ:SEQ + P], qkt[:, 8 + 2 * h + k, P:SEQ],
                                               qkt[:, 2 * h + k, P:SEQ], start=(k == 0), stop=(k == 1))
                    ins.then_inc(S["s_done"], 1)

                def values(h):
                    pe.wait_ge(S["pm_ready"], MH)
                    pe.wait_ge(S["v_ready"], 4)
                    b = HEAD_BANK[h]
                    nc.tensor.matmul(ps[:, b, 0:MDH + 1], probs[:, h, 0:P], vaug[:, 0, h, :], start=True, stop=True)
                    nc.tensor.matmul(ps[:, b + 1, 0:MDH + 1], probs[:, h, P:SEQ], vaug[:, 0, h, :], start=True,
                                     stop=False)
                    nc.tensor.matmul(ps[:, b + 1, 0:MDH + 1], probs[:, h, SEQ:SEQ + P], vaug[:, 1, h, :],
                                     start=False, stop=True).then_inc(S["pv_done"], 1)

                def last_head():
                    pe.wait_ge(S["og_ready"], 4)
                    values(3)

                slots[1] += [lambda: gate_products(S, 3 * j), lambda: rms_rows(S, n)]
                slots[2].append(lambda: gate_rows(S, 3 * j, (slice(0, MH), slice(MH, 2 * MH))))
                slots[6].append(turn_rows)
                slots[7].append(spread_m)
                for m in range(4):
                    slots[2 * m + 2].append(lambda m=m: turn_qk(m))
                for h in range(MH):
                    slots[11].append(lambda h=h: scores(h))
                for h in range(3):
                    slots[13].append(lambda h=h: values(h))
                return slots, last_head

            def plan_b(n, j):
                S = FS
                slots = {k: [] for k in range(16)}

                def turn_rows():
                    pe.wait_ge(S["rows"], 2)
                    for t in range(NT):
                        ins = nc.tensor.transpose(ps[:, 7, FH * t:FH * (t + 1)],
                                                  ptbuf[0:FH, 1, t * P:(t + 1) * P], ident[0:FH, 0:FH])
                    ins.then_inc(S["cols_turned"], 1)

                def spread_f(q):
                    if q == 1:
                        pe.wait_ge(S["cols_ready"], 1)
                    if q >= 2:
                        pe.wait_ge(S["fb_copied"], 4 * (q - 1))
                    for h in (2 * q, 2 * q + 1):
                        ins = spread(6 + q % 2, (h % 2) * SEQ, ptbuf[0:FH, 1, 0:SEQ], FH, h)
                    ins.then_inc(S["fb_done"], 1)

                def turn_qk(m):
                    if m >= 2:
                        pe.wait_ge(S["qk_ready"], 2 * (m - 1))
                    turn_nat(S, m, S["natn_ready"], 2 * (m + 1), 2 * (m % 2))

                def scores(h):
                    if h == 0:
                        pe.wait_ge(S["qk_ready"], 8)
                    if h >= 2:
                        pe.wait_ge(S["z_ready"], h - 1)
                    q, k = qkt[:, h, :], qkt[:, FH + h, :]
                    nc.tensor.matmul(ps[:, h % 2, 0:P], q[:, 0:P], k[:, 0:P], start=True, stop=True)
                    nc.tensor.matmul(ps[:, h % 2, P:3 * P], q[:, P:SEQ], k, start=True, stop=True).then_inc(
                        S["s_done"], 1)

                def turn_probs(h):
                    pe.wait_ge(S["p_ready"], 2 * (h + 1))
                    if h >= 2:
                        pe.wait_ge(S["pt_ready"], h - 1)
                    for b in range(3):
                        ins = nc.tensor.transpose(ps[:, 2 + h % 2, b * P:(b + 1) * P],
                                                  zbuf[:, h % 2, b * P:(b + 1) * P], ident[:])
                    ins.then_inc(S["p_turned"], 1)

                def values(h):
                    pe.wait_ge(S["pt_ready"], h + 1)
                    if h == 0:
                        pe.wait_ge(S["v_ready"], 4)
                    if h == 4:
                        pe.wait_ge(S["y_done"], 3 * 2 - 2)
                    if h == 6:
                        pe.wait_ge(G["src_ready"], 4 * (STAGE[n] + 1) + 2)
                    v = [vaug[:, t, :, :].rearrange("p h n -> p (h n)")[:, h * FDH:(h + 1) * FDH] for t in range(NT)]
                    bank, q, pt = 6 + (h // 2) % 2, (h % 2) * SEQ, ptbuf[:, h % 2, :]
                    nc.tensor.matmul(ps[:, bank, q:q + P], pt[:, 0:P], v[0], start=True, stop=True)
                    nc.tensor.matmul(ps[:, bank, q + P:q + SEQ], pt[:, P:SEQ], v[0], start=True, stop=False)
                    nc.tensor.matmul(ps[:, bank, q + P:q + SEQ], pt[:, SEQ:SEQ + P], v[1], start=False,
                                     stop=True).then_inc(S["pv_done"], 1)

                slots[1] += [lambda: gate_products(S, 1), lambda: rms_rows(S, n)]
                slots[2].append(lambda: gate_rows(S, 1, (slice(0, FH),)))
                slots[4].append(turn_rows)
                for q in range(4):
                    slots[4 + q].append(lambda q=q: spread_f(q))
                for m in range(4):
                    slots[2 * m + 3].append(lambda m=m: turn_qk(m))
                for k in range(6):
                    for step, pair in ((values, k - 2), (turn_probs, k - 1), (scores, k)):
                        if 0 <= pair < 4:
                            slots[10 + k] += [lambda f=step, h=2 * pair: f(h), lambda f=step, h=2 * pair + 1: f(h)]
                return slots, None

            def plan_c(n, j):
                S = LS
                slots = {k: [] for k in range(12)}

                def gate_up():
                    pe.wait_ge(S["glrt_ready"], 1)
                    for h in range(GH):
                        ins = nc.tensor.matmul(ps[:, 6 + h // 2, (h % 2) * SEQ:(h % 2 + 1) * SEQ],
                                               glaup[:, h * GDK:(h + 1) * GDK], glrt, start=True, stop=True)
                    ins.then_inc(S["z_done"], 1)

                def level(lv):
                    if lv == 0:
                        pe.wait_ge(S["qk_ready"], 4)
                        q, k = qkflat[:, 0:1024], qkflat[:, 1024:2048]
                    else:
                        pe.wait_ge(S["qs_ready"], lv)
                        pe.wait_ge(S["ks_ready"], lv)
                        q, k = qs[lv % 2], ks[lv % 2]
                    if lv >= 2:
                        pe.wait_ge(S["a_ready"], lv - 1)
                    for h in range(GH):
                        base = h * SEQ
                        if lv == GLA_LEVELS - 1:
                            ins = nc.tensor.matmul(ps[:, 0, h * P:(h + 1) * P], k[:, base:base + P],
                                                   q[:, base + P:base + SEQ], start=True, stop=True)
                            continue
                        for t in range(NT):
                            m, c = 2 * h + t, slice(base + t * P, base + (t + 1) * P)
                            ins = nc.tensor.matmul(ps[:, 2 * (lv % 2) + m // 4, (m % 4) * P:(m % 4 + 1) * P],
                                                   k[:, c], q[:, c], start=True, stop=True)
                    ins.then_inc(S["lvl_done"], 1)

                def values(h):
                    b = HEAD_BANK[h]
                    if h == 0:
                        pe.wait_ge(S["v_ready"], 4)
                        pe.wait_ge(S["a_ready"], GLA_LEVELS - 1)
                        pe.wait_ge(S["ax_ready"], 1)
                    if h == 3:
                        pe.wait_ge(S["og_ready"], 4)
                    nc.tensor.matmul(ps[:, b, 0:GDV], amat[:, 2 * h, :], vaug[:, 0, h, 0:GDV], start=True, stop=True)
                    nc.tensor.matmul(ps[:, b + 1, 0:GDV], across[:, h, :], vaug[:, 0, h, 0:GDV], start=True,
                                     stop=False)
                    nc.tensor.matmul(ps[:, b + 1, 0:GDV], amat[:, 2 * h + 1, :], vaug[:, 1, h, 0:GDV], start=False,
                                     stop=True).then_inc(S["pv_done"], 1)

                slots[1] += [lambda: gate_products(S, 2), lambda: rms_rows(S, n)]
                slots[2].append(lambda: gate_rows(S, 2, (slice(0, GRANK),)))
                slots[3].append(gate_up)
                for m in range(2):
                    slots[2 * m + 2].append(lambda m=m: turn_nat(S, m, S["nat_ready"], 2 * (m + 1), 2 * m))
                for lv in range(GLA_LEVELS - 1):
                    slots[GLA_PE[lv]].append(lambda lv=lv: level(lv))
                for h in range(3):
                    slots[11].append(lambda h=h: values(h))
                slots[11] += [lambda: turn(STAGE[n] + 1, MIX_GROUPS["C"], (0, 1)), lambda: values(3)]
                return slots, lambda: level(GLA_LEVELS - 1)

            def mixer(n, kind, j):
                u0, s, pu = FIRST_UNIT[n], STAGE[n], PROJ_UNITS[kind]
                slots, late = {"A": plan_a, "B": plan_b, "C": plan_c}[kind](n, j)
                S = {"A": MS[j], "B": FS, "C": LS}[kind]
                qk = {"A": 4, "B": 4, "C": 2}[kind]
                copies = [(S["nat_ready"], 2 * m) for m in range(qk)] + \
                         [(S["v_ready"], 2 * m) for m in range(2)] + [(S["og_ready"], 2 * m) for m in range(2)]

                def turn_half():
                    turn(s + 1, MIX_GROUPS[kind], (0, 1))

                inside = late if kind == "C" else turn_half

                entry(n)
                for k in range(1, pu):
                    if k > 1:
                        read = None
                        if k % 2 == 0:
                            done, before = copies[k // 2 - 1]
                            read = [(done, before + 1), (done, before + 2)]
                        proj_unit(u0 + k, k % 2, read_out=read,
                                  weave=inside if k == pu - 1 else None)
                    for step in slots[k]:
                        step()

                def rows_of(q):
                    return (lambda t, k: xt_hi[:, t, 2 * q + k, :]), (lambda t, k: xt_lo[:, t, 2 * q + k, :])

                pe.wait_ge(G["xt_lo_ready"], 4 * (s + 1) + 2)
                pe.wait_ge(G["w_lo_ready"], u0 + pu + 1)
                out_tile(u0 + pu, 0, *rows_of(0), True, False)
                if kind == "A":
                    late()
                if kind != "B":
                    pe.wait_ge(S["y_done"], 4)
                out_tile(u0 + pu, 1, *rows_of(0), True, False)
                out_unit(u0 + pu + 1, *rows_of(1), False, False,
                         weave={(0, 1): lambda: turn(s + 1, MIX_GROUPS[kind], (2, 3))})
                pe.wait_ge(G["xt_lo_ready"], 4 * (s + 1) + 4)
                out_unit(u0 + pu + 2, *rows_of(2), False, False)
                out_unit(u0 + pu + 3, *rows_of(3), False, True, weave=next_norm(n))

            pe.wait_ge(G["ident_in"], 16)
            for n, (kind, j) in enumerate(SUBS):
                if kind == "F":
                    ffn(n, j)
                else:
                    mixer(n, kind, j)


def kernel(**inputs):
    import numpy as np
    import concourse.bacc as bacc
    from concourse.bass_utils import run_bass_kernel_spmd as run

    a = {k: np.asarray(v) for k, v in inputs.items()}

    def in_units(w, cols):
        w = w.reshape(2, 4, P, cols // BANK, BANK).transpose(3, 0, 2, 1, 4)
        return w.reshape(-1, P, UNIT)

    def out_units(w):
        return w.reshape(-1, 2, P, D).transpose(0, 2, 1, 3).reshape(-1, P, UNIT)

    stream = np.empty((N_UNITS, P, UNIT), np.float32)
    gate = np.zeros((DEPTH, P, P), np.float32)
    vecs = np.empty((N_VEC, D), np.float32)
    sel = np.zeros((33, DEPTH, 16), np.float32)
    for n, (kind, j) in enumerate(SUBS):
        u, layer = FIRST_UNIT[n], n // 3
        vecs[VEC[n]] = a["norm_w"][layer, n % 3]
        if kind == "F":
            w1 = a["ffn_w_in"][j // 2, j % 2].reshape(D, 2, NCH, HC).transpose(0, 2, 1, 3).reshape(D, 2 * F)
            w1 = in_units(w1, 2 * F)
            w2 = out_units(a["ffn_w_out"][j // 2, j % 2])
            stream[u:u + 2] = w1[0:2]
            body = stream[u + 2:u + FFN_UNITS - 1].reshape(NCH - 1, 3, P, UNIT)
            body[:, 0:2] = w1[2:].reshape(NCH - 1, 2, P, UNIT)
            body[:, 2] = w2[0:NCH - 1]
            stream[u + FFN_UNITS - 1] = w2[NCH - 1]
            continue
        name = {"A": "mlstm", "B": "fox", "C": "gla"}[kind]
        w, pu, width = a[name + "_w_in"][j], PROJ_UNITS[kind], GCOLS[kind]
        main = w.shape[1] - width
        stream[u:u + pu] = in_units(w[:, 0:main], main)
        stream[u + pu:u + pu + OUT_UNITS] = out_units(a[name + "_w_out"][j])
        gate[layer, :, 0:KT * width] = w[:, main:].reshape(KT, P, width).transpose(1, 0, 2).reshape(P, KT * width)
        for q in range(width):
            sel[q, layer, q] = sel[width + q, layer, q] = 1.0
        if kind == "A":
            sel[32, layer, 0:width] = a["mlstm_b_gate"][j]
            vecs[VEC[n] + 1] = a["mlstm_norm_w"][j]
        if kind == "B":
            sel[32, layer, 0:width] = a["fox_b_f"][j]
        if kind == "C":
            vecs[VEC[n] + 1] = a["gla_norm_w"][j]
    vecs[N_VEC - 1] = a["final_norm_w"]

    masks = np.zeros((P, 8, P), np.float32)
    for q in range(P):
        masks[q, 0, q] = 1
        for lv in range(1, 8):
            size = 1 << (lv - 1)
            if q // size % 2 == 0:
                t0 = (q // size + 1) * size
                masks[q, lv, t0:t0 + size] = 1

    arrays = {
        "stream": stream,
        "x": a["x"],
        "vecs": vecs,
        "gate_w": gate.transpose(1, 0, 2),
        "gate_sel": sel,
        "conv_w": a["mlstm_conv_w"].reshape(2, 4, 16, P).transpose(3, 0, 2, 1),
        "fox_qk": a["fox_qk_norm"][0].transpose(1, 0),
        "gla_up": a["gla_w_gate_up"][0],
        "gla_b": a["gla_b_gate"][0].reshape(GH, GDK).transpose(1, 0),
        "masks": masks,
        "ident": np.eye(P, dtype=np.float32),
    }
    nc = bacc.Bacc("TRN2", target_bir_lowering=False, num_devices=1)
    aps = []
    for name in arrays:
        arrays[name] = np.ascontiguousarray(arrays[name])
        aps.append(nc.dram_tensor("in_" + name, arrays[name].shape, mybir.dt.from_np(arrays[name].dtype),
                                  kind="ExternalInput").ap())
    out = nc.dram_tensor("out_y", (1, SEQ, D), F32, kind="ExternalOutput").ap()
    build(nc, *aps, out)
    r = run(nc, [{"in_" + k: v for k, v in arrays.items()}], core_ids=[0])
    return r.results[0]["out_y"]
```
